# Optimizing a Trainium2 kernel written in Bass

```python
import functools
import jax, jax.numpy as jnp
from jax import lax
import numpy as np

D_MODEL = 1024
BATCH = 1
SEQ = 1024
DEPTH = 2
DEC_BATCH = 8
DEC_SEQ = 1
PAST_LEN = 2048
PAGE_SIZE = 128

A_HEADS = 4
A_DK = 128
A_DV = 128
HGRN_CHUNK = 64
B_HEADS = 8
B_KV_HEADS = 2
B_GROUP = B_HEADS // B_KV_HEADS
B_HD = 64
L_CMP = 32
D_CMP = 16
CMP_HID = 64
L_SLC = 64
N_SEL = 16
WINDOW = 512
Q_BLOCK = 128
SEL_FORCE = 1e9
CONV_DIM = D_MODEL
CONV_W = 3
D_FF = 2816
EPS = 1e-6
N_A = (DEPTH + 1) // 2
N_C = DEPTH // 2
AB_MIX = A_HEADS * A_DV + B_HEADS * B_HD
KV_W = 2 * B_KV_HEADS * B_HD
AB_SPLIT = (A_HEADS * A_DK, A_HEADS * A_DK, A_HEADS * A_DV, A_HEADS * A_DV,
            B_HEADS * B_HD, KV_W, KV_W, KV_W, 3 * B_HEADS)
AB_IN = sum(AB_SPLIT)

kernel_name = 'hgrn2_nsa_shortconv_convffn_step'

def rmsnorm(x, w):
    xf = x.astype(jnp.float32)
    y = xf * lax.rsqrt(jnp.mean(xf * xf, axis=-1, keepdims=True) + EPS)
    return (y * w.astype(jnp.float32)).astype(x.dtype)

def causal_dwconv(u, buf, w):
    t = u.shape[1]
    ext = jnp.concatenate([buf.astype(u.dtype), u], axis=1)
    y = ext[:, 0:t] * w[0]
    for j in range(1, CONV_W):
        y = y + ext[:, j:j + t] * w[j]
    return y, ext[:, t:]

def masked_softmax(s, mask):
    s = jnp.where(mask, s, -jnp.inf)
    m = jnp.max(s, axis=-1, keepdims=True)
    m = jnp.where(jnp.isfinite(m), m, 0.0)
    e = jnp.exp(s - m)
    d = jnp.sum(e, axis=-1, keepdims=True)
    return e / jnp.where(d > 0, d, 1.0)

def alibi_slopes():
    h = jnp.arange(1, B_HEADS + 1, dtype=jnp.float32)
    return (2.0 ** (-8.0 * h / B_HEADS)).reshape(B_KV_HEADS, B_GROUP)

def split_ab(proj):
    parts, off = [], 0
    for n in AB_SPLIT:
        parts.append(proj[..., off:off + n])
        off += n
    return parts

def hgrn2_chunk(S, inp):
    q, la, k, v = inp
    A = jnp.cumsum(la, axis=2)
    c = q.shape[2]
    o_inter = jnp.einsum('bhtk,bhkv->bhtv', q * jnp.exp(A), S)
    causal = jnp.tril(jnp.ones((c, c), dtype=bool))
    diff = A[:, :, :, None, :] - A[:, :, None, :, :]
    decay = jnp.exp(jnp.where(causal[None, None, :, :, None], diff, -jnp.inf))
    att = jnp.einsum('bhtk,bhtsk,bhsk->bhts', q, decay, k)
    o = o_inter + jnp.einsum('bhts,bhsv->bhtv', att, v)
    a_end = A[:, :, -1:, :]
    S_new = jnp.exp(a_end[:, :, 0, :])[..., None] * S + jnp.einsum('bhsk,bhsv->bhkv', k * jnp.exp(a_end - A), v)
    return S_new, o

def hgrn2_mixer(qa, fl, ia, ga, lb, norm_w, S0, chunk):
    b, t = qa.shape[:2]

    def heads(z):
        return z.reshape(b, t, A_HEADS, -1).transpose(0, 2, 1, 3).astype(jnp.float32)

    q, v = heads(qa), heads(ia)
    lbh = lb.reshape(A_HEADS, A_DK)[None, :, None, :]
    f = lbh + (1.0 - lbh) * jax.nn.sigmoid(heads(fl))
    la = jnp.log(f)
    k = 1.0 - f
    n = t // chunk

    def to_chunks(z):
        return z.reshape(b, A_HEADS, n, chunk, z.shape[-1]).transpose(2, 0, 1, 3, 4)

    S_fin, o = lax.scan(hgrn2_chunk, S0.astype(jnp.float32),
                        (to_chunks(q), to_chunks(la), to_chunks(k), to_chunks(v)))
    o = o.transpose(1, 0, 3, 2, 4).reshape(b, t, A_HEADS, A_DV)
    o = o * lax.rsqrt(jnp.mean(o * o, axis=-1, keepdims=True) + EPS)
    o = o * norm_w.reshape(A_HEADS, A_DV).astype(jnp.float32)
    o = o * jax.nn.sigmoid(ga.reshape(b, t, A_HEADS, A_DV).astype(jnp.float32))
    return o.reshape(b, t, A_HEADS * A_DV).astype(qa.dtype), S_fin

def nsa_compress(kv, pe, w1, w2):
    b, t = kv.shape[:2]
    n16 = t // D_CMP
    r_n = L_CMP // D_CMP
    nc = n16 - r_n + 1
    ch = kv.reshape(b, n16, D_CMP, 2, B_KV_HEADS, B_HD)
    w1r = w1.reshape(2, L_CMP, B_HD, CMP_HID)
    pre = jnp.einsum('kid,kidm->km', pe, w1r)[None, None, :, None, :]
    for r in range(r_n):
        part = jnp.einsum('bnikhd,kidm->bnkhm', ch, w1r[:, r * D_CMP:(r + 1) * D_CMP])
        pre = pre + part[:, r:r + nc]
    hid = jax.nn.silu(pre)
    return jnp.einsum('bnkhm,kmd->bnkhd', hid, w2)

def shared_attention(qg, qpos, k, v, kpos, mask, slopes):
    s = jnp.einsum('btkgd,bnkd->bkgtn', qg, k).astype(jnp.float32) * (B_HD ** -0.5)
    dist = (qpos[:, None] - kpos[None, :]).astype(jnp.float32)
    s = s - slopes[None, :, :, None, None] * dist
    p = masked_softmax(s, mask)
    o = jnp.einsum('bkgtn,bnkd->btkgd', p.astype(v.dtype), v)
    return o, p

def gathered_attention(qg, qpos, k, v, kpos, slopes):
    s = jnp.einsum('btkgd,bktnd->bkgtn', qg, k).astype(jnp.float32) * (B_HD ** -0.5)
    dist = (qpos[None, None, :, None] - kpos).astype(jnp.float32)
    s = s - slopes[None, :, :, None, None] * dist[:, :, None]
    mask = (kpos <= qpos[None, None, :, None])[:, :, None]
    p = masked_softmax(s, mask)
    return jnp.einsum('bkgtn,bktnd->btkgd', p.astype(v.dtype), v)

def select_blocks(p_cmp, qpos, n_cmp, n_blk, n_sel):
    imp = jnp.sum(p_cmp, axis=2)
    ci = jnp.arange(n_cmp)[:, None] * D_CMP
    sj = jnp.arange(n_blk)[None, :] * L_SLC
    cover = ((ci < sj + L_SLC) & (ci + L_CMP > sj)).astype(jnp.float32)
    score = jnp.einsum('bktc,cj->bktj', imp, cover)
    jb = jnp.arange(n_blk)[None, :]
    cur = (qpos // L_SLC)[:, None]
    forced = (jb == 0) | (jb == cur) | (jb == cur - 1)
    score = jnp.where(forced, SEL_FORCE, score)
    score = jnp.where(jb > cur, -jnp.inf, score)
    _, idx = lax.top_k(score, n_sel)
    return idx

def nsa_core(q, qpos, gates, comp, gather_fn, n_blk, wkv, wpos, slopes):
    b, tq = q.shape[:2]
    qg = q.reshape(b, tq, B_KV_HEADS, B_GROUP, B_HD)
    n_cmp = comp.shape[1]
    cpos = jnp.arange(n_cmp) * D_CMP + (L_CMP - 1)
    cmask = cpos[None, :] <= qpos[:, None]
    o_cmp, p_cmp = shared_attention(qg, qpos, comp[:, :, 0], comp[:, :, 1], cpos, cmask, slopes)
    idx = select_blocks(p_cmp, qpos, n_cmp, n_blk, min(N_SEL, n_blk))
    k_sel, v_sel = gather_fn(idx)
    nk = idx.shape[-1] * L_SLC
    kpos = (idx[..., None] * L_SLC + jnp.arange(L_SLC)).reshape(b, B_KV_HEADS, tq, nk)
    o_slc = gathered_attention(qg, qpos, k_sel.reshape(b, B_KV_HEADS, tq, nk, B_HD),
                               v_sel.reshape(b, B_KV_HEADS, tq, nk, B_HD), kpos, slopes)
    wmask = (wpos[None, :] <= qpos[:, None]) & (wpos[None, :] > qpos[:, None] - WINDOW) & (wpos[None, :] >= 0)
    o_win, _ = shared_attention(qg, qpos, wkv[:, :, 0], wkv[:, :, 1], wpos, wmask, slopes)
    g = jax.nn.sigmoid(gates.astype(jnp.float32)).reshape(b, tq, B_KV_HEADS, B_GROUP, 3)
    o = g[..., 0:1] * o_cmp + g[..., 1:2] * o_slc + g[..., 2:3] * o_win
    return o.reshape(b, tq, B_HEADS * B_HD).astype(q.dtype)

def gather_local_blocks(blocks, idx):
    bi = jnp.arange(blocks.shape[0])[:, None, None, None]
    gi = jnp.arange(B_KV_HEADS)[None, :, None, None]
    r = blocks[bi, idx, :, :, gi, :]
    return r[..., 0, :], r[..., 1, :]

def gather_paged_blocks(pool, page_table, li, new_blocks, nb_past, idx):
    b = idx.shape[0]
    bpp = PAGE_SIZE // L_SLC
    bi = jnp.arange(b)[:, None, None, None]
    gi = jnp.arange(B_KV_HEADS)[None, :, None, None]
    li_idx = jnp.full((1, 1, 1, 1), li, dtype=jnp.int32)
    jp = jnp.clip(idx, 0, nb_past - 1)
    phys = page_table[bi, jp // bpp]
    sub = jp % bpp
    pool_r = pool.reshape(pool.shape[0], bpp, L_SLC, *pool.shape[2:])
    r_past = pool_r[phys, sub, :, li_idx, :, gi, :]
    jn = jnp.clip(idx - nb_past, 0, new_blocks.shape[1] - 1)
    r_new = new_blocks[bi, jn, :, :, gi, :]
    r = jnp.where((idx >= nb_past)[..., None, None, None], r_new, r_past.astype(r_new.dtype))
    return r[..., 0, :], r[..., 1, :]

def nsa_prompt(q, gates, cmp_kv, slc_kv, win_kv, pe, w1, w2, slopes):
    b, s = q.shape[:2]
    comp = nsa_compress(cmp_kv, pe, w1, w2)
    nb = s // L_SLC
    blocks = slc_kv.reshape(b, nb, L_SLC, 2, B_KV_HEADS, B_HD)
    gather_fn = functools.partial(gather_local_blocks, blocks)
    win_pad = jnp.pad(win_kv, ((0, 0), (WINDOW, 0), (0, 0), (0, 0), (0, 0)))

    def one_block(qb):
        q0 = qb * Q_BLOCK
        q_blk = lax.dynamic_slice_in_dim(q, q0, Q_BLOCK, axis=1)
        g_blk = lax.dynamic_slice_in_dim(gates, q0, Q_BLOCK, axis=1)
        w_blk = lax.dynamic_slice_in_dim(win_pad, q0, WINDOW + Q_BLOCK, axis=1)
        qpos = q0 + jnp.arange(Q_BLOCK)
        wpos = q0 - WINDOW + jnp.arange(WINDOW + Q_BLOCK)
        return nsa_core(q_blk, qpos, g_blk, comp, gather_fn, nb, w_blk, wpos, slopes)

    out = lax.map(one_block, jnp.arange(s // Q_BLOCK))
    return out.transpose(1, 0, 2, 3).reshape(b, s, B_HEADS * B_HD)

def nsa_sample(q, gates, cmp_new, slc_new, win_new, cache_cmp_kv, cache_slc_kv, win_buf, page_table, li,
               pe, w1, w2, slopes):
    bd, t = q.shape[:2]
    n_pages = page_table.shape[1]
    past = n_pages * PAGE_SIZE
    li_idx = jnp.full((1, 1), li, dtype=jnp.int32)
    past_cmp = cache_cmp_kv[page_table, :, li_idx].reshape(bd, past, 2, B_KV_HEADS, B_HD)
    rows = jnp.concatenate([past_cmp.astype(cmp_new.dtype), cmp_new], axis=1)
    rows = jnp.pad(rows, ((0, 0), (0, (-(past + t)) % D_CMP), (0, 0), (0, 0), (0, 0)))
    comp = nsa_compress(rows, pe, w1, w2)
    nb_past = past // L_SLC
    n_new = -(-t // L_SLC)
    new_blocks = jnp.pad(slc_new, ((0, 0), (0, n_new * L_SLC - t), (0, 0), (0, 0), (0, 0)))
    new_blocks = new_blocks.reshape(bd, n_new, L_SLC, 2, B_KV_HEADS, B_HD)
    gather_fn = functools.partial(gather_paged_blocks, cache_slc_kv, page_table, li, new_blocks, nb_past)
    wb = win_buf.shape[1]
    wkv = jnp.concatenate([win_buf.astype(win_new.dtype), win_new], axis=1)
    wpos = past - wb + jnp.arange(wb + t)
    qpos = past + jnp.arange(t)
    o = nsa_core(q, qpos, gates, comp, gather_fn, nb_past + n_new, wkv, wpos, slopes)
    return o, wkv[:, t:]

def short_conv_mixer(h, w_in, conv_w, w_out, buf):
    xin, cg, bg = jnp.split(h @ w_in, 3, axis=-1)
    y, new_buf = causal_dwconv(cg * xin, buf, conv_w)
    return (bg * y) @ w_out, new_buf

def conv_ffn(h, w_up, conv_w, w_down, buf):
    u, new_buf = causal_dwconv(h @ w_up, buf, conv_w)
    a, g = jnp.split(u, 2, axis=-1)
    return (jax.nn.silu(a) * g) @ w_down, new_buf

def setup_inputs(seed: int = 0) -> dict:
    key = jax.random.key(seed)
    ks = iter(jax.random.split(key, 32))

    def nrm(shape, scale):
        return jax.random.normal(next(ks), shape, jnp.float32) * scale

    def gain(shape):
        return 1.0 + nrm(shape, 0.05)

    n_pages = PAST_LEN // PAGE_SIZE
    n_used = DEC_BATCH * n_pages
    n_pool = (5 * n_used + 3) // 4
    wb = min(WINDOW, PAST_LEN)
    page_table = jax.random.permutation(next(ks), n_pool)[:n_used].reshape(DEC_BATCH, n_pages).astype(jnp.int32)
    return {
        'x_prompt': nrm((BATCH, SEQ, D_MODEL), 1.0),
        'x_sample': nrm((DEC_BATCH, DEC_SEQ, D_MODEL), 1.0),
        'cache_cmp_kv': nrm((n_pool, PAGE_SIZE, N_A, 2, B_KV_HEADS, B_HD), 1.0),
        'cache_slc_kv': nrm((n_pool, PAGE_SIZE, N_A, 2, B_KV_HEADS, B_HD), 1.0),
        'state_win_kv': nrm((N_A, DEC_BATCH, wb, 2, B_KV_HEADS, B_HD), 1.0),
        'state_hgrn': nrm((N_A, DEC_BATCH, A_HEADS, A_DK, A_DV), 0.5),
        'state_sconv': nrm((N_C, DEC_BATCH, CONV_W - 1, CONV_DIM), 1.0),
        'state_ffn': nrm((DEPTH, DEC_BATCH, CONV_W - 1, 2 * D_FF), 1.0),
        'page_table': page_table,
        'norm_mix': gain((DEPTH, D_MODEL)),
        'norm_ffn': gain((DEPTH, D_MODEL)),
        'norm_final': gain((D_MODEL,)),
        'ab_w_in': nrm((N_A, D_MODEL, AB_IN), D_MODEL ** -0.5),
        'ab_w_out': nrm((N_A, AB_MIX, D_MODEL), AB_MIX ** -0.5),
        'hgrn_lb_logits': nrm((N_A + 1, A_HEADS * A_DK), 0.5),
        'hgrn_norm': gain((N_A, A_HEADS * A_DV)),
        'cmp_pe': nrm((N_A, 2, L_CMP, B_HD), 0.5),
        'cmp_w1': nrm((N_A, 2, L_CMP * B_HD, CMP_HID), (L_CMP * B_HD) ** -0.5),
        'cmp_w2': nrm((N_A, 2, CMP_HID, B_HD), CMP_HID ** -0.5),
        'c_w_in': nrm((N_C, D_MODEL, 3 * CONV_DIM), D_MODEL ** -0.5),
        'c_conv': nrm((N_C, CONV_W, CONV_DIM), CONV_W ** -0.5),
        'c_w_out': nrm((N_C, CONV_DIM, D_MODEL), CONV_DIM ** -0.5),
        'ffn_up': nrm((DEPTH, D_MODEL, 2 * D_FF), D_MODEL ** -0.5),
        'ffn_conv': nrm((DEPTH, CONV_W, 2 * D_FF), CONV_W ** -0.5),
        'ffn_down': nrm((DEPTH, D_FF, D_MODEL), D_FF ** -0.5),
    }

def reference(x_prompt, x_sample, cache_cmp_kv, cache_slc_kv, state_win_kv, state_hgrn, state_sconv, state_ffn,
              page_table, norm_mix, norm_ffn, norm_final, ab_w_in, ab_w_out, hgrn_lb_logits, hgrn_norm,
              cmp_pe, cmp_w1, cmp_w2, c_w_in, c_conv, c_w_out, ffn_up, ffn_conv, ffn_down):
    slopes = alibi_slopes()
    lbs = jnp.cumsum(jax.nn.softmax(hgrn_lb_logits.astype(jnp.float32), axis=0), axis=0)
    b, s = x_prompt.shape[:2]
    bd, t = x_sample.shape[:2]
    wb = state_win_kv.shape[2]
    xp, xs = x_prompt, x_sample
    p_cmp, p_slc, p_win, p_hg, p_sc, p_ff = [], [], [], [], [], []
    s_cmp, s_slc, s_win, s_hg, s_sc, s_ff = [], [], [], [], [], []
    for l in range(DEPTH):
        if l % 2 == 0:
            la = l // 2
            qa, fl, ia, ga, qb, kc, ksl, kw, gb = split_ab(rmsnorm(xp, norm_mix[l]) @ ab_w_in[la])
            kc, ksl, kw = [z.reshape(b, s, 2, B_KV_HEADS, B_HD) for z in (kc, ksl, kw)]
            oa, hg = hgrn2_mixer(qa, fl, ia, ga, lbs[la], hgrn_norm[la],
                                 jnp.zeros((b, A_HEADS, A_DK, A_DV), jnp.float32), HGRN_CHUNK)
            ob = nsa_prompt(qb, gb, kc, ksl, kw, cmp_pe[la], cmp_w1[la], cmp_w2[la], slopes)
            xp = xp + jnp.concatenate([oa, ob], axis=-1) @ ab_w_out[la]
            p_cmp.append(kc)
            p_slc.append(ksl)
            p_win.append(jnp.pad(kw, ((0, 0), (max(wb - s, 0), 0), (0, 0), (0, 0), (0, 0)))[:, -wb:])
            p_hg.append(hg)
            qa, fl, ia, ga, qb, kc, ksl, kw, gb = split_ab(rmsnorm(xs, norm_mix[l]) @ ab_w_in[la])
            kc, ksl, kw = [z.reshape(bd, t, 2, B_KV_HEADS, B_HD) for z in (kc, ksl, kw)]
            oa, hg = hgrn2_mixer(qa, fl, ia, ga, lbs[la], hgrn_norm[la], state_hgrn[la], t)
            ob, win = nsa_sample(qb, gb, kc, ksl, kw, cache_cmp_kv, cache_slc_kv, state_win_kv[la], page_table, la,
                                 cmp_pe[la], cmp_w1[la], cmp_w2[la], slopes)
            xs = xs + jnp.concatenate([oa, ob], axis=-1) @ ab_w_out[la]
            s_cmp.append(kc)
            s_slc.append(ksl)
            s_win.append(win)
            s_hg.append(hg)
        else:
            lc = l // 2
            yp, bp = short_conv_mixer(rmsnorm(xp, norm_mix[l]), c_w_in[lc], c_conv[lc], c_w_out[lc],
                                      jnp.zeros((b, CONV_W - 1, CONV_DIM), xp.dtype))
            xp = xp + yp
            p_sc.append(bp)
            ys, bs = short_conv_mixer(rmsnorm(xs, norm_mix[l]), c_w_in[lc], c_conv[lc], c_w_out[lc], state_sconv[lc])
            xs = xs + ys
            s_sc.append(bs)
        yp, bp = conv_ffn(rmsnorm(xp, norm_ffn[l]), ffn_up[l], ffn_conv[l], ffn_down[l],
                          jnp.zeros((b, CONV_W - 1, 2 * D_FF), xp.dtype))
        xp = xp + yp
        p_ff.append(bp)
        ys, bs = conv_ffn(rmsnorm(xs, norm_ffn[l]), ffn_up[l], ffn_conv[l], ffn_down[l], state_ffn[l])
        xs = xs + ys
        s_ff.append(bs)
    y_prompt = rmsnorm(xp, norm_final)
    y_sample = rmsnorm(xs, norm_final)
    return (y_prompt, y_sample,
            jnp.stack(p_cmp, axis=2), jnp.stack(p_slc, axis=2), jnp.stack(p_win, axis=0),
            jnp.stack(p_hg, axis=0), jnp.stack(p_sc, axis=0), jnp.stack(p_ff, axis=0),
            jnp.stack(s_cmp, axis=2), jnp.stack(s_slc, axis=2), jnp.stack(s_win, axis=0),
            jnp.stack(s_hg, axis=0), jnp.stack(s_sc, axis=0), jnp.stack(s_ff, axis=0))


_drawn_inputs = setup_inputs


def setup_inputs(seed=0):
    import zlib

    import numpy as np

    out = dict(_drawn_inputs(seed))
    spreads = {}
    factors = {}
    for name, (base, spread) in spreads.items():
        noise = np.random.default_rng([zlib.crc32(name.encode()), seed]).standard_normal(out[name].shape)
        drawn = base * np.exp(spread * noise) if base else spread * noise
        out[name] = __import__('jax').numpy.asarray(drawn.astype(out[name].dtype))
    for name, factor in factors.items():
        out[name] = (out[name] * factor).astype(out[name].dtype)
    return out
```

```python
from contextlib import ExitStack, contextmanager

import numpy as np

import concourse.bass as bass
from concourse import mybir

F32 = mybir.dt.float32
I32 = mybir.dt.int32
ALU = mybir.AluOpType
ACT = mybir.ActivationFunctionType
AX_X = mybir.AxisListType.X
ds = bass.ds

P = 128
D = 1024
KD = D // P
T = 1024
NB = 8
TT = T + NB
NC = T // P
TN = 3
TW = TT // TN
FF = 2816
KF = FF // P
KH = KF // 2
HA = 4
LEV = 7
HB, HD = 8, 64
KVW = 256
PAST, PAGE = 2048, 128
NPG = PAST // PAGE
NPOOL = 160
WIN = 512
CMP, STRIDE = 32, 16
NCP = T // STRIDE - 1
NCS = PAST // STRIDE - 1
NBLK = PAST // 64 + 1
NSEL = 16
EPS = 1e-6
FAR = 1e30
WCH = KH * P
NORMS = 5


class Chain:

    def __init__(self, engine, sem):
        self.engine, self.sem, self.base, self.k = engine, sem, 0, 0

    def up(self, instruction):
        instruction.then_inc(self.sem, 1)
        self.k += 1

    def settle(self):
        self.engine.wait_ge(self.sem, self.base + self.k)

    def link(self, instruction):
        self.up(instruction)
        self.settle()

    @contextmanager
    def turns(self, count, per):
        start = self.base + self.k
        with self.engine.Fori(0, count) as i:
            self.base, self.k = i * per + start, 0
            yield i
            assert self.k == per, f"the body raises {self.k} times, not {per}"
        self.base, self.k = start + count * per, 0


def at(i, per, first):
    return first if i is None else i * per + first


HEAD_TILES = 5
HEAD_PS = HEAD_TILES + 1 + 1 + NC + 1
PLAN = {}
PLAN_N = {}


def plan():
    u, w = 2, 0
    for name, tiles, chunks in (
        ("norm0", 1, 0), ("heads", HA * HEAD_PS, HA * HEAD_TILES), ("kv", 12, 6), ("gates", 1, 0),
        ("squeeze", 2 * (NB + 1), 0), ("sample", 8, 0),
        ("mix_out", KD, KD), ("norm1", 1, 0), ("up0", 2 * KF, 2 * KF), ("down0", KD, 2 * KD), ("norm2", 1, 0),
        ("conv_in", 3 * KD, 3 * KD), ("conv_out", KD, KD), ("norm3", 1, 0), ("up1", 2 * KF, 2 * KF), ("down1", KD, 2 * KD),
        ("norm4", 1, 0),
    ):
        PLAN[name] = (u, w)
        PLAN_N[name] = tiles
        u += tiles
        w += chunks
    PLAN["end"] = (u, w)


plan()


WK = KF * TT
WKW = 1056


def program(nc, x, wk8, wdn, small, cst, hmask, s_hgrn, wgate, pages, cmp_t, slc_kt, slc_v, win_kt, win_v, state_win,
            w1, w2, pe_t, csn, bias_w, bias_s, tri, table, table_c, s_ff, w_ff, s_sc, w_sc,
            o_y, o_hgrn_p, o_hgrn_s, o_cmp_p, o_slc_p, o_win_p, o_cmp_s, o_slc_s, o_win_s, o_sc, o_ff):
    with ExitStack() as ctx:
        def sb(name, shape, dt=F32):
            return ctx.enter_context(nc.sbuf_tensor(name, shape, dt))

        def sem(name):
            return ctx.enter_context(nc.semaphore(name))

        xT = sb("xT", [P, KD, TT])
        hT = sb("hT", [P, KD, TT])
        W = sb("W", [P, 2, WCH])
        R = sb("R", [P, 31900])
        sm = sb("sm", [P, NORMS * KD + 12])
        lb = sb("lb", [P, 5, HA])
        cs = sb("cs", [P, 4, P])
        eps = sb("eps", [P, 8])
        pg = sb("pg", [1, NB * NPG], I32)
        PS = ctx.enter_context(nc.psum_tensor("PS", [P, 8, 512], F32))
        ident, mean_d, mean_v, ones = (cs[:, n, :] for n in range(4))

        def reg(at0, *shape):
            n = 1
            for s in shape:
                n *= s
            v = R[:, at0:at0 + n]
            if len(shape) == 2:
                v = v.rearrange("p (a b) -> p a b", b=shape[1])
            if len(shape) == 3:
                v = v.rearrange("p (a b c) -> p a b c", b=shape[1], c=shape[2])
            return v

        mix = reg(0, KD, TT)
        QT, FT, KT, VT = (reg(8256 + n * TT, TT) for n in range(4))
        SL, SN = reg(12384, NB, P), reg(13408, NB, P)
        o = 15416
        AL = reg(o, TT)
        G = reg(o + 1032, LEV, T)
        QE = reg(o + 8200, T)
        KE = reg(o + 9224, T)
        VH = reg(o + 10248, NC + 2, P)
        AM = reg(o + 11528, 2, (LEV + 1) * P)
        AT = reg(o + 13576, 2, P)
        KN = reg(o + 13832, 2, P)
        OT = reg(o + 14088, TT)
        S = reg(o + 15120, P)
        EE = reg(o + 15248, NC)
        VMs = reg(o + 11528, NB, P)[0:NB]
        WG = sb("WG", [P, KD, 3 * HB])
        HM = sb("HM", [P, LEV + 1, P])
        KVT = reg(8256, 4, TT)
        VSL, VWN = reg(12384, NC, P), reg(13408, NC, P)
        SNT = reg(14432, 6, P)
        GT = reg(15200, NC + 1, 3 * HB)
        NAT = reg(15416, 4, T)
        VX = reg(27712, TT)
        W1 = hT[:, :, :].rearrange("p a b -> p (a b)")[:, 0:2 * CMP * P].rearrange("p (k i m) -> p k i m", k=2, i=CMP)
        XC = [reg(19520 + n * 2 * PAST, 2, PAST) for n in range(2)]
        KC, VC = reg(27712, NB + 1, P), reg(28864, NB + 1, P)
        W2, PE_T, HID = reg(30016, 2, P), reg(30528, 2, CMP), reg(30272, 2, P)
        PB = reg(30592, 2)
        QB = reg(30016, NB, NB * HB)
        KW = hT[:, :, :].rearrange("p a b -> p (a b)")[:, 0:NB * WIN].rearrange("p (b n) -> p b n", b=NB)
        VW = hT[:, :, :].rearrange("p a b -> p (a b)")[:, NB * WIN:2 * NB * WIN].rearrange(
            "p (b t n) -> p b t n", b=NB, t=WIN // P)
        KB = [reg(19520 + n * PAST, PAST) for n in range(2)]
        VB = [reg(23616 + n * PAST, NPG, P) for n in range(2)]
        TRI, TA, TB = (reg(23616 + n * 1089, NBLK, NBLK)[0:64] for n in range(3))
        SX, SB = reg(15416, PAST + 1)[0:64], reg(17465, PAST + 1)[0:64]
        PTS, PTW = reg(17465, NPG, 64), reg(18489, WIN // P, 64)
        SW = reg(31214, WIN + 1)[0:64]
        PC, PCG = reg(30600, P)[0:64], reg(31086, P)[0:64]
        IT, PCT = reg(30728, 64), reg(30792, 64)
        SCO, RANK, SELB = (reg(30856 + n * NBLK, NBLK)[0:64] for n in range(3))
        GS, NM, DS, RI = (reg(30956 + 3 * n, 3)[0:64] for n in range(4))
        T8 = reg(30968, 2, NB)[0:64]
        G24 = reg(30984, 3 * HB)[0:64]
        OB = reg(31008, 64)
        PN = reg(31728, 2, 64)[0:NB]
        HF = HM[:, :, :].rearrange("p a b -> p (a b)")
        BW, CSN = HF[0:64, 0:WIN + 1], HF[:, WIN + 1:WIN + 1 + 330]
        SAME, COVER, BC = CSN[0:64, 0:64], CSN[0:NCS, 64:97], CSN[0:64, 97:97 + NCS]
        B8, B8T, H24 = CSN[0:64, 224:232], CSN[0:NB, 232:296], CSN[0:64, 296:320]
        NSL, VALID = CSN[:, 320:328], CSN[:, 328:329]
        TAB, TABC = reg(15416, T + 640), reg(17080, NC, 64)
        SS = reg(17592, 3, 1792)
        PT = reg(22968, 2, 14 * P)
        NG, DG, RG = (reg(26552 + 9 * n, 3, 3) for n in range(3))
        Z = reg(0, KF, TT)
        CY = reg(0, KD, TT)
        U = [reg(WK + n * WKW, WKW) for n in range(2)]
        Y = [reg(WK + (2 + n) * WKW, TT) for n in range(2)]
        o = WK + 4 * WKW
        FS = reg(o, 2 * KF, 2, NB)
        FW = reg(o + 704, 2 * KF, 3)
        FO = reg(o + 836, 2 * KF, 2 * (NB + 1))
        CSS = reg(o + 1628, KD, 2, NB)
        CSW = reg(o + 1756, KD, 3)
        CO = reg(o + 1780, KD, 2 * (NB + 1))
        SQ = [reg(WK + n * WKW + 2, TT) for n in range(2)]
        ACC, RS = reg(WK + 2 * WKW, TT), reg(WK + 3 * WKW, TT)

        x_in = [sem(f"x_in{k}") for k in range(KD)]
        c_in = sem("c_in")
        w_in = [sem(f"w_in{n}") for n in range(2)]
        ps_full = sem("ps_full")
        ps_free = [sem(f"ps_free{n}") for n in range(2)]
        sq_here = sem("sq_here")
        acc_here = sem("acc_here")
        h_here = sem("h_here")
        lb_exp = sem("lb_exp")
        lb_sum = sem("lb_sum")
        f_here = sem("f_here")
        k_here = sem("k_here")
        la_here = sem("la_here")
        a_here = sem("a_here")
        diff_here = sem("diff_here")
        exp_here = sem("exp_here")
        g_here = sem("g_here")
        sl_in = sem("sl_in")
        vm_here = sem("vm_here")
        sn_here = sem("sn_here")
        so_here = sem("so_here")
        at_here = sem("at_here")
        oc_here = sem("oc_here")
        s_here = sem("s_here")
        ot_sq = sem("ot_sq")
        mix_here = sem("mix_here")
        sn_out = sem("sn_out")
        s_out = sem("s_out")
        half_used = sem("half_used")
        nat_out = sem("nat_out")
        snat_out = sem("snat_out")
        w1_zero = sem("w1_zero")
        w1_in = sem("w1_in")
        xc_in0 = sem("xc_in0")
        xc_in1 = sem("xc_in1")
        vec_in = sem("vec_in")
        win_in = sem("win_in")
        bias_in = sem("bias_in")
        tri_in = sem("tri_in")
        qb_zero = sem("qb_zero")
        qb_here = sem("qb_here")
        sx_max = sem("sx_max")
        sx_exp = sem("sx_exp")
        pc_here = sem("pc_here")
        kb_in0 = sem("kb_in0")
        kb_in1 = sem("kb_in1")
        kb_used = sem("kb_used")
        vb_in0 = sem("vb_in0")
        vb_in1 = sem("vb_in1")
        vb_used = sem("vb_used")
        rank_done = sem("rank_done")
        sp_here = sem("sp_here")
        win_copied = sem("win_copied")
        tab_in = sem("tab_in")
        sc_full = sem("sc_full")
        sc_free = sem("sc_free")
        mx_here = sem("mx_here")
        ex_here = sem("ex_here")
        rg_here = sem("rg_here")
        p_here = sem("p_here")
        t_full = sem("t_full")
        t_free = sem("t_free")
        pv_full = sem("pv_full")
        pv_free = sem("pv_free")
        ob_here = sem("ob_here")
        rd_here = sem("rd_here")
        pw_here = sem("pw_here")
        pad_here = sem("pad_here")
        up_in = sem("up_in")
        y_here = sem("y_here")
        silu_here = sem("silu_here")
        z_here = sem("z_here")
        u_here = sem("u_here")
        st_here = sem("st_here")
        out_y = sem("out_y")
        out_st = sem("out_st")
        pb_here = sem("pb_here")
        sw_here = sem("sw_here")
        dve_done, act_done, pool_done = sem("dve_done"), sem("act_done"), sem("pool_done")

        def bank(u):
            return PS[:, 3 * (u % 2):3 * (u % 2) + 3, :]

        def wide(u):
            return bank(u)[:, :, 0:TW]

        def three(v):
            return v.rearrange("p (n m) -> p n m", n=TN)

        def wait_full(e, u, i=None, per=0):
            e.wait_ge(ps_full, at(i, per, u - 1))

        def wait_free(e, u, i=None, per=0):
            e.wait_ge(ps_free[u % 2], at(i, per // 2, u // 2))

        def wait_emptied(e, u, i=None, per=0):
            wait_free(e, u + 2, i, per)

        block = ctx.enter_context(nc.Block())
        U_N0, _ = PLAN["norm0"]
        U_H, W_H = PLAN["heads"]
        HP2, HT2 = 2 * HEAD_PS, 2 * HEAD_TILES
        U_KV, W_KV = PLAN["kv"]
        U_G, _ = PLAN["gates"]
        U_C, _ = PLAN["squeeze"]
        U_S, _ = PLAN["sample"]
        kv_tile = [U_KV] + [U_KV + 2 * n - 1 for n in range(1, 6)]
        kv_turn = [U_KV + 2 * n + 2 for n in range(5)] + [U_KV + 11]
        xc_in, kb_in, vb_in = (xc_in0, xc_in1), (kb_in0, kb_in1), (vb_in0, vb_in1)
        groups = [-(-(i + 1 + min(i + 1, 5) + 1) // 4) for i in range(NC)]

        def blocks(i):
            wide_ones = ([("slc", t, (NC - 1 - i + t) * P) for t in range(i + 1)]
                         + [("win", t, T + (4 - i + t) * P) for t in range(max(0, i - 4), i + 1)])
            return wide_ones[:1] + [("cmp", 0, T + 640)] + wide_ones[1:]

        units = [(i, j, half) for i in range(NC) for j in range(HA) for half in range(2)]
        group_at = [0]
        for i, _, _ in units:
            group_at.append(group_at[-1] + groups[i])

        def attention(ahead, first, second):
            for n in range(ahead):
                first(n, *units[n])
            for n in range(len(units)):
                if n + ahead < len(units):
                    first(n + ahead, *units[n + ahead])
                second(n, *units[n])

        def spans(i):
            return ((1, slice((NC - 1 - i) * P, T)), (2, slice(T + (4 - min(i, 4)) * P, T + 640)),
                    (0, slice(T + 640, T + 640 + NCP)))

        def pages_of(engine, first, what, dst, signal, free=lambda: None):
            with engine.Fori(0, NPG // 4) as j:
                pages = [engine.value_load(pg[0:1, ds(first + j * 4 + n, 1)], min_val=0, max_val=NPOOL - 1)
                         for n in range(4)]
                for n, page in enumerate(pages):
                    if n == 0:
                        free()
                    src = what[ds(page, 1)]
                    src = src.rearrange("a p b -> p a b" if len(what.shape) == 3 else "a p k b -> p (a k) b")
                    engine.dma_start(dst(j * 4 + n), src).then_inc(signal, 16)

        def cmp_pages(engine, b):
            def dst(j):
                return XC[b][:, :, ds(j * P, P)]

            pages_of(engine, b * NPG, cmp_t, dst, xc_in[b])
            with engine.Fori(0, NB // 2 - 1) as i:
                pages_of(engine, i * (2 * NPG) + (b + 2) * NPG, cmp_t, dst, xc_in[b],
                         lambda: wait_full(engine, U_C + 2 + 2 * b, i, 4))

        def slc_pages(engine, b):
            def key(j):
                return KB[b].unsqueeze(1)[:, :, ds(j * P, P)]

            def value(j):
                return VB[b][:, ds(j, 1), :]

            pages_of(engine, b * NPG, slc_kt, key, kb_in[b])
            with engine.Fori(0, NB // 2 - 1) as i:
                pages_of(engine, i * (2 * NPG) + (b + 2) * NPG, slc_kt, key, kb_in[b],
                         lambda: engine.wait_ge(kb_used, at(i, 2, b + 1)))
            engine.wait_ge(rank_done, 1)
            pages_of(engine, b * NPG, slc_v, value, vb_in[b])
            with engine.Fori(0, NB // 2 - 1) as i:
                pages_of(engine, i * (2 * NPG) + (b + 2) * NPG, slc_v, value, vb_in[b],
                         lambda: engine.wait_ge(vb_used, at(i, 2, b + 1)))

        @block.sync
        def _(sp):
            for k in range(KD):
                sp.dma_start(xT[:, k, :], x[:, k, :]).then_inc(x_in[k], 16)
            sp.dma_start(cs[:, :, :], cst).then_inc(c_in, 16)
            sp.dma_start(sm[:, :], small).then_inc(c_in, 16)
            sp.dma_start(HM[:, :, :], hmask).then_inc(c_in, 16)
            sp.dma_start(WG[:, :, :], wgate).then_inc(c_in, 16)
            sp.dma_start(pg[:, :], pages).then_inc(c_in, 16)
            for w in range(2):
                sp.dma_start(W[:, w, 0:D], wk8[w]).then_inc(w_in[w], 16)
            with sp.Fori(0, HA // 2) as i:
                for hh in range(2):
                    for k in range(HEAD_TILES):
                        w = W_H + hh * HEAD_TILES + k
                        wait_full(sp, U_H + hh * HEAD_PS + k, i, HP2)
                        sp.dma_start(W[:, w % 2, 0:D].unsqueeze(1),
                                     wk8[ds(i * HT2 + (w + 2), 1)].rearrange("a p n -> p a n")
                                     ).then_inc(w_in[w % 2], 16)
            for n in range(6):
                wait_full(sp, kv_tile[n])
                sp.dma_start(W[:, n % 2, 0:D], wk8[W_KV + n + 2]).then_inc(w_in[n % 2], 16)
            sp.wait_ge(w1_zero, 1)
            sp.wait_ge(s_out, 16 * (HA + 1))
            w1f = W1.rearrange("p k i m -> p (k i) m")
            for n in range(2):
                sp.dma_start(w1f[64 * n:64 * n + 64, :, 64 * n:64 * n + 64], w1).then_inc(w1_in, 16)
                sp.dma_start(W2[64 * n:64 * n + 64, :, 64 * n:64 * n + 64], w2).then_inc(w1_in, 16)
                sp.dma_start(PE_T[64 * n:64 * n + 64], pe_t).then_inc(w1_in, 16)

            sp.wait_ge(c_in, 16 * 5)
            wait_full(sp, U_G)
            sp.wait_ge(mix_here, HA)
            sp.dma_start(CSN, csn).then_inc(vec_in, 16)
            sp.dma_start(BW, bias_w).then_inc(vec_in, 16)
            cmp_pages(sp, 0)
            wait_full(sp, U_S - 1)
            sp.dma_start(KW, win_kt).then_inc(win_in, 16)
            sp.dma_start(VW, win_v).then_inc(win_in, 16)
            sp.wait_ge(nat_out, 16 * 6)
            sp.dma_start(SB, bias_s).then_inc(bias_in, 16)
            sp.dma_start(TRI, tri).then_inc(tri_in, 16)
            slc_pages(sp, 0)
            wait_full(sp, U_S + 7)
            sp.dma_start(TAB, table).then_inc(tab_in, 16)
            sp.dma_start(TABC, table_c).then_inc(tab_in, 16)
            sp.wait_ge(pv_full, len(units))

            def after_tiles(u, n, index, following):
                with sp.Fori(0, n // 2 - 1) as i:
                    for k in range(2):
                        wait_full(sp, u + k, i, 2)
                        sp.dma_start(W[:, k, 0:D].unsqueeze(1),
                                     wk8[ds(i * 2 + (index + 2 + k), 1)].rearrange("a p n -> p a n")
                                     ).then_inc(w_in[k], 16)
                for k in range(2):
                    wait_full(sp, u + n - 2 + k)
                    if following is not None:
                        sp.dma_start(W[:, k, 0:following.shape[2]], following[k]).then_inc(w_in[k], 16)

            def after_down(u, tiles_before, chunks, following):
                with sp.Fori(0, KD - 1) as i:
                    sp.wait_ge(half_used, at(i, 1, tiles_before + 1))
                    sp.dma_start(W[:, 0, :].unsqueeze(1), chunks[ds(i * 2 + 2, 1)].rearrange("a p n -> p a n")
                                 ).then_inc(w_in[0], 16)
                    wait_full(sp, u, i, 1)
                    sp.dma_start(W[:, 1, :].unsqueeze(1), chunks[ds(i * 2 + 3, 1)].rearrange("a p n -> p a n")
                                 ).then_inc(w_in[1], 16)
                sp.wait_ge(half_used, tiles_before + KD)
                if following is not None:
                    sp.dma_start(W[:, 0, 0:D], following[0]).then_inc(w_in[0], 16)
                wait_full(sp, u + KD - 1)
                if following is not None:
                    sp.dma_start(W[:, 1, 0:D], following[1]).then_inc(w_in[1], 16)

            def states(layer):
                sp.dma_start(FS, s_ff[layer]).then_inc(up_in, 16)
                sp.dma_start(FW, w_ff[layer]).then_inc(up_in, 16)

            states(0)
            sp.dma_start(CSS, s_sc).then_inc(up_in, 16)
            sp.dma_start(CSW, w_sc).then_inc(up_in, 16)
            i8 = PLAN["mix_out"][1]
            after_tiles(PLAN["mix_out"][0], KD, i8, wk8[i8 + KD:i8 + KD + 2])
            i8 += KD
            after_tiles(PLAN["up0"][0], 2 * KF, i8, wdn[0, 0:2])
            sp.wait_ge(st_here, 2 + 2 * KF)
            sp.dma_start(o_ff[0], FO).then_inc(out_st, 16)
            i8 += 2 * KF
            after_down(PLAN["down0"][0], 0, wdn[0], wk8[i8:i8 + 2])
            sp.wait_ge(out_st, 16)
            states(1)
            after_tiles(PLAN["conv_in"][0], 3 * KD, i8, wk8[i8 + 3 * KD:i8 + 3 * KD + 2])
            i8 += 3 * KD
            sp.wait_ge(st_here, 2 + 2 * KF + KD)
            sp.dma_start(o_sc, CO).then_inc(out_st, 16)
            after_tiles(PLAN["conv_out"][0], KD, i8, wk8[i8 + KD:i8 + KD + 2])
            i8 += KD
            after_tiles(PLAN["up1"][0], 2 * KF, i8, wdn[1, 0:2])
            sp.wait_ge(st_here, 2 + 4 * KF + KD)
            sp.dma_start(o_ff[1], FO).then_inc(out_st, 16)
            after_down(PLAN["down1"][0], KD, wdn[1], None)
            for k in range(KD):
                sp.wait_ge(h_here, 4 * KD + k + 1)
                sp.dma_start(o_y[:, k, :], hT[:, k, :]).then_inc(out_y, 16)
            sp.wait_ge(out_y, 16 * KD)
            sp.wait_ge(out_st, 16 * 3)
            sp.wait_ge(nat_out, 16 * 6)
            sp.wait_ge(snat_out, 16 * 6)
            sp.wait_ge(win_copied, 16)
            sp.wait_ge(sn_out, 16 * 5)
            sp.wait_ge(s_out, 16 * 5)

        @block.gpsimd
        def _(pool):
            pool.memset(eps[:, 0:1], EPS).then_inc(ps_free[0], 1)
            pool.memset(eps[:, 1:2], 0.0).then_inc(ps_free[1], 1)
            pool.memset(eps[:, 2:3], 0.0).then_inc(acc_here, 2)
            pool.memset(eps[:, 3:4], 0.0).then_inc(sn_out, 16)
            pool.memset(eps[:, 4:5], 0.0).then_inc(s_out, 16)
            pool.memset(eps[:, 5:6], 0.0).then_inc(st_here, 2)
            pool.memset(eps[:, 6:7], 0.0).then_inc(z_here, 1)
            with pool.Fori(0, HA // 2) as i:
                for hh in range(2):
                    u = U_H + hh * HEAD_PS
                    h = i * 2 + hh
                    pool.dma_start(SL, s_hgrn[:, ds(h, 1)].rearrange("b a k v -> k (b a) v")).then_inc(sl_in, 16)
                    pool.wait_ge(f_here, at(i, 2, hh + 1))
                    pool.tensor_tensor(KT, ones[:, 0:1].to_broadcast([P, TT]), FT, ALU.subtract).then_inc(k_here, 1)
                    pool.wait_ge(k_here, at(i, 2, hh + 1))
                    wait_emptied(pool, u + 1, i, HP2)
                    for lev in range(LEV):
                        g = G[:, lev, :].rearrange("p (n t m) -> p n t m", t=2, m=1 << lev)
                        q = QT[:, 0:T].rearrange("p (n t m) -> p n t m", t=2, m=1 << lev)
                        k = KT[:, 0:T].rearrange("p (n t m) -> p n t m", t=2, m=1 << lev)
                        pool.wait_ge(exp_here, at(i, 2 * (LEV + 2), hh * (LEV + 2) + lev + 2))
                        pool.tensor_tensor(g[:, :, 0, :], g[:, :, 0, :], k[:, :, 0, :], ALU.mult)
                        pool.tensor_tensor(g[:, :, 1, :], g[:, :, 1, :], q[:, :, 1, :], ALU.mult).then_inc(g_here, 1)
                    pool.wait_ge(s_here, at(i, 2 * (NC + 1), hh * (NC + 1) + 1))
                    pool.tensor_tensor(QE, QE, QT[:, 0:T], ALU.mult)
                    pool.wait_ge(exp_here, at(i, 2 * (LEV + 2), (hh + 1) * (LEV + 2)))
                    pool.tensor_tensor(KE, KE, KT[:, 0:T], ALU.mult).then_inc(g_here, 1)
                    pool.wait_ge(sn_here, at(i, 2, hh + 1))

            pool.dma_start(o_win_s[:, 0:WIN - 1], state_win[:, 1:WIN]).then_inc(win_copied, 16)
            pool.wait_ge(mix_here, HA)
            wait_full(pool, U_G)
            pool.memset(W2, 0.0)
            pool.memset(W1, 0.0).then_inc(w1_zero, 1)
            pool.wait_ge(c_in, 16 * 5)
            cmp_pages(pool, 1)
            wait_full(pool, U_S - 1)
            pool.memset(QB, 0.0).then_inc(qb_zero, 1)
            slc_pages(pool, 1)

            for n, (i, _, _) in enumerate(units):
                part = SS[:, n % 3, spans(i)[0][1]]
                pool.wait_ge(rg_here, n + 1)
                pool.tensor_scalar(part, part, RG[:, n % 3, 1:2], None, ALU.mult).then_inc(p_here, 1)

            def ffn_rows(before):
                with pool.Fori(0, KF // 2) as i:
                    for n in range(4):
                        t = i * 4 + n
                        pool.wait_ge(u_here, at(i, 4, before + n + 1))
                        o18 = FO[:, ds(t, 1), :]
                        smp = o18[:, :, 2:2 + 2 * NB].rearrange("p a (b r) -> p a b r", r=2)
                        pool.tensor_copy(o18[:, :, 0:2], U[n % 2][:, T:T + 2].unsqueeze(1))
                        pool.tensor_copy(smp[:, :, :, 1], U[n % 2][:, T + 2:T + 2 + NB].unsqueeze(1))
                        pool.tensor_copy(smp[:, :, :, 0], FS[:, ds(t, 1), 1, :]).then_inc(st_here, 1)

            pool.wait_ge(up_in, 16 * 4)
            ffn_rows(0)
            with pool.Fori(0, KD // 2) as i:
                for n in range(2):
                    t = i * 2 + n
                    pool.wait_ge(u_here, at(i, 2, 2 * KF + n + 1))
                    o18 = CO[:, ds(t, 1), :]
                    smp = o18[:, :, 2:2 + 2 * NB].rearrange("p a (b r) -> p a b r", r=2)
                    pool.tensor_copy(o18[:, :, 0:2], U[n][:, T:T + 2].unsqueeze(1))
                    pool.tensor_copy(smp[:, :, :, 1], U[n][:, T + 2:T + 2 + NB].unsqueeze(1))
                    pool.tensor_copy(smp[:, :, :, 0], CSS[:, ds(t, 1), 1, :]).then_inc(st_here, 1)
            pool.wait_ge(up_in, 16 * 6)
            ffn_rows(2 * KF + KD)

        @block.scalar
        def _(act):
            act.wait_ge(lb_sum, 1)
            act.activation(lb[:, 1:3, :], lb[:, 1:3, :], ACT.Exp).then_inc(lb_exp, 1)
            for k in range(KD):
                act.wait_ge(x_in[k], 16)
                act.wait_ge(acc_here, k + 1)
                act.activation(SQ[k % 2], xT[:, k, :], ACT.Square).then_inc(sq_here, 1)
            wait_full(act, U_N0)
            act.activation(three(RS), wide(U_N0), ACT.Sqrt, bias=eps[:, 0:1]).then_inc(ps_free[U_N0 % 2], 1)
            with act.Fori(0, HA // 2) as i:
                for hh in range(2):
                    u = U_H + hh * HEAD_PS
                    h = i * 2 + hh
                    wait_full(act, u, i, HP2)
                    act.activation(three(FT), wide(u), ACT.Sigmoid).then_inc(ps_free[u % 2], 1)
                    act.wait_ge(f_here, at(i, 2, hh + 1))
                    act.activation(AL, FT, ACT.Ln).then_inc(la_here, 1)
                    wait_full(act, u + 1, i, HP2)
                    act.activation(three(QT), wide(u + 1), ACT.Copy).then_inc(ps_free[(u + 1) % 2], 1)
                    act.wait_ge(a_here, at(i, 2 * NC, (hh + 1) * NC))
                    act.activation(QE, AL[:, 0:T], ACT.Exp).then_inc(exp_here, 1)
                    for lev in range(LEV):
                        act.wait_ge(diff_here, at(i, 2 * (LEV + 1), hh * (LEV + 1) + lev + 1))
                        act.activation(G[:, lev, :], G[:, lev, :], ACT.Exp).then_inc(exp_here, 1)
                    act.wait_ge(diff_here, at(i, 2 * (LEV + 1), (hh + 1) * (LEV + 1)))
                    act.activation(KE, KE, ACT.Exp).then_inc(exp_here, 1)
                    wait_full(act, u + 2, i, HP2)
                    act.activation(three(VT), wide(u + 2), ACT.Copy).then_inc(ps_free[u % 2], 1)
                    wait_full(act, u + 3, i, HP2)
                    act.activation(three(mix[:, ds(h, 1), :].rearrange("p a n -> p (a n)")), wide(u + 3), ACT.Sigmoid
                                   ).then_inc(ps_free[(u + 1) % 2], 1)
                    wait_full(act, u + 4, i, HP2)
                    act.activation(three(mix[:, ds(h + HA, 1), :].rearrange("p a n -> p (a n)")), wide(u + 4), ACT.Copy,
                                   scale=HD ** -0.5).then_inc(ps_free[u % 2], 1)
                    wait_full(act, u + 5, i, HP2)
                    v = bank(u + 5)
                    for n in range(2):
                        act.activation(VH[:, 4 * n:4 * n + 4, :], v[:, n, :].rearrange("p (a b) -> p a b", b=P), ACT.Copy)
                    act.activation(VH[0:NB, NC:NC + 2, :], v[0:NB, 2, 0:2 * P].rearrange("p (a b) -> p a b", b=P),
                                   ACT.Copy).then_inc(ps_free[(u + 1) % 2], 1)
                    act.wait_ge(sn_here, at(i, 2, hh + 1))
                    act.dma_start(o_hgrn_s[:, ds(h, 1)].rearrange("b a k v -> k (b a) v"), SN).then_inc(sn_out, 16)
                    act.wait_ge(s_here, at(i, 2 * (NC + 1), (hh + 1) * (NC + 1)))
                    act.dma_start(o_hgrn_p[ds(h, 1)].rearrange("a k v -> k a v"), S.unsqueeze(1)).then_inc(s_out, 16)
                    wait_emptied(act, u + 14, i, HP2)
                    act.activation(G[:, 0, 0:T], OT[:, 0:T], ACT.Square)
                    act.activation(G[:, 1, 0:NB], OT[:, T:TT], ACT.Square).then_inc(ot_sq, 1)
                    wait_full(act, u + 15, i, HP2)
                    act.activation(G[:, 2, :], bank(u + 15)[:, 0:2, :].rearrange("p a b -> p (a b)"), ACT.Sqrt, bias=eps[:, 0:1])
                    act.activation(G[:, 3, 0:NB], bank(u + 15)[:, 2, 0:NB], ACT.Sqrt,
                                   bias=eps[:, 0:1]).then_inc(ps_free[(u + 1) % 2], 1)

            act.wait_ge(sn_out, 16 * (HA + 1))
            kv_out = (o_cmp_p[:, 0], o_cmp_p[:, 1], o_slc_p[:, 0], o_slc_p[:, 1], o_win_p[:, 0], o_win_p[:, 1])
            kv_out_s = (o_cmp_s[:, 0], o_cmp_s[:, 1], o_slc_s[:, 0], o_slc_s[:, 1], o_win_s[:, WIN - 1, 0],
                        o_win_s[:, WIN - 1, 1])
            held = (KVT[:, 0, :], KVT[:, 1, :], KVT[:, 2, :], VX, KVT[:, 3, :], VX)
            turned = (NAT[:, 0], NAT[:, 1], NAT[:, 2], VSL.rearrange("p a b -> p (a b)"), NAT[:, 3],
                      VWN.rearrange("p a b -> p (a b)"))

            def hold(n):
                wait_full(act, kv_tile[n])
                act.activation(three(held[n]), wide(kv_tile[n]), ACT.Copy).then_inc(ps_free[kv_tile[n] % 2], 1)

            def turn(n):
                u = kv_turn[n]
                wait_full(act, u)
                act.activation(turned[n], bank(u)[:, 0:2, :].rearrange("p a b -> p (a b)"), ACT.Copy)
                act.activation(SNT[0:NB, n, :], bank(u)[0:NB, 2, 0:P], ACT.Copy).then_inc(ps_free[u % 2], 1)
                wait_emptied(act, u)
                rows = turned[n].rearrange("p (c d) -> p c d", d=P)
                if n >= 4:
                    rows = rows[:, NC - WIN // P:]
                act.dma_start(kv_out[n].rearrange("(c p) d -> p c d", p=P), rows).then_inc(nat_out, 16)
                act.dma_start(kv_out_s[n], SNT[0:NB, n, :]).then_inc(snat_out, 16)

            hold(0)
            act.wait_ge(mix_here, HA)
            for n in range(1, 6):
                hold(n)
                turn(n - 1)
            turn(5)
            wait_full(act, U_G)
            act.activation(GT[:, 0:NC, :].rearrange("p a b -> p (a b)"), bank(U_G)[:, 0, 0:NC * 24], ACT.Sigmoid)
            act.activation(GT[0:NB, NC, :], bank(U_G)[0:NB, 0, NC * 24:(NC + 1) * 24], ACT.Sigmoid
                           ).then_inc(ps_free[U_G % 2], 1)

            def squeeze(n, u, i, per, cols):
                hid = bank(u)
                wait_full(act, u, i, per)
                if i is None:
                    act.activation(PB, hid[:, 2, 0:2], ACT.Copy).then_inc(pb_here, 1)
                    act.wait_ge(pb_here, 1)
                act.activation(HID[:, 0, 0:cols], hid[:, 0, 0:cols], ACT.Silu, bias=PB[:, 0:1])
                act.activation(HID[:, 1, 0:cols], hid[:, 1, 0:cols], ACT.Silu, bias=PB[:, 1:2]).then_inc(ps_free[u % 2], 1)
                wait_full(act, u + 1, i, per)
                kv = bank(u + 1)
                act.activation(KC[:, ds(n, 1), 0:cols], kv[:, 0:1, 0:cols], ACT.Copy)
                act.activation(VC[0:cols, ds(n, 1), :], kv[0:cols, 1:2, 0:P], ACT.Copy).then_inc(ps_free[(u + 1) % 2], 1)

            squeeze(NB, U_C, None, 0, NCP)
            with act.Fori(0, NB // 2) as i:
                for b in range(2):
                    squeeze(i * 2 + b, U_C + 2 + 2 * b, i, 4, NCS)

            for n, (row, c) in enumerate(((PC[:, 0:NCS], 0), (SW, 2), (SX, 1))):
                act.wait_ge(sx_max, n + 1)
                act.activation(row, row, ACT.Exp, bias=NM[:, c:c + 1], accum_out=DS[:, c:c + 1]).then_inc(sx_exp, 1)

            def first(n, i, j, half):
                act.wait_ge(mx_here, n + 1)
                for c, cols in spans(i):
                    part = SS[:, n % 3, cols]
                    ins = act.activation(part, part, ACT.Exp, bias=NG[:, n % 3, c:c + 1], accum_out=DG[:, n % 3, c:c + 1])
                ins.then_inc(ex_here, 1)

            def heads_out(pair):
                i, j = pair // HA, pair % HA
                act.wait_ge(pv_full, 2 * pair + 2)
                act.activation(mix[:, HA + j, i * P:(i + 1) * P], PS[:, 6 + pair % 2, 0:P], ACT.Copy).then_inc(pv_free, 1)

            def second(n, i, j, half):
                for g in range(groups[i]):
                    m = len(blocks(i)[4 * g:4 * g + 4])
                    act.wait_ge(t_full, group_at[n] + g + 1)
                    act.activation(PT[:, half, 4 * g * P:(4 * g + m) * P], PS[:, 4 + (group_at[n] + g) % 2, 0:m * P], ACT.Copy
                                   ).then_inc(t_free, 1)
                if half == 0 and n:
                    heads_out(n // 2 - 1)

            act.wait_ge(ob_here, 1)
            attention(1, first, second)
            heads_out(len(units) // 2 - 1)

            def stage_squares(name, norm, tiles):
                act.wait_ge(st_here, 2 + tiles)
                u = PLAN[name][0]
                with act.Fori(0, KD // 2) as i:
                    for n in range(2):
                        act.wait_ge(acc_here, at(i, 2, KD * norm + n + 1))
                        wait_emptied(act, u + n, i, 2)
                        act.activation(SQ[n].unsqueeze(1), xT[:, ds(i * 2 + n, 1), :], ACT.Square).then_inc(sq_here, 1)
                u = PLAN[f"norm{norm}"][0]
                wait_full(act, u)
                act.activation(three(RS), wide(u), ACT.Sqrt, bias=eps[:, 0:1]).then_inc(ps_free[u % 2], 1)

            def ffn_up(name, tiles, pairs):
                u = PLAN[name][0]
                with act.Fori(0, KF // 2) as i:
                    for p in range(2):
                        for n in range(2):
                            t = u + 2 * p + n
                            wait_full(act, t, i, 4)
                            act.wait_ge(z_here, at(i, 2, pairs + p + 1))
                            act.wait_ge(st_here, at(i, 4, tiles + 2 * p + n + 1))
                            act.activation(three(U[n][:, 2:2 + TT]), wide(t), ACT.Copy).then_inc(u_here, 1)
                            act.activation(three(Y[n]), wide(t), ACT.Copy, scale=FW[:, ds(i * 4 + 2 * p + n, 1), 2]
                                           ).then_inc(ps_free[t % 2], 1)
                        act.wait_ge(y_here, at(i, 2, pairs + p + 1))
                        act.activation(Y[0], Y[0], ACT.Silu).then_inc(silu_here, 1)

            stage_squares("mix_out", 1, 0)
            act.wait_ge(up_in, 16 * 4)
            ffn_up("up0", 0, 0)
            stage_squares("down0", 2, 2 * KF)
            u = PLAN["conv_in"][0]
            with act.Fori(0, KD // 2) as i:
                for n in range(2):
                    act.wait_ge(u_here, at(i, 2, 2 * KF + n))
                    wait_full(act, u + 3 * n, i, 6)
                    act.activation(three(Y[0]), wide(u + 3 * n), ACT.Copy).then_inc(ps_free[(u + 3 * n) % 2], 1)
            stage_squares("conv_out", 3, 2 * KF + KD)
            act.wait_ge(up_in, 16 * 6)
            ffn_up("up1", 2 * KF + KD, KF)
            stage_squares("down1", 4, 4 * KF + KD)

        @block.vector
        def _(dve):
            own = Chain(dve, dve_done)
            dve.memset(ACC, 0.0).then_inc(dve_done, 1)
            own.k += 1
            dve.wait_ge(c_in, 16 * 5)
            lg = sm[:, NORMS * KD:NORMS * KD + 8].rearrange("p (a h) -> p a h", a=2)
            own.link(dve.tensor_tensor(lb[:, 0, :], lg[:, 0, :], lg[:, 1, :], ALU.max))
            dve.tensor_tensor(lb[:, 1, :], lg[:, 0, :], lb[:, 0, :], ALU.subtract)
            dve.tensor_tensor(lb[:, 2, :], lg[:, 1, :], lb[:, 0, :], ALU.subtract).then_inc(lb_sum, 1)
            dve.wait_ge(lb_exp, 1)
            own.link(dve.tensor_tensor(lb[:, 0, :], lb[:, 1, :], lb[:, 2, :], ALU.add))
            own.link(dve.reciprocal(lb[:, 0, :], lb[:, 0, :]))
            own.link(dve.tensor_tensor(lb[:, 3, :], lb[:, 1, :], lb[:, 0, :], ALU.mult))
            own.link(dve.tensor_scalar(lb[:, 4, :], lb[:, 3, :], -1.0, 1.0, ALU.mult, ALU.add))
            for k in range(KD):
                dve.wait_ge(sq_here, k + 1)
                dve.wait_ge(acc_here, k + 2)
                dve.tensor_tensor(ACC, ACC, SQ[k % 2], ALU.add).then_inc(acc_here, 1)
            wait_emptied(dve, U_N0)
            own.link(dve.reciprocal(RS, RS))
            for k in range(KD):
                dve.scalar_tensor_tensor(hT[:, k, :], xT[:, k, :], sm[:, k:k + 1], RS, ALU.mult, ALU.mult
                                         ).then_inc(h_here, 1)
            with own.turns(HA // 2, 2 * 11) as i:
                for hh in range(2):
                    u = U_H + hh * HEAD_PS
                    h = i * 2 + hh
                    wait_emptied(dve, u, i, HP2)
                    dve.tensor_scalar(FT, FT, lb[:, 4, ds(h, 1)], lb[:, 3, ds(h, 1)], ALU.mult, ALU.add
                                      ).then_inc(f_here, 1)
                    dve.wait_ge(la_here, at(i, 2, hh + 1))
                    for c in range(NC):
                        a = AL[:, c * P:(c + 1) * P]
                        dve.tensor_tensor_scan(a, ones, a, 0.0, ALU.mult, ALU.add).then_inc(a_here, 1)
                    dve.wait_ge(a_here, at(i, 2 * NC, (hh + 1) * NC))
                    for lev in range(LEV):
                        m = 1 << lev
                        a = AL[:, 0:T].rearrange("p (n t m) -> p n t m", t=2, m=m)
                        g = G[:, lev, :].rearrange("p (n t m) -> p n t m", t=2, m=m)
                        mid = a[:, :, 0, m - 1:m].to_broadcast([P, T // (2 * m), m])
                        dve.tensor_tensor(g[:, :, 0, :], mid, a[:, :, 0, :], ALU.subtract)
                        dve.tensor_tensor(g[:, :, 1, :], a[:, :, 1, :], mid, ALU.subtract).then_inc(diff_here, 1)
                    a = AL[:, 0:T].rearrange("p (n m) -> p n m", m=P)
                    dve.tensor_tensor(KE.rearrange("p (n m) -> p n m", m=P), a[:, :, P - 1:P].to_broadcast([P, NC, P]),
                                      a, ALU.subtract).then_inc(diff_here, 1)
                    dve.wait_ge(exp_here, at(i, 2 * (LEV + 2), hh * (LEV + 2) + 1))
                    dve.tensor_copy(EE.unsqueeze(2), QE.rearrange("p (n m) -> p n m", m=P)[:, :, P - 1:P]
                                    ).then_inc(s_here, 1)
                    wait_emptied(dve, u + 5, i, HP2)
                    dve.tensor_tensor(VMs, VH[0:NB, NC:NC + 1, :].to_broadcast([NB, NB, P]),
                                      ident[0:NB, 0:NB].unsqueeze(2).to_broadcast([NB, NB, P]), ALU.mult
                                      ).then_inc(vm_here, 1)
                    wait_full(dve, u + 6, i, HP2)
                    dve.wait_ge(sl_in, at(i, 32, 16 * (hh + 1)))
                    dve.wait_ge(sn_out, at(i, 32, 16 * (hh + 1)))
                    ps = bank(u + 6)
                    for b in range(NB):
                        ins = dve.scalar_tensor_tensor(SN[:, b, :], SL[:, b, :], FT[:, T + b:T + b + 1],
                                                       ps[:, b // 4, (b % 4) * P:(b % 4 + 1) * P], ALU.mult, ALU.add)
                    ins.then_inc(sn_here, 1)
                    dve.wait_ge(so_here, at(i, 2, hh + 1))
                    dve.tensor_copy(OT[:, T:TT], ps[:, 2, 0:NB]).then_inc(ps_free[u % 2], 1)
                    for c in range(NC):
                        uc = u + 7 + c
                        ps = bank(uc)
                        wait_full(dve, uc, i, HP2)
                        am = AM[:, c % 2, :]
                        own.link(dve.tensor_tensor(am, ps[:, 0:2, :].rearrange("p a b -> p (a b)"),
                                                   HM[:, :, :].rearrange("p a b -> p (a b)"), ALU.mult))
                        dve.tensor_reduce(AT[:, c % 2, :], am.rearrange("p (l t) -> p t l", t=P), AX_X, ALU.add)
                        dve.tensor_copy(KN[:, c % 2, :], ps[:, 2, 0:P]).then_inc(at_here, 1)
                        dve.wait_ge(oc_here, at(i, 2 * NC, hh * NC + c + 1))
                        if c == 0:
                            dve.wait_ge(s_out, at(i, 32, 16 * (hh + 1)))
                            dve.tensor_copy(S, ps[:, 2, 2 * P:3 * P]).then_inc(s_here, 1)
                        else:
                            dve.wait_ge(s_here, at(i, 2 * (NC + 1), hh * (NC + 1) + c + 1))
                            dve.scalar_tensor_tensor(S, S, EE[:, c:c + 1], ps[:, 2, 2 * P:3 * P], ALU.mult, ALU.add
                                                     ).then_inc(s_here, 1)
                        dve.tensor_copy(OT[:, c * P:(c + 1) * P], ps[:, 2, P:2 * P]).then_inc(ps_free[uc % 2], 1)
                    wait_emptied(dve, u + 15, i, HP2)
                    dve.reciprocal(G[:, 2, :], G[:, 2, :])
                    own.link(dve.reciprocal(G[:, 3, 0:NB], G[:, 3, 0:NB]))
                    gain = sm[:, ds(h + (NORMS * KD + 8), 1)]
                    own.up(dve.scalar_tensor_tensor(OT[:, 0:T], OT[:, 0:T], gain, G[:, 2, :], ALU.mult, ALU.mult))
                    own.link(dve.scalar_tensor_tensor(OT[:, T:TT], OT[:, T:TT], gain, G[:, 3, 0:NB], ALU.mult, ALU.mult))
                    m = mix[:, ds(h, 1), :].rearrange("p a n -> p (a n)")
                    dve.tensor_tensor(m, m, OT, ALU.mult).then_inc(mix_here, 1)

            wait_full(dve, U_S - 1)
            dve.wait_ge(qb_zero, 1)
            qf = QB.rearrange("p b c -> p (b c)")
            for half in range(2):
                rows = slice(64 * half, 64 * half + 64)
                for j in range(HA):
                    ins = dve.tensor_copy(qf[rows, j + 4 * half:j + 4 * half + 72 * (NB - 1) + 1:72],
                                          mix[rows, HA + j, T:TT])
            ins.then_inc(qb_here, 1)

            wait_full(dve, U_S)
            ps = bank(U_S)
            dve.tensor_tensor(G24, ps[0:64, 1, 0:24], H24, ALU.mult)
            dve.tensor_tensor(PC[:, 0:NCS], ps[0:64, 0, 0:NCS], BC, ALU.add).then_inc(ps_free[U_S % 2], 1)
            wait_emptied(dve, U_S)
            own.link(dve.tensor_reduce(GS, G24.rearrange("p (h c) -> p c h", c=3), AX_X, ALU.add))
            dve.tensor_reduce(NM[:, 0:1], PC[:, 0:NCS], AX_X, ALU.max, negate=True).then_inc(sx_max, 1)
            wait_full(dve, U_S + 1)
            ps = bank(U_S + 1)
            dve.wait_ge(vec_in, 32)
            dve.tensor_tensor(SW[:, 0:WIN], ps[0:64, 0, :], BW[:, 0:WIN], ALU.add)
            dve.tensor_tensor(SW[:, WIN:WIN + 1], ps[0:64, 1, 0:1], BW[:, WIN:WIN + 1], ALU.add
                              ).then_inc(ps_free[(U_S + 1) % 2], 1)
            wait_emptied(dve, U_S + 1)
            dve.tensor_reduce(NM[:, 2:3], SW, AX_X, ALU.max, negate=True).then_inc(sx_max, 1)
            dve.wait_ge(sx_exp, 1)
            own.link(dve.reciprocal(RI[:, 0:1], DS[:, 0:1]))
            dve.tensor_scalar(PC[:, 0:NCS], PC[:, 0:NCS], RI[:, 0:1], None, ALU.mult).then_inc(pc_here, 1)
            dve.wait_ge(pc_here, 1)
            dve.tensor_scalar(PCG[:, 0:NCS], PC[:, 0:NCS], GS[:, 0:1], None, ALU.mult).then_inc(pc_here, 1)
            wait_full(dve, U_S + 2)
            dve.tensor_copy(IT[0:NCS], bank(U_S + 2)[0:NCS, 0, 0:64]).then_inc(ps_free[U_S % 2], 1)
            dve.wait_ge(sx_exp, 2)
            own.link(dve.reciprocal(RI[:, 2:3], DS[:, 2:3]))
            dve.tensor_scalar(SW, SW, RI[:, 2:3], GS[:, 2:3], ALU.mult, ALU.mult).then_inc(sw_here, 1)
            wait_full(dve, U_S + 3)
            ps = bank(U_S + 3)
            dve.tensor_copy(SCO, ps[0:64, 0, 0:NBLK])
            dve.tensor_copy(PCT[0:NCS], ps[0:NCS, 1, 0:64]).then_inc(ps_free[(U_S + 3) % 2], 1)
            wait_emptied(dve, U_S + 3)
            own.link(dve.memset(SCO[:, 0:1], 1e9))
            own.link(dve.memset(SCO[:, NBLK - 2:NBLK], 1e9))
            dve.wait_ge(tri_in, 16)
            square = [64, NBLK, NBLK]
            other, mine = SCO.unsqueeze(1).to_broadcast(square), SCO.unsqueeze(2).to_broadcast(square)
            own.up(dve.tensor_tensor(TA, other, mine, ALU.is_gt))
            own.link(dve.tensor_tensor(TB, other, mine, ALU.is_equal))
            own.link(dve.tensor_tensor(TB, TB, TRI, ALU.mult))
            own.link(dve.tensor_tensor(TA, TA, TB, ALU.add))
            own.link(dve.tensor_reduce(RANK, TA, AX_X, ALU.add))
            dve.tensor_scalar(SELB, RANK, float(NSEL), -FAR, ALU.is_ge, ALU.mult).then_inc(rank_done, 1)
            dve.wait_ge(rank_done, 1)
            dve.wait_ge(bias_in, 16)
            sb3 = SB[:, 0:PAST].rearrange("p (b n) -> p b n", n=64)
            own.link(dve.tensor_tensor(sb3, sb3, SELB[:, 0:NBLK - 1].unsqueeze(2).to_broadcast([64, NBLK - 1, 64]), ALU.add))
            wait_full(dve, U_S + 5)
            d, e = bank(U_S + 4), bank(U_S + 5)
            flat = "p a b -> p (a b)"
            dve.tensor_tensor(SX[:, PAST:PAST + 1], d[0:64, 2, 0:1], SB[:, PAST:PAST + 1], ALU.add)
            dve.tensor_tensor(SX[:, 0:1024], d[0:64, 0:2, :].rearrange(flat), SB[:, 0:1024], ALU.add
                              ).then_inc(ps_free[U_S % 2], 1)
            dve.tensor_tensor(SX[:, 1024:PAST], e[0:64, 0:2, :].rearrange(flat), SB[:, 1024:PAST], ALU.add
                              ).then_inc(ps_free[(U_S + 1) % 2], 1)
            wait_emptied(dve, U_S + 4)
            wait_emptied(dve, U_S + 5)
            dve.tensor_reduce(NM[:, 1:2], SX, AX_X, ALU.max, negate=True).then_inc(sx_max, 1)
            dve.wait_ge(sx_exp, 3)
            own.link(dve.reciprocal(RI[:, 1:2], DS[:, 1:2]))
            own.link(dve.tensor_scalar(SX, SX, RI[:, 1:2], GS[:, 1:2], ALU.mult, ALU.mult))
            dve.wait_ge(sw_here, 1)
            own.up(dve.tensor_scalar(T8[:, 0, :], B8, SX[:, PAST:PAST + 1], None, ALU.mult))
            dve.tensor_scalar(T8[:, 1, :], B8, SW[:, WIN:WIN + 1], None, ALU.mult).then_inc(sp_here, 1)
            wait_full(dve, U_S + 6)
            ps = bank(U_S + 6)
            dve.tensor_copy(PTS.rearrange(flat), ps[:, 0:2, :].rearrange(flat))
            dve.tensor_copy(PTW.rearrange(flat), ps[:, 2, 0:256])
            dve.tensor_copy(PN.rearrange(flat), ps[0:NB, 2, 256:384]).then_inc(ps_free[U_S % 2], 1)
            wait_full(dve, U_S + 7)
            own.link(dve.tensor_reduce(OB, bank(U_S + 7)[:, 0, 0:320].rearrange("p (a c) -> p c a", c=64), AX_X, ALU.add))
            ob = OB.rearrange("p (b h) -> p h b", h=HB)
            dve.tensor_copy(mix[0:64, HA:2 * HA, T:TT], ob[0:64, 0:HA, :])
            dve.tensor_copy(mix[64:128, HA:2 * HA, T:TT], ob[64:128, HA:2 * HA, :]).then_inc(ps_free[(U_S + 7) % 2], 1)
            wait_emptied(dve, U_S + 7)
            own.k += 1
            dve.memset(OB[:, 0:1], 0.0).then_inc(dve_done, 1)
            dve.memset(OB[:, 1:2], 0.0).then_inc(ob_here, 1)

            psf = PS[:, :, :].rearrange(flat)
            dve.wait_ge(tab_in, 32)

            def first(n, i, j, half):
                dve.wait_ge(sc_full, n + 1)
                if n >= 3:
                    dve.wait_ge(pv_full, n - 2)
                for c, cols in spans(i):
                    tab = TABC[:, i, 0:NCP] if c == 0 else TAB[:, cols]
                    ins = dve.scalar_tensor_tensor(SS[:, n % 3, cols], tab, NSL[:, j + 4 * half:j + 4 * half + 1],
                                                   psf[:, cols], ALU.mult, ALU.add)
                ins.then_inc(sc_free, 1)
                dve.wait_ge(sc_free, n + 1)
                for c, cols in spans(i):
                    ins = dve.tensor_reduce(NG[:, n % 3, c:c + 1], SS[:, n % 3, cols], AX_X, ALU.max, negate=True)
                ins.then_inc(mx_here, 1)

            def second(n, i, j, half):
                rg = RG[:, n % 3, :]
                dve.wait_ge(ex_here, n + 1)
                dve.reciprocal(rg, DG[:, n % 3, :]).then_inc(rd_here, 1)
                dve.wait_ge(rd_here, n + 1)
                h = j + 4 * half
                gate = GT[:, i, 3 * h:3 * h + 3]
                if i == 0:
                    dve.scalar_tensor_tensor(rg[:, 0:1], rg[:, 0:1], VALID, gate[:, 0:1], ALU.mult, ALU.mult)
                    dve.tensor_tensor(rg[:, 1:3], rg[:, 1:3], gate[:, 1:3], ALU.mult).then_inc(rg_here, 1)
                else:
                    dve.tensor_tensor(rg, rg, gate, ALU.mult).then_inc(rg_here, 1)
                dve.wait_ge(rg_here, n + 1)
                for c, cols in spans(i)[1:]:
                    part = SS[:, n % 3, cols]
                    ins = dve.tensor_scalar(part, part, rg[:, c:c + 1], None, ALU.mult)
                ins.then_inc(pw_here, 1)

            attention(1, first, second)
            dve.wait_ge(pv_full, len(units))
            dve.wait_ge(nat_out, 16 * 6)
            dve.wait_ge(snat_out, 16 * 6)
            for n in range(2):
                ins = dve.memset(U[n][:, 0:2], 0.0)
            ins.then_inc(pad_here, 1)

            def residual(name, norm):
                u = PLAN[name][0]
                own.link(dve.memset(ACC, 0.0))
                with dve.Fori(0, KD // 2) as i:
                    for n in range(2):
                        wait_full(dve, u + n, i, 2)
                        t = xT[:, ds(i * 2 + n, 1), :].rearrange("p a (n m) -> p (a n) m", n=TN)
                        dve.tensor_tensor(t, t, wide(u + n), ALU.add).then_inc(ps_free[(u + n) % 2], 1)
                        dve.wait_ge(sq_here, at(i, 2, KD * norm + n + 1))
                        dve.wait_ge(acc_here, at(i, 2, KD * norm + n + 2))
                        dve.tensor_tensor(ACC, ACC, SQ[n], ALU.add).then_inc(acc_here, 1)
                u = PLAN[f"norm{norm}"][0]
                wait_emptied(dve, u)
                own.link(dve.reciprocal(RS, RS))
                for k in range(KD):
                    dve.scalar_tensor_tensor(hT[:, k, :], xT[:, k, :], sm[:, norm * KD + k:norm * KD + k + 1], RS,
                                             ALU.mult, ALU.mult).then_inc(h_here, 1)

            def taps(y, row, old, weight, last=None):
                own.up(dve.scalar_tensor_tensor(y[:, 0:T], row[:, 1:1 + T], weight(1), y[:, 0:T], ALU.mult, ALU.add))
                own.link(dve.scalar_tensor_tensor(y[:, T:TT], old(1), weight(1), y[:, T:TT], ALU.mult, ALU.add))
                own.up(dve.scalar_tensor_tensor(y[:, 0:T], row[:, 0:T], weight(0), y[:, 0:T], ALU.mult, ALU.add))
                ins = dve.scalar_tensor_tensor(y[:, T:TT], old(0), weight(0), y[:, T:TT], ALU.mult, ALU.add)
                if last is None:
                    own.link(ins)
                else:
                    ins.then_inc(last, 1)

            def ffn_up(name, tiles, pairs):
                u = PLAN[name][0]
                with own.turns(KF // 2, 14) as i:
                    for p in range(2):
                        for n in range(2):
                            t = 2 * p + n
                            wait_emptied(dve, u + t, i, 4)
                            dve.wait_ge(u_here, at(i, 4, tiles + t + 1))
                            taps(Y[n], U[n], lambda r: FS[:, ds(i * 4 + t, 1), r, :].rearrange("p a b -> p (a b)"),
                                 lambda r: FW[:, ds(i * 4 + t, 1), r], None if n else y_here)
                        dve.wait_ge(silu_here, at(i, 2, pairs + p + 1))
                        dve.tensor_tensor(Z[:, ds(i * 2 + p, 1), :], Y[0].unsqueeze(1), Y[1].unsqueeze(1), ALU.mult
                                          ).then_inc(z_here, 1)

            residual("mix_out", 1)
            ffn_up("up0", 0, 0)
            dve.wait_ge(z_here, 1 + KF)
            residual("down0", 2)
            u = PLAN["conv_in"][0]
            with own.turns(KD // 2, 8) as i:
                for n in range(2):
                    t = i * 2 + n
                    v = u + 3 * n
                    wait_full(dve, v + 1, i, 6)
                    wait_emptied(dve, v, i, 6)
                    dve.wait_ge(st_here, at(i, 2, 2 * KF + n + 1))
                    dve.tensor_tensor(three(U[n][:, 2:2 + TT]), three(Y[0]), wide(v + 1), ALU.mult
                                      ).then_inc(u_here, 1)
                    dve.wait_ge(u_here, at(i, 2, 2 * KF + n + 1))
                    dve.tensor_scalar(Y[1], U[n][:, 2:2 + TT], CSW[:, ds(t, 1), 2], None, ALU.mult
                                      ).then_inc(ps_free[(v + 1) % 2], 1)
                    wait_emptied(dve, v + 1, i, 6)
                    taps(Y[1], U[n], lambda r: CSS[:, ds(t, 1), r, :].rearrange("p a b -> p (a b)"),
                         lambda r: CSW[:, ds(t, 1), r])
                    wait_full(dve, v + 2, i, 6)
                    dve.tensor_tensor(CY[:, ds(t, 1), :].rearrange("p a (n m) -> p (a n) m", n=TN), three(Y[1]),
                                      wide(v + 2), ALU.mult).then_inc(ps_free[v % 2], 1)
            wait_emptied(dve, PLAN["conv_out"][0] - 1)
            residual("conv_out", 3)
            ffn_up("up1", 2 * KF + KD, KF)
            dve.wait_ge(z_here, 1 + 2 * KF)
            residual("down1", 4)

        @block.tensor
        def _(pe):
            def norm(u, n):
                pe.wait_ge(c_in, 16 * 5)
                pe.wait_ge(acc_here, 2 + KD * (n + 1))
                wait_free(pe, u)
                for m in range(TN):
                    ins = pe.matmul(wide(u)[:, m, :], mean_d, ACC[:, m * TW:(m + 1) * TW], start=True, stop=True)
                ins.then_inc(ps_full, 1)

            def tile(u, w, src, i=None, up=0, wp=0, ready=0):
                wait_free(pe, u, i, up)
                pe.wait_ge(w_in[w % 2], at(i, 8 * wp, 16 * (w // 2 + 1)))
                for k in range(KD):
                    if ready:
                        pe.wait_ge(h_here, ready + k)
                    for m in range(TN):
                        ins = pe.matmul(wide(u)[:, m, :], W[:, w % 2, k * P:(k + 1) * P],
                                        src[:, k, m * TW:(m + 1) * TW], start=(k == 0), stop=(k == KD - 1))
                ins.then_inc(ps_full, 1)

            norm(U_N0, 0)
            pe.wait_ge(h_here, KD)
            with pe.Fori(0, HA // 2) as i:
                for hh in range(2):
                    u = U_H + hh * HEAD_PS
                    for k in range(HEAD_TILES):
                        tile(u + k, W_H + hh * HEAD_TILES + k, hT, i, HP2, HT2)
                    wait_free(pe, u + 5, i, HP2)
                    wait_emptied(pe, u + 2, i, HP2)
                    pe.wait_ge(k_here, at(i, 2, hh + 1))
                    ps = bank(u + 5)
                    for c in range(NC):
                        pe.transpose(ps[:, c // 4, (c % 4) * P:(c % 4 + 1) * P], VT[:, c * P:(c + 1) * P], ident)
                    pe.transpose(ps[0:NB, 2, 0:P], VT[:, T:TT], ident)
                    pe.transpose(ps[0:NB, 2, P:2 * P], KT[:, T:TT], ident).then_inc(ps_full, 1)
                    wait_free(pe, u + 6, i, HP2)
                    pe.wait_ge(vm_here, at(i, 2, hh + 1))
                    pss = bank(u + 6)
                    for n in range(2):
                        ins = pe.matmul(pss[:, n, :], VH[0:NB, NC + 1, :], VMs[:, 4 * n:4 * n + 4, :],
                                        start=True, stop=True)
                    ins.then_inc(ps_full, 1)

                    def att(c):
                        uc = u + 7 + c
                        wait_free(pe, uc, i, HP2)
                        ps = bank(uc)
                        tok = slice(c * P, (c + 1) * P)
                        pe.matmul(ps[:, 0, 0:P], KT[:, tok], QT[:, tok], start=True, stop=True)
                        for lev in range(LEV):
                            n = lev + 1
                            pe.matmul(ps[:, n // 4, (n % 4) * P:(n % 4 + 1) * P], G[:, lev, tok], G[:, lev, tok],
                                      start=True, stop=True)
                        pe.transpose(ps[:, 2, 0:P], KE[:, tok], ident).then_inc(ps_full, 1)

                    pe.wait_ge(g_here, at(i, 2 * (LEV + 1), (hh + 1) * (LEV + 1)))
                    att(0)
                    pe.wait_ge(sn_here, at(i, 2, hh + 1))
                    for b in range(NB):
                        ins = pe.matmul(pss[:, 2, b:b + 1], SN[:, b, :], QT[:, T + b:T + b + 1], start=True, stop=True)
                    ins.then_inc(so_here, 1)
                    for c in range(NC):
                        if c + 1 < NC:
                            att(c + 1)
                        ps = bank(u + 7 + c)
                        tok = slice(c * P, (c + 1) * P)
                        pe.wait_ge(at_here, at(i, 2 * NC, hh * NC + c + 1))
                        pe.matmul(ps[:, 2, P:2 * P], VH[:, c, :], AT[:, c % 2, :], start=True, stop=(c == 0))
                        if c:
                            pe.wait_ge(s_here, at(i, 2 * (NC + 1), hh * (NC + 1) + c + 1))
                            pe.matmul(ps[:, 2, P:2 * P], S, QE[:, tok], start=False, stop=True)
                        pe.matmul(ps[:, 2, 2 * P:3 * P], KN[:, c % 2, :], VH[:, c, :], start=True, stop=True
                                  ).then_inc(oc_here, 1)
                    wait_free(pe, u + 15, i, HP2)
                    pe.wait_ge(ot_sq, at(i, 2, hh + 1))
                    ps = bank(u + 15)
                    for n in range(2):
                        pe.matmul(ps[:, n, :], mean_v, G[:, 0, n * 512:(n + 1) * 512], start=True, stop=True)
                    pe.matmul(ps[:, 2, 0:NB], mean_v, G[:, 1, 0:NB], start=True, stop=True).then_inc(ps_full, 1)

            held = (KVT[:, 0, :], KVT[:, 1, :], KVT[:, 2, :], VX, KVT[:, 3, :], VX)

            def turn(n):
                u = kv_turn[n]
                wait_free(pe, u)
                wait_emptied(pe, kv_tile[n])
                ps = bank(u)
                for c in range(NC):
                    pe.transpose(ps[:, c // 4, (c % 4) * P:(c % 4 + 1) * P], held[n][:, c * P:(c + 1) * P], ident)
                pe.transpose(ps[0:NB, 2, 0:P], held[n][:, T:TT], ident).then_inc(ps_full, 1)

            tile(kv_tile[0], W_KV, hT)
            for n in range(1, 6):
                tile(kv_tile[n], W_KV + n, hT)
                turn(n - 1)
            turn(5)
            wait_free(pe, U_G)
            for c in range(NC + 1):
                tok = slice(c * P, min((c + 1) * P, TT))
                for k in range(KD):
                    ins = pe.matmul(bank(U_G)[0:min(P, TT - c * P), 0, c * 24:(c + 1) * 24], hT[:, k, tok], WG[:, k, :],
                                    start=(k == 0), stop=(k == KD - 1))
            ins.then_inc(ps_full, 1)

            def squeeze(u, i, per, cols, source):
                wait_free(pe, u, i, per)
                ps = bank(u)
                for k in range(2):
                    for r in range(CMP):
                        ins = pe.matmul(ps[:, k, 0:cols], W1[:, k, r, :], source(k, r), start=(r == 0), stop=(r == CMP - 1))
                if i is None:
                    for k in range(2):
                        for r in range(CMP):
                            ins = pe.matmul(ps[:, 2, k:k + 1], W1[:, k, r, :], PE_T[:, k, r:r + 1],
                                            start=(r == 0), stop=(r == CMP - 1))
                ins.then_inc(ps_full, 1)
                wait_free(pe, u + 1, i, per)
                wait_emptied(pe, u, i, per)
                kv = bank(u + 1)
                pe.matmul(kv[:, 0, 0:cols], W2[:, 0, :], HID[:, 0, 0:cols], start=True, stop=True)
                pe.matmul(kv[0:cols, 1, 0:P], HID[:, 1, 0:cols], W2[:, 1, :], start=True, stop=True).then_inc(ps_full, 1)

            pe.wait_ge(w1_in, 16 * 6)
            squeeze(U_C, None, 0, NCP, lambda k, r: KVT[:, k, r:r + STRIDE * (NCP - 1) + 1:STRIDE])
            with pe.Fori(0, NB // 2) as i:
                for b in range(2):
                    pe.wait_ge(xc_in[b], at(i, 16 * NPG, 16 * NPG))
                    squeeze(U_C + 2 + 2 * b, i, 4, NCS,
                            lambda k, r: XC[b][:, k, r:r + STRIDE * (NCS - 1) + 1:STRIDE])

            pe.wait_ge(qb_here, 1)
            pe.wait_ge(vec_in, 32)
            wait_emptied(pe, U_S - 1)
            wait_free(pe, U_S)
            ps = bank(U_S)
            pe.matmul(ps[0:64, 1, 0:24], B8T, GT[0:NB, NC, :], start=True, stop=True)
            for b in range(NB):
                ins = pe.matmul(ps[0:64, 0, 0:NCS], QB[:, b, :], KC[:, b, 0:NCS], start=(b == 0), stop=(b == NB - 1))
            ins.then_inc(ps_full, 1)
            wait_free(pe, U_S + 1)
            pe.wait_ge(win_in, 32)
            ps = bank(U_S + 1)
            for b in range(NB):
                pe.matmul(ps[0:64, 0, :], QB[:, b, :], KW[:, b, :], start=(b == 0), stop=(b == NB - 1))
            for b in range(NB):
                ins = pe.matmul(ps[0:64, 1, 0:1], QB[:, b, :], KVT[:, 3, T + b:T + b + 1], start=(b == 0),
                                stop=(b == NB - 1))
            ins.then_inc(ps_full, 1)
            wait_free(pe, U_S + 2)
            pe.wait_ge(pc_here, 1)
            pe.matmul(bank(U_S + 2)[0:NCS, 0, 0:64], PC[:, 0:NCS], SAME, start=True, stop=True).then_inc(ps_full, 1)
            wait_free(pe, U_S + 3)
            ps = bank(U_S + 3)
            pe.wait_ge(pc_here, 2)
            pe.transpose(ps[0:NCS, 1, 0:64], PCG[:, 0:NCS], ident[0:64, 0:64])
            wait_emptied(pe, U_S + 2)
            pe.matmul(ps[0:64, 0, 0:NBLK], IT[0:NCS], COVER, start=True, stop=True).then_inc(ps_full, 1)
            wait_free(pe, U_S + 4)
            wait_free(pe, U_S + 5)
            d, e = bank(U_S + 4), bank(U_S + 5)
            for b in range(NB):
                pe.matmul(d[0:64, 2, 0:1], QB[:, b, :], KVT[:, 2, T + b:T + b + 1], start=(b == 0), stop=(b == NB - 1))
            for b in range(NB):
                pe.wait_ge(kb_in[b % 2], 16 * NPG * (b // 2 + 1))
                for n in range(4):
                    ins = pe.matmul((d, e)[n // 2][0:64, n % 2, :], QB[:, b, :], KB[b % 2][:, n * 512:(n + 1) * 512],
                                    start=(b == 0), stop=(b == NB - 1))
                    if b == NB - 1 and n % 2:
                        ins.then_inc(ps_full, 1)
                if b < NB - 1:
                    ins.then_inc(kb_used, 1)
            wait_free(pe, U_S + 6)
            pe.wait_ge(sp_here, 1)
            ps = bank(U_S + 6)
            i64 = ident[0:64, 0:64]
            for t in range(NPG):
                pe.transpose(ps[:, t // 8, (t % 8) * 64:(t % 8 + 1) * 64], SX[:, t * P:(t + 1) * P], i64)
            for t in range(WIN // P):
                pe.transpose(ps[:, 2, t * 64:(t + 1) * 64], SW[:, t * P:(t + 1) * P], i64)
            for n in range(2):
                ins = pe.matmul(ps[0:NB, 2, 256 + 64 * n:320 + 64 * n], T8[:, n, :], i64, start=True, stop=True)
            ins.then_inc(ps_full, 1)
            wait_free(pe, U_S + 7)
            wait_emptied(pe, U_S + 6)
            ps = bank(U_S + 7)
            pe.matmul(ps[:, 0, 128:192], SNT[0:NB, 3, :], PN[:, 0, :], start=True, stop=True)
            pe.matmul(ps[:, 0, 256:320], SNT[0:NB, 5, :], PN[:, 1, :], start=True, stop=True)
            for b in range(NB):
                pe.matmul(ps[:, 0, b * 8:b * 8 + 8], VC[0:NCS, b, :], PCT[0:NCS, b * 8:b * 8 + 8], start=True, stop=True)
                for t in range(WIN // P):
                    pe.matmul(ps[:, 0, 192 + b * 8:200 + b * 8], VW[:, b, t, :], PTW[:, t, b * 8:b * 8 + 8],
                              start=(t == 0), stop=(t == WIN // P - 1))
            for b in range(NB):
                pe.wait_ge(vb_in[b % 2], 16 * NPG * (b // 2 + 1))
                for t in range(NPG):
                    ins = pe.matmul(ps[:, 0, 64 + b * 8:72 + b * 8], VB[b % 2][:, t, :], PTS[:, t, b * 8:b * 8 + 8],
                                    start=(t == 0), stop=(t == NPG - 1))
                if b < NB - 1:
                    ins.then_inc(vb_used, 1)
            ins.then_inc(ps_full, 1)

            def first(n, i, j, half):
                rows = slice(64 * half, 64 * half + 64)
                q = mix[rows, HA + j, i * P:(i + 1) * P]
                psf = PS[:, :, :].rearrange("p a b -> p (a b)")
                if n:
                    pe.wait_ge(sc_free, n)
                (_, slc), (_, win), (_, cmp) = spans(i)
                for cols, key, src in (slc, 0, 2), (win, max(0, i - 4) * P, 3):
                    lo = cols.start
                    while lo < cols.stop:
                        end = min(cols.stop, (lo // 512 + 1) * 512)
                        pe.matmul(psf[:, lo:end], q, KVT[rows, src, key:key + end - lo], start=True, stop=True)
                        lo, key = end, key + end - lo
                pe.matmul(psf[:, cmp], q, KC[rows, NB, 0:NCP], start=True, stop=True).then_inc(sc_full, 1)

            def second(n, i, j, half):
                bl = blocks(i)
                rows = slice(64 * half, 64 * half + 64)

                def values(g):
                    pe.wait_ge(t_free, group_at[n] + g + 1)
                    if g == 0 and half == 0 and n >= 4:
                        pe.wait_ge(pv_free, n // 2 - 1)
                    for b, (kind, t, _) in enumerate(bl[4 * g:4 * g + 4]):
                        p = PT[:, half, (4 * g + b) * P:(4 * g + b + 1) * P]
                        if kind == "cmp":
                            v, p = VC[0:NCP, NB, rows], p[0:NCP]
                        else:
                            v = (VSL if kind == "slc" else VWN)[:, t, rows]
                        ins = pe.matmul(PS[rows, 6 + n // 2 % 2, 0:P], v, p, start=(g == b == 0),
                                        stop=(4 * g + b == len(bl) - 1), skip_group_check=True)
                    return ins

                pe.wait_ge(p_here, n + 1)
                pe.wait_ge(pw_here, n + 1)
                for g in range(groups[i]):
                    if group_at[n] + g >= 2:
                        pe.wait_ge(t_free, group_at[n] + g - 1)
                    for b, (kind, _, c) in enumerate(bl[4 * g:4 * g + 4]):
                        m = NCP if kind == "cmp" else P
                        ins = pe.transpose(PS[0:m, 4 + (group_at[n] + g) % 2, b * P:(b + 1) * P],
                                           SS[:, n % 3, c:c + m], ident)
                    ins.then_inc(t_full, 1)
                    if g:
                        values(g - 1)
                values(groups[i] - 1).then_inc(pv_full, 1)

            wait_free(pe, U_S + 8)
            wait_free(pe, U_S + 9)
            attention(2, first, second)
            pe.wait_ge(pv_free, HA * NC)

            def stage(name, src, count=None, source_sem=None, base=0):
                u, w = PLAN[name]
                n = PLAN_N[name]
                with pe.Fori(0, n // 2) as i:
                    for k in range(2):
                        wait_free(pe, u + k, i, 2)
                        pe.wait_ge(w_in[(w + k) % 2], at(i, 16, 16 * ((w + k) // 2 + 1)))
                        for f in range(KD):
                            if k == 0 and source_sem is not None:
                                pe.wait_ge(source_sem, base + f + 1)
                            for m in range(TN):
                                ins = pe.matmul(wide(u + k)[:, m, :], W[:, (w + k) % 2, f * P:(f + 1) * P],
                                                src[:, f, m * TW:(m + 1) * TW], start=(f == 0), stop=(f == KD - 1))
                        ins.then_inc(ps_full, 1)

            def down(name, base):
                u, w = PLAN[name]
                with pe.Fori(0, KD // 2) as i:
                    for k in range(2):
                        wait_free(pe, u + k, i, 2)
                        for n in range(2):
                            pe.wait_ge(w_in[n], at(i, 32, 16 * ((w + 2 * k) // 2 + 1)))
                            for f in range(KH):
                                g = n * KH + f
                                if k == 0:
                                    pe.wait_ge(z_here, base + g + 2)
                                for m in range(TN):
                                    ins = pe.matmul(wide(u + k)[:, m, :], W[:, n, f * P:(f + 1) * P],
                                                    Z[:, g, m * TW:(m + 1) * TW], start=(g == 0), stop=(g == KF - 1))
                            ins.then_inc(ps_full if n else half_used, 1)

            stage("mix_out", mix)
            norm(PLAN["norm1"][0], 1)
            stage("up0", hT, source_sem=h_here, base=KD)
            down("down0", 0)
            norm(PLAN["norm2"][0], 2)
            stage("conv_in", hT, source_sem=h_here, base=2 * KD)
            wait_emptied(pe, PLAN["conv_out"][0] - 1)
            stage("conv_out", CY)
            norm(PLAN["norm3"][0], 3)
            stage("up1", hT, source_sem=h_here, base=3 * KD)
            down("down1", KF)
            norm(PLAN["norm4"][0], 4)


def kernel(**inputs):
    import concourse.bacc as bacc
    from concourse.bass_utils import run_bass_kernel_spmd as run

    a = {k: np.asarray(v) for k, v in inputs.items()}
    r = np.arange

    def columns(w, cols):
        k = w.shape[0] // P
        return w[:, cols].reshape(k, P, len(cols)).transpose(1, 0, 2).reshape(P, -1)

    def feature(v):
        v = v.reshape(v.shape[:-1] + (-1, P))
        return np.moveaxis(v, (-1, -2), (0, 1))

    ab, ab_out = a["ab_w_in"][0], a["ab_w_out"][0]
    pair = [np.concatenate([j * HD + r(HD), (j + HA) * HD + r(HD)]) for j in range(HA)]
    chunks = []
    for h in range(HA):
        chunks += [columns(ab, off + h * P + r(P)) for off in (512, 0, 1024, 1536)] + [columns(ab, 2048 + pair[h])]
    chunks += [columns(ab, 2560 + n * P + r(P)) for n in range(6)]
    mixed = np.concatenate([r(HA * P)] + [HA * P + p for p in pair])
    chunks += [columns(ab_out[mixed], n * P + r(P)) for n in range(KD)]
    hidden = np.stack([r(KF), KF + r(KF)], 1).reshape(-1)
    up = [[columns(a["ffn_up"][n], t * P + r(P)) for t in hidden] for n in range(2)]
    three = np.stack([r(KD), KD + r(KD), 2 * KD + r(KD)], 1).reshape(-1)
    chunks += up[0] + [columns(a["c_w_in"][0], t * P + r(P)) for t in three]
    chunks += [columns(a["c_w_out"][0], t * P + r(P)) for t in range(KD)] + up[1]
    down = [[columns(a["ffn_down"][n][h * KH * P:(h + 1) * KH * P], t * P + r(P)) for t in range(KD) for h in range(2)]
            for n in range(2)]

    x = np.concatenate([a["x_prompt"][0], a["x_sample"][:, 0]])
    small = np.concatenate([feature(v) for v in (
        a["norm_mix"][0], a["norm_ffn"][0], a["norm_mix"][1], a["norm_ffn"][1], a["norm_final"],
        a["hgrn_lb_logits"][0], a["hgrn_lb_logits"][1], a["hgrn_norm"][0])], 1)

    s, t = np.meshgrid(r(P), r(P), indexing="ij")
    cst = np.zeros((P, 4, P), np.float32)
    cst[:, 0], cst[:, 1], cst[:, 2], cst[:, 3] = np.eye(P), 1 / D, 1 / P, 1
    hmask = np.zeros((P, LEV + 1, P), np.float32)
    hmask[:, 0] = np.eye(P)
    for lev in range(LEV):
        m = 1 << lev
        hmask[:, lev + 1] = (s // (2 * m) == t // (2 * m)) & (s // m % 2 == 0) & (t // m % 2 == 1)
    slope = 2.0 ** (-8.0 * (r(HB) + 1) / HB)
    row = r(NB * HB)
    csn = np.zeros((P, 330), np.float32)
    csn[0:64, 0:64] = row[:, None] // HA == row[None] // HA
    start, block = r(NCS)[:, None] * STRIDE, r(NBLK)[None] * 64
    csn[0:NCS, 64:97] = (start < block + 64) & (start + CMP > block)
    by_row = slope[row % HB][:, None]
    csn[0:64, 97:97 + NCS] = -by_row * (PAST - (start[:, 0] + CMP - 1))[None]
    csn[0:64, 224:232] = row[:, None] // HB == r(NB)[None]
    csn[0:NB, 232:296] = row[None] // HB == r(NB)[:, None]
    csn[0:64, 296:320] = row[:, None] % HB == r(3 * HB)[None] // 3
    csn[:, 320:328] = -slope
    csn[:, 328] = r(P) >= CMP - 1
    bias_w = (-by_row * (WIN - r(WIN + 1))[None]).astype(np.float32)
    bias_w[:, 0] = -FAR
    bias_s = (-by_row * (PAST - r(PAST + 1))[None]).astype(np.float32)
    tri = np.broadcast_to((r(NBLK)[None] < r(NBLK)[:, None]).astype(np.float32), (64, NBLK, NBLK))
    far = lambda dist, keep: np.where(keep, dist, FAR).astype(np.float32)
    dist = r(P)[:, None] - (r(T) - (T - P))[None]
    dist_w = r(P)[:, None] - (r(640) - 512)[None]
    table = np.concatenate([far(dist, dist >= 0), far(dist_w, (dist_w >= 0) & (dist_w < WIN))], 1)
    dist_c = (r(NC) * P)[None, :, None] + r(P)[:, None, None] - (r(64) * STRIDE + CMP - 1)[None, None]
    table_c = far(dist_c, dist_c >= 0)

    def rows_t(v):
        return feature(v).transpose(0, 1, 3, 2)

    w1 = a["cmp_w1"][0].reshape(2, CMP, HD, 64).transpose(2, 0, 1, 3).reshape(HD, 2 * CMP, 64)
    win = a["state_win_kv"][0].reshape(NB, WIN, 2, P)
    cmp_pool, slc_pool = (a[n].reshape(NPOOL, PAGE, 2, P) for n in ("cache_cmp_kv", "cache_slc_kv"))
    given = {
        "x": feature(x).transpose(0, 1, 2), "wk8": np.stack(chunks), "wdn": np.stack([np.stack(d) for d in down]),
        "small": small, "cst": cst, "hmask": hmask, "s_hgrn": a["state_hgrn"][0],
        "wgate": columns(ab, 3328 + r(24)).reshape(P, KD, 24), "pages": a["page_table"].reshape(1, -1),
        "cmp_t": cmp_pool.transpose(0, 3, 2, 1), "slc_kt": slc_pool[:, :, 0].transpose(0, 2, 1), "slc_v": slc_pool[:, :, 1],
        "win_kt": win[:, :, 0].transpose(2, 0, 1),
        "win_v": win[:, :, 1].reshape(NB, WIN // P, P, P).transpose(2, 0, 1, 3), "state_win": win,
        "w1": w1, "w2": a["cmp_w2"][0].transpose(1, 0, 2), "pe_t": a["cmp_pe"][0].transpose(2, 0, 1),
        "csn": csn, "bias_w": bias_w, "bias_s": bias_s, "tri": tri, "table": table, "table_c": table_c,
        "s_ff": np.stack([rows_t(a["state_ffn"][n])[:, hidden] for n in range(2)]),
        "w_ff": np.stack([feature(a["ffn_conv"][n])[:, hidden] for n in range(2)]),
        "s_sc": rows_t(a["state_sconv"][0]), "w_sc": feature(a["c_conv"][0]),
    }
    made = {
        "o_y": (P, KD, TT), "o_hgrn_p": (HA, P, P), "o_hgrn_s": (NB, HA, P, P), "o_cmp_p": (T, 2, P), "o_slc_p": (T, 2, P),
        "o_win_p": (WIN, 2, P), "o_cmp_s": (NB, 2, P), "o_slc_s": (NB, 2, P), "o_win_s": (NB, WIN, 2, P),
        "o_sc": (P, KD, 2 * (NB + 1)), "o_ff": (2, P, 2 * KF, 2 * (NB + 1)),
    }
    nc = bacc.Bacc("TRN2", target_bir_lowering=False, num_devices=1)
    arrays = {n: np.ascontiguousarray(v) for n, v in given.items()}
    args = [nc.dram_tensor(n, v.shape, mybir.dt.from_np(v.dtype), kind="ExternalInput").ap() for n, v in arrays.items()]
    args += [nc.dram_tensor(n, v, F32, kind="ExternalOutput").ap() for n, v in made.items()]
    program(nc, *args)
    o = run(nc, [arrays], core_ids=[0]).results[0]

    y = o["o_y"].transpose(2, 1, 0).reshape(TT, D)

    def last_rows(v, order=None):
        if order is not None:
            back = np.empty_like(v)
            back[:, order] = v
            v = back
        v = v.transpose(2, 1, 0).reshape(2 * (NB + 1), -1)
        return v[:2][None], v[2:].reshape(NB, 2, -1)

    sc_p, sc_s = last_rows(o["o_sc"])
    ff = [last_rows(o["o_ff"][n], hidden) for n in range(2)]
    kv = (2, 2, HD)
    return (
        y[:T][None], y[T:][:, None],
        o["o_cmp_p"].reshape(1, T, 1, *kv), o["o_slc_p"].reshape(1, T, 1, *kv), o["o_win_p"].reshape(1, 1, WIN, *kv),
        o["o_hgrn_p"][None, None], sc_p[None], np.stack([f[0] for f in ff]),
        o["o_cmp_s"].reshape(NB, 1, 1, *kv), o["o_slc_s"].reshape(NB, 1, 1, *kv), o["o_win_s"].reshape(1, NB, WIN, *kv),
        o["o_hgrn_s"][None], sc_s[None], np.stack([f[1] for f in ff]),
    )
```

```python
from contextlib import ExitStack, contextmanager

import numpy as np

import concourse.bass as bass
from concourse import mybir

F32 = mybir.dt.float32
F16 = mybir.dt.float16
I32 = mybir.dt.int32
ALU = mybir.AluOpType
ACT = mybir.ActivationFunctionType
AX_X = mybir.AxisListType.X
ds = bass.ds

P = 128
D = 1024
KD = D // P
T = 1024
NB = 8
TT = T + NB
NC = T // P
TN = 3
TW = TT // TN
FF = 2816
KF = FF // P
KH = KF // 2
HA = 4
LEV = 7
HB, HD = 8, 64
KVW = 256
PAST, PAGE = 2048, 128
NPG = PAST // PAGE
NPOOL = 160
WIN = 512
CMP, STRIDE = 32, 16
NCP = T // STRIDE - 1
NCS = PAST // STRIDE - 1
NBLK = PAST // 64 + 1
NSEL = 16
EPS = 1e-6
FAR = 1e30
WCH = KH * P
NORMS = 5
UNIT = 64.0


class Chain:

    def __init__(self, engine, sem):
        self.engine, self.sem, self.base, self.k = engine, sem, 0, 0

    def up(self, instruction):
        instruction.then_inc(self.sem, 1)
        self.k += 1

    def settle(self):
        self.engine.wait_ge(self.sem, self.base + self.k)

    def link(self, instruction):
        self.up(instruction)
        self.settle()

    @contextmanager
    def turns(self, count, per):
        start = self.base + self.k
        with self.engine.Fori(0, count) as i:
            self.base, self.k = i * per + start, 0
            yield i
            assert self.k == per, f"the body raises {self.k} times, not {per}"
        self.base, self.k = start + count * per, 0


def at(i, per, first):
    return first if i is None else i * per + first


HEAD_TILES = 5
HEAD_PS = HEAD_TILES + 1 + 1 + NC + 1
PLAN = {}
PLAN_N = {}


def plan():
    u, w = 2, 0
    for name, tiles, chunks in (
        ("norm0", 1, 0), ("heads", HA * HEAD_PS, HA * HEAD_TILES), ("kv", 12, 6), ("gates", 1, 0),
        ("squeeze", 2 * (NB + 1), 0), ("sample", 8, 0),
        ("mix_out", KD, KD), ("norm1", 1, 0), ("up0", 2 * KF, 2 * KF), ("down0", KD, 2 * KD), ("norm2", 1, 0),
        ("conv_in", 3 * KD, 3 * KD), ("conv_out", KD, KD), ("norm3", 1, 0), ("up1", 2 * KF, 2 * KF), ("down1", KD, 2 * KD),
        ("norm4", 1, 0),
    ):
        PLAN[name] = (u, w)
        PLAN_N[name] = tiles
        u += tiles
        w += chunks
    PLAN["end"] = (u, w)


plan()


WK = KF * TT
WKW = 1056


def program(nc, x, wk8, wdn, small, cst, hmask, s_hgrn, wgate, pages, cmp_t, slc_kt, slc_v, win_kt, win_v, state_win,
            w1, w2, pe_t, csn, bias_w, bias_s, tri, table, table_c, s_ff, w_ff, s_sc, w_sc,
            o_y, o_hgrn_p, o_hgrn_s, o_cmp_p, o_slc_p, o_win_p, o_cmp_s, o_slc_s, o_win_s, o_sc, o_ff):
    with ExitStack() as ctx:
        def sb(name, shape, dt=F32):
            return ctx.enter_context(nc.sbuf_tensor(name, shape, dt))

        def sem(name):
            return ctx.enter_context(nc.semaphore(name))

        xT = sb("xT", [P, KD, TT])
        hT = sb("hT", [P, KD, TT])
        W = sb("W", [P, 2, WCH])
        R = sb("R", [P, 31900])
        sm = sb("sm", [P, NORMS * KD + 12])
        lb = sb("lb", [P, 5, HA])
        cs = sb("cs", [P, 4, P])
        eps = sb("eps", [P, 8])
        pg = sb("pg", [1, NB * NPG], I32)
        PS = ctx.enter_context(nc.psum_tensor("PS", [P, 8, 512], F32))
        ident, mean_d, mean_v, ones = (cs[:, n, :] for n in range(4))

        def reg(at0, *shape):
            n = 1
            for s in shape:
                n *= s
            v = R[:, at0:at0 + n]
            if len(shape) == 2:
                v = v.rearrange("p (a b) -> p a b", b=shape[1])
            if len(shape) == 3:
                v = v.rearrange("p (a b c) -> p a b c", b=shape[1], c=shape[2])
            return v

        mix = reg(0, KD, TT)
        QT, FT, KT, VT = (reg(8256 + n * TT, TT) for n in range(4))
        SL, SN = reg(12384, NB, P), reg(13408, NB, P)
        o = 15416
        AL = reg(o, TT)
        G = reg(o + 1032, LEV, T)
        QE = reg(o + 8200, T)
        KE = reg(o + 9224, T)
        VH = reg(o + 10248, NC + 2, P)
        AM = reg(o + 11528, 2, (LEV + 1) * P)
        AT = reg(o + 13576, 2, P)
        KN = reg(o + 13832, 2, P)
        OT = reg(o + 14088, TT)
        S = reg(o + 15120, P)
        EE = reg(o + 15248, NC)
        VMs = reg(o + 11528, NB, P)[0:NB]
        WG = sb("WG", [P, KD, 3 * HB])
        HM = sb("HM", [P, LEV + 1, P])
        KVT = reg(8256, 4, TT)
        VSL, VWN = reg(12384, NC, P), reg(13408, NC, P)
        SNT = reg(14432, 6, P)
        GT = reg(15200, NC + 1, 3 * HB)
        NAT = reg(15416, 4, T)
        VX = reg(27712, TT)
        W1 = hT[:, :, :].rearrange("p a b -> p (a b)")[:, 0:2 * CMP * P].rearrange("p (k i m) -> p k i m", k=2, i=CMP)
        XC = [reg(19520 + n * 2 * PAST, 2, PAST) for n in range(2)]
        KC, VC = reg(27712, NB + 1, P), reg(28864, NB + 1, P)
        W2, PE_T, HID = reg(30016, 2, P), reg(30528, 2, CMP), reg(30272, 2, P)
        PB = reg(30592, 2)
        QB = reg(30016, NB, NB * HB)
        KW = hT[:, :, :].rearrange("p a b -> p (a b)")[:, 0:NB * WIN].rearrange("p (b n) -> p b n", b=NB)
        VW = hT[:, :, :].rearrange("p a b -> p (a b)")[:, NB * WIN:2 * NB * WIN].rearrange(
            "p (b t n) -> p b t n", b=NB, t=WIN // P)
        KB = [reg(19520 + n * PAST, PAST) for n in range(2)]
        VB = [reg(23616 + n * PAST, NPG, P) for n in range(2)]
        TRI, TA, TB = (reg(23616 + n * 1089, NBLK, NBLK)[0:64] for n in range(3))
        SX, SB = reg(15416, PAST + 1)[0:64], reg(17465, PAST + 1)[0:64]
        PTS, PTW = reg(17465, NPG, 64), reg(18489, WIN // P, 64)
        SW = reg(31214, WIN + 1)[0:64]
        PC, PCG = reg(30600, P)[0:64], reg(31086, P)[0:64]
        IT, PCT = reg(30728, 64), reg(30792, 64)
        SCO, RANK, SELB = (reg(30856 + n * NBLK, NBLK)[0:64] for n in range(3))
        GS, NM, DS, RI = (reg(30956 + 3 * n, 3)[0:64] for n in range(4))
        T8 = reg(30968, 2, NB)[0:64]
        G24 = reg(30984, 3 * HB)[0:64]
        OB = reg(31008, 64)
        PN = reg(31728, 2, 64)[0:NB]
        HF = HM[:, :, :].rearrange("p a b -> p (a b)")
        BW, CSN = HF[0:64, 0:WIN + 1], HF[:, WIN + 1:WIN + 1 + 330]
        SAME, COVER, BC = CSN[0:64, 0:64], CSN[0:NCS, 64:97], CSN[0:64, 97:97 + NCS]
        B8, B8T, H24 = CSN[0:64, 224:232], CSN[0:NB, 232:296], CSN[0:64, 296:320]
        NSL, VALID = CSN[:, 320:328], CSN[:, 328:329]
        TAB, TABC = reg(15416, T + 640), reg(17080, NC, 64)
        SS = reg(17592, 3, 1792)
        PT = reg(22968, 2, 14 * P)
        NG, DG, RG = (reg(26552 + 9 * n, 3, 3) for n in range(3))
        Z = reg(0, KF, TT)
        U = [reg(WK + n * WKW, WKW) for n in range(2)]
        Y = [reg(WK + (2 + n) * WKW, TT) for n in range(2)]
        o = WK + 4 * WKW
        FS = reg(o, 2 * KF, 2, NB)
        FW = reg(o + 704, 2 * KF, 3)
        FO = reg(o + 836, 2 * KF, 2 * (NB + 1))
        CSS = reg(o + 1628, KD, 2, NB)
        CSW = reg(o + 1756, KD, 3)
        CO = reg(o + 1780, KD, 2 * (NB + 1))
        SQ = [reg(WK + n * WKW + 2, TT) for n in range(2)]
        FWD = reg(31668, 2 * KF)

        def halves(v):
            return v.bitcast(F16)

        H2 = halves(hT[:, :, :].rearrange("p a b -> p (a b)")).rearrange("p (k s n) -> p k s n", s=2, n=TT)
        Z2 = halves(reg(0, KF * TT)).rearrange("p (k s n) -> p k s n", s=2, n=TT)
        W2H = halves(reg(28852, 2 * WCH)).rearrange("p (w s n) -> p w s n", w=2, s=2)
        HN = reg(0, KD, TT)
        ACC, RS = reg(WK + 2 * WKW, TT), reg(WK + 3 * WKW, TT)

        x_in = [sem(f"x_in{k}") for k in range(KD)]
        c_in = sem("c_in")
        w_in = [sem(f"w_in{n}") for n in range(2)]
        ps_full = sem("ps_full")
        ps_free = [sem(f"ps_free{n}") for n in range(2)]
        sq_here = sem("sq_here")
        acc_here = sem("acc_here")
        h_here = sem("h_here")
        lb_exp = sem("lb_exp")
        lb_sum = sem("lb_sum")
        f_here = sem("f_here")
        k_here = sem("k_here")
        la_here = sem("la_here")
        a_here = sem("a_here")
        diff_here = sem("diff_here")
        exp_here = sem("exp_here")
        g_here = sem("g_here")
        sl_in = sem("sl_in")
        vm_here = sem("vm_here")
        sn_here = sem("sn_here")
        so_here = sem("so_here")
        at_here = sem("at_here")
        oc_here = sem("oc_here")
        s_here = sem("s_here")
        ot_sq = sem("ot_sq")
        mix_here = sem("mix_here")
        sn_out = sem("sn_out")
        s_out = sem("s_out")
        half_used = sem("half_used")
        nat_out = sem("nat_out")
        snat_out = sem("snat_out")
        w1_zero = sem("w1_zero")
        w1_in = sem("w1_in")
        xc_in0 = sem("xc_in0")
        xc_in1 = sem("xc_in1")
        vec_in = sem("vec_in")
        win_in = sem("win_in")
        bias_in = sem("bias_in")
        tri_in = sem("tri_in")
        qb_zero = sem("qb_zero")
        qb_here = sem("qb_here")
        sx_max = sem("sx_max")
        sx_exp = sem("sx_exp")
        pc_here = sem("pc_here")
        kb_in0 = sem("kb_in0")
        kb_in1 = sem("kb_in1")
        kb_used = sem("kb_used")
        vb_in0 = sem("vb_in0")
        vb_in1 = sem("vb_in1")
        vb_used = sem("vb_used")
        rank_done = sem("rank_done")
        sp_here = sem("sp_here")
        win_copied = sem("win_copied")
        tab_in = sem("tab_in")
        sc_full = sem("sc_full")
        sc_free = sem("sc_free")
        mx_here = sem("mx_here")
        ex_here = sem("ex_here")
        rg_here = sem("rg_here")
        p_here = sem("p_here")
        t_full = sem("t_full")
        t_free = sem("t_free")
        pv_full = sem("pv_full")
        pv_free = sem("pv_free")
        ob_here = sem("ob_here")
        rd_here = sem("rd_here")
        pw_here = sem("pw_here")
        pad_here = sem("pad_here")
        up_in = sem("up_in")
        y_here = sem("y_here")
        silu_here = sem("silu_here")
        z_here = sem("z_here")
        u_here = sem("u_here")
        st_here = sem("st_here")
        out_y = sem("out_y")
        out_st = sem("out_st")
        pb_here = sem("pb_here")
        sw_here = sem("sw_here")
        wh_here = sem("wh_here")
        w_split = sem("w_split")
        t_here = sem("t_here")
        hi_here = sem("hi_here")
        lo_even = sem("lo_even")
        lo_odd = sem("lo_odd")
        mix_hi = sem("mix_hi")
        mix_a = sem("mix_a")
        mix_b = sem("mix_b")
        zm_here = sem("zm_here")
        zhi_here = sem("zhi_here")
        cy_here = sem("cy_here")
        cy_hi = sem("cy_hi")
        fwd_here = sem("fwd_here")
        dve_done, act_done, pool_done = sem("dve_done"), sem("act_done"), sem("pool_done")

        def bank(u):
            return PS[:, 3 * (u % 2):3 * (u % 2) + 3, :]

        def wide(u):
            return bank(u)[:, :, 0:TW]

        def three(v):
            return v.rearrange("p (n m) -> p n m", n=TN)

        def wait_full(e, u, i=None, per=0):
            e.wait_ge(ps_full, at(i, per, u - 1))

        def wait_free(e, u, i=None, per=0):
            e.wait_ge(ps_free[u % 2], at(i, per // 2, u // 2))

        def wait_emptied(e, u, i=None, per=0):
            wait_free(e, u + 2, i, per)

        block = ctx.enter_context(nc.Block())
        U_N0, _ = PLAN["norm0"]
        U_H, W_H = PLAN["heads"]
        HP2, HT2 = 2 * HEAD_PS, 2 * HEAD_TILES
        U_KV, W_KV = PLAN["kv"]
        U_G, _ = PLAN["gates"]
        U_C, _ = PLAN["squeeze"]
        U_S, _ = PLAN["sample"]
        _, W_M = PLAN["mix_out"]
        kv_tile = [U_KV] + [U_KV + 2 * n - 1 for n in range(1, 6)]
        kv_turn = [U_KV + 2 * n + 2 for n in range(5)] + [U_KV + 11]
        xc_in, kb_in, vb_in = (xc_in0, xc_in1), (kb_in0, kb_in1), (vb_in0, vb_in1)
        groups = [-(-(i + 1 + min(i + 1, 5) + 1) // 4) for i in range(NC)]

        def blocks(i):
            wide_ones = ([("slc", t, (NC - 1 - i + t) * P) for t in range(i + 1)]
                         + [("win", t, T + (4 - i + t) * P) for t in range(max(0, i - 4), i + 1)])
            return wide_ones[:1] + [("cmp", 0, T + 640)] + wide_ones[1:]

        units = [(i, j, half) for i in range(NC) for j in range(HA) for half in range(2)]
        group_at = [0]
        for i, _, _ in units:
            group_at.append(group_at[-1] + groups[i])

        def attention(ahead, first, second):
            for n in range(ahead):
                first(n, *units[n])
            for n in range(len(units)):
                if n + ahead < len(units):
                    first(n + ahead, *units[n + ahead])
                second(n, *units[n])

        def spans(i):
            return ((1, slice((NC - 1 - i) * P, T)), (2, slice(T + (4 - min(i, 4)) * P, T + 640)),
                    (0, slice(T + 640, T + 640 + NCP)))

        def pages_of(engine, first, what, dst, signal, free=lambda: None):
            with engine.Fori(0, NPG // 4) as j:
                pages = [engine.value_load(pg[0:1, ds(first + j * 4 + n, 1)], min_val=0, max_val=NPOOL - 1)
                         for n in range(4)]
                for n, page in enumerate(pages):
                    if n == 0:
                        free()
                    src = what[ds(page, 1)]
                    src = src.rearrange("a p b -> p a b" if len(what.shape) == 3 else "a p k b -> p (a k) b")
                    engine.dma_start(dst(j * 4 + n), src).then_inc(signal, 16)

        def cmp_pages(engine, b):
            def dst(j):
                return XC[b][:, :, ds(j * P, P)]

            pages_of(engine, b * NPG, cmp_t, dst, xc_in[b])
            with engine.Fori(0, NB // 2 - 1) as i:
                pages_of(engine, i * (2 * NPG) + (b + 2) * NPG, cmp_t, dst, xc_in[b],
                         lambda: wait_full(engine, U_C + 2 + 2 * b, i, 4))

        def slc_pages(engine, b):
            def key(j):
                return KB[b].unsqueeze(1)[:, :, ds(j * P, P)]

            def value(j):
                return VB[b][:, ds(j, 1), :]

            pages_of(engine, b * NPG, slc_kt, key, kb_in[b])
            with engine.Fori(0, NB // 2 - 1) as i:
                pages_of(engine, i * (2 * NPG) + (b + 2) * NPG, slc_kt, key, kb_in[b],
                         lambda: engine.wait_ge(kb_used, at(i, 2, b + 1)))
            engine.wait_ge(rank_done, 1)
            pages_of(engine, b * NPG, slc_v, value, vb_in[b])
            with engine.Fori(0, NB // 2 - 1) as i:
                pages_of(engine, i * (2 * NPG) + (b + 2) * NPG, slc_v, value, vb_in[b],
                         lambda: engine.wait_ge(vb_used, at(i, 2, b + 1)))

        STEP, at_step = {}, 0
        for name, steps in (("mix_out", KD), ("up0", 2 * KF), ("down0", 2 * KD), ("conv_in", 3 * KD), ("conv_out", KD),
                            ("up1", 2 * KF), ("down1", 2 * KD)):
            STEP[name] = at_step
            at_step += steps

        def split_high(act, c, i=None, per=0, width=D):
            n = c % 2
            act.wait_ge(w_in[n], at(i, 8 * per, 16 * ((W_M + c) // 2 + 1)))
            act.activation(W2H[:, n, 0, 0:width], W[:, n, 0:width], ACT.Copy, scale=UNIT).then_inc(wh_here, 1)

        def split_low(dve, c, i=None, per=0, width=D):
            n = c % 2
            dve.wait_ge(wh_here, at(i, per, c + 1))
            dve.scalar_tensor_tensor(W2H[:, n, 1, 0:width], W[:, n, 0:width], UNIT, W2H[:, n, 0, 0:width],
                                     ALU.mult, ALU.subtract).then_inc(w_split, 1)

        @block.sync
        def _(sp):
            for k in range(KD):
                sp.dma_start(xT[:, k, :], x[:, k, :]).then_inc(x_in[k], 16)
            sp.dma_start(cs[:, :, :], cst).then_inc(c_in, 16)
            sp.dma_start(sm[:, :], small).then_inc(c_in, 16)
            sp.dma_start(HM[:, :, :], hmask).then_inc(c_in, 16)
            sp.dma_start(WG[:, :, :], wgate).then_inc(c_in, 16)
            sp.dma_start(pg[:, :], pages).then_inc(c_in, 16)
            for w in range(2):
                sp.dma_start(W[:, w, 0:D], wk8[w]).then_inc(w_in[w], 16)
            with sp.Fori(0, HA // 2) as i:
                for hh in range(2):
                    for k in range(HEAD_TILES):
                        w = W_H + hh * HEAD_TILES + k
                        wait_full(sp, U_H + hh * HEAD_PS + k, i, HP2)
                        sp.dma_start(W[:, w % 2, 0:D].unsqueeze(1),
                                     wk8[ds(i * HT2 + (w + 2), 1)].rearrange("a p n -> p a n")
                                     ).then_inc(w_in[w % 2], 16)
            for n in range(6):
                wait_full(sp, kv_tile[n])
                sp.dma_start(W[:, n % 2, 0:D], wk8[W_KV + n + 2]).then_inc(w_in[n % 2], 16)
            sp.wait_ge(w1_zero, 1)
            sp.wait_ge(s_out, 16 * (HA + 1))
            w1f = W1.rearrange("p k i m -> p (k i) m")
            for n in range(2):
                sp.dma_start(w1f[64 * n:64 * n + 64, :, 64 * n:64 * n + 64], w1).then_inc(w1_in, 16)
                sp.dma_start(W2[64 * n:64 * n + 64, :, 64 * n:64 * n + 64], w2).then_inc(w1_in, 16)
                sp.dma_start(PE_T[64 * n:64 * n + 64], pe_t).then_inc(w1_in, 16)

            sp.wait_ge(c_in, 16 * 5)
            wait_full(sp, U_G)
            sp.wait_ge(mix_here, HA)
            sp.dma_start(CSN, csn).then_inc(vec_in, 16)
            sp.dma_start(BW, bias_w).then_inc(vec_in, 16)
            cmp_pages(sp, 0)
            wait_full(sp, U_S - 1)
            sp.dma_start(KW, win_kt).then_inc(win_in, 16)
            sp.dma_start(VW, win_v).then_inc(win_in, 16)
            sp.wait_ge(nat_out, 16 * 6)
            sp.dma_start(SB, bias_s).then_inc(bias_in, 16)
            sp.dma_start(TRI, tri).then_inc(tri_in, 16)
            slc_pages(sp, 0)
            wait_full(sp, U_S + 7)
            sp.dma_start(TAB, table).then_inc(tab_in, 16)
            sp.dma_start(TABC, table_c).then_inc(tab_in, 16)
            sp.wait_ge(pv_full, len(units))

            def after_tiles(name, index, following):
                c, n = STEP[name], PLAN_N[name]
                with sp.Fori(0, n // 2 - 1) as i:
                    for k in range(2):
                        sp.wait_ge(w_split, at(i, 2, c + k + 1))
                        sp.dma_start(W[:, k, 0:D].unsqueeze(1),
                                     wk8[ds(i * 2 + (index + 2 + k), 1)].rearrange("a p n -> p a n")
                                     ).then_inc(w_in[k], 16)
                for k in range(2):
                    sp.wait_ge(w_split, c + n - 2 + k + 1)
                    sp.dma_start(W[:, k, 0:following.shape[2]], following[k]).then_inc(w_in[k], 16)

            def after_down(name, chunks, following):
                c = STEP[name]
                with sp.Fori(0, KD - 1) as i:
                    for k in range(2):
                        sp.wait_ge(w_split, at(i, 2, c + k + 1))
                        sp.dma_start(W[:, k, :].unsqueeze(1), chunks[ds(i * 2 + 2 + k, 1)].rearrange("a p n -> p a n")
                                     ).then_inc(w_in[k], 16)
                if following is not None:
                    for k in range(2):
                        sp.wait_ge(w_split, c + 2 * KD - 1 + k)
                        sp.dma_start(W[:, k, 0:D], following[k]).then_inc(w_in[k], 16)

            def states(layer):
                sp.dma_start(FS, s_ff[layer]).then_inc(up_in, 16)
                sp.dma_start(FW, w_ff[layer]).then_inc(up_in, 16)

            states(0)
            sp.dma_start(CSS, s_sc).then_inc(up_in, 16)
            sp.dma_start(CSW, w_sc).then_inc(up_in, 16)
            i8 = PLAN["mix_out"][1]
            after_tiles("mix_out", i8, wk8[i8 + KD:i8 + KD + 2])
            i8 += KD
            after_tiles("up0", i8, wdn[0, 0:2])
            sp.wait_ge(st_here, 2 + 2 * KF)
            sp.dma_start(o_ff[0], FO).then_inc(out_st, 16)
            i8 += 2 * KF
            after_down("down0", wdn[0], wk8[i8:i8 + 2])
            sp.wait_ge(out_st, 16)
            states(1)
            after_tiles("conv_in", i8, wk8[i8 + 3 * KD:i8 + 3 * KD + 2])
            i8 += 3 * KD
            sp.wait_ge(st_here, 2 + 2 * KF + KD)
            sp.dma_start(o_sc, CO).then_inc(out_st, 16)
            after_tiles("conv_out", i8, wk8[i8 + KD:i8 + KD + 2])
            i8 += KD
            after_tiles("up1", i8, wdn[1, 0:2])
            sp.wait_ge(st_here, 2 + 4 * KF + KD)
            sp.dma_start(o_ff[1], FO).then_inc(out_st, 16)
            after_down("down1", wdn[1], None)
            for k in range(KD):
                sp.wait_ge(h_here, KD + k + 1)
                sp.dma_start(o_y[:, k, :], hT[:, k, :]).then_inc(out_y, 16)
            sp.wait_ge(out_y, 16 * KD)
            sp.wait_ge(out_st, 16 * 3)
            sp.wait_ge(nat_out, 16 * 6)
            sp.wait_ge(snat_out, 16 * 6)
            sp.wait_ge(win_copied, 16)
            sp.wait_ge(sn_out, 16 * 5)
            sp.wait_ge(s_out, 16 * 5)

        @block.gpsimd
        def _(pool):
            pool.memset(eps[:, 0:1], EPS).then_inc(ps_free[0], 1)
            pool.memset(eps[:, 1:2], 0.0).then_inc(ps_free[1], 1)
            pool.memset(eps[:, 2:3], 0.0).then_inc(acc_here, 2)
            pool.memset(eps[:, 3:4], 0.0).then_inc(sn_out, 16)
            pool.memset(eps[:, 4:5], 0.0).then_inc(s_out, 16)
            pool.memset(eps[:, 5:6], 0.0).then_inc(st_here, 2)
            pool.memset(eps[:, 6:7], 0.0).then_inc(z_here, 1)
            pool.memset(eps[:, 7:8], 0.0).then_inc(cy_here, 1)
            with pool.Fori(0, HA // 2) as i:
                for hh in range(2):
                    u = U_H + hh * HEAD_PS
                    h = i * 2 + hh
                    pool.dma_start(SL, s_hgrn[:, ds(h, 1)].rearrange("b a k v -> k (b a) v")).then_inc(sl_in, 16)
                    pool.wait_ge(f_here, at(i, 2, hh + 1))
                    pool.tensor_tensor(KT, ones[:, 0:1].to_broadcast([P, TT]), FT, ALU.subtract).then_inc(k_here, 1)
                    pool.wait_ge(k_here, at(i, 2, hh + 1))
                    wait_emptied(pool, u + 1, i, HP2)
                    for lev in range(LEV):
                        g = G[:, lev, :].rearrange("p (n t m) -> p n t m", t=2, m=1 << lev)
                        q = QT[:, 0:T].rearrange("p (n t m) -> p n t m", t=2, m=1 << lev)
                        k = KT[:, 0:T].rearrange("p (n t m) -> p n t m", t=2, m=1 << lev)
                        pool.wait_ge(exp_here, at(i, 2 * (LEV + 2), hh * (LEV + 2) + lev + 2))
                        pool.tensor_tensor(g[:, :, 0, :], g[:, :, 0, :], k[:, :, 0, :], ALU.mult)
                        pool.tensor_tensor(g[:, :, 1, :], g[:, :, 1, :], q[:, :, 1, :], ALU.mult).then_inc(g_here, 1)
                    pool.wait_ge(s_here, at(i, 2 * (NC + 1), hh * (NC + 1) + 1))
                    pool.tensor_tensor(QE, QE, QT[:, 0:T], ALU.mult)
                    pool.wait_ge(exp_here, at(i, 2 * (LEV + 2), (hh + 1) * (LEV + 2)))
                    pool.tensor_tensor(KE, KE, KT[:, 0:T], ALU.mult).then_inc(g_here, 1)
                    pool.wait_ge(sn_here, at(i, 2, hh + 1))

            pool.dma_start(o_win_s[:, 0:WIN - 1], state_win[:, 1:WIN]).then_inc(win_copied, 16)
            pool.wait_ge(mix_here, HA)
            wait_full(pool, U_G)
            pool.memset(W2, 0.0)
            pool.memset(W1, 0.0).then_inc(w1_zero, 1)
            pool.wait_ge(c_in, 16 * 5)
            cmp_pages(pool, 1)
            wait_full(pool, U_S - 1)
            pool.memset(QB, 0.0).then_inc(qb_zero, 1)
            slc_pages(pool, 1)

            for n, (i, _, _) in enumerate(units):
                part = SS[:, n % 3, spans(i)[0][1]]
                pool.wait_ge(rg_here, n + 1)
                pool.tensor_scalar(part, part, RG[:, n % 3, 1:2], None, ALU.mult).then_inc(p_here, 1)
                if n % 8 == 4 and n // 8 < HA:
                    k = n // 8
                    pool.tensor_copy(H2[:, k, 0, :], mix[:, k, :]).then_inc(mix_hi, 1)
                    pool.wait_ge(mix_hi, k + 1)
                    pool.tensor_tensor(H2[:, k, 1, :], mix[:, k, :], H2[:, k, 0, :], ALU.subtract).then_inc(mix_a, 1)

            def ffn_rows(tiles, pairs):
                with pool.Fori(0, KF // 2) as i:
                    for p in range(2):
                        for n in range(2):
                            k = 2 * p + n
                            t = i * 4 + k
                            pool.wait_ge(u_here, at(i, 4, tiles + k + 1))
                            o18 = FO[:, ds(t, 1), :]
                            smp = o18[:, :, 2:2 + 2 * NB].rearrange("p a (b r) -> p a b r", r=2)
                            pool.tensor_copy(o18[:, :, 0:2], U[n][:, T:T + 2].unsqueeze(1))
                            pool.tensor_copy(smp[:, :, :, 1], U[n][:, T + 2:T + 2 + NB].unsqueeze(1))
                            pool.tensor_copy(smp[:, :, :, 0], FS[:, ds(t, 1), 1, :]).then_inc(st_here, 1)
                        row = Z2[:, ds(i * 2 + p, 1), :, :]
                        pool.wait_ge(zhi_here, at(i, 2, pairs + p + 1))
                        pool.tensor_tensor(row[:, :, 1, :], Y[0].unsqueeze(1), row[:, :, 0, :], ALU.subtract
                                           ).then_inc(z_here, 1)

            def low_halves(norm):
                for k in range(1, KD, 2):
                    pool.wait_ge(hi_here, KD * (norm - 1) + k + 1)
                    pool.tensor_tensor(H2[:, k, 1, :], HN[:, k, :], H2[:, k, 0, :], ALU.subtract).then_inc(lo_odd, 1)

            pool.wait_ge(up_in, 16 * 4)
            low_halves(1)
            ffn_rows(0, 0)
            low_halves(2)
            with pool.Fori(0, KD // 2) as i:
                for n in range(2):
                    t = i * 2 + n
                    pool.wait_ge(u_here, at(i, 2, 2 * KF + n + 1))
                    o18 = CO[:, ds(t, 1), :]
                    smp = o18[:, :, 2:2 + 2 * NB].rearrange("p a (b r) -> p a b r", r=2)
                    pool.tensor_copy(o18[:, :, 0:2], U[n][:, T:T + 2].unsqueeze(1))
                    pool.tensor_copy(smp[:, :, :, 1], U[n][:, T + 2:T + 2 + NB].unsqueeze(1))
                    pool.tensor_copy(smp[:, :, :, 0], CSS[:, ds(t, 1), 1, :]).then_inc(st_here, 1)
                    row = Z2[:, ds(t, 1), :, :]
                    pool.wait_ge(cy_hi, at(i, 2, n + 1))
                    pool.tensor_tensor(row[:, :, 1, :], Y[1].unsqueeze(1), row[:, :, 0, :], ALU.subtract
                                       ).then_inc(cy_here, 1)
            pool.wait_ge(up_in, 16 * 6)
            low_halves(3)
            ffn_rows(2 * KF + KD, KF)

        @block.scalar
        def _(act):
            act.wait_ge(lb_sum, 1)
            act.activation(lb[:, 1:3, :], lb[:, 1:3, :], ACT.Exp).then_inc(lb_exp, 1)
            for k in range(KD):
                act.wait_ge(x_in[k], 16)
                act.wait_ge(acc_here, k + 1)
                act.activation(SQ[k % 2], xT[:, k, :], ACT.Square).then_inc(sq_here, 1)
            wait_full(act, U_N0)
            act.activation(three(RS), wide(U_N0), ACT.Sqrt, bias=eps[:, 0:1]).then_inc(ps_free[U_N0 % 2], 1)
            with act.Fori(0, HA // 2) as i:
                for hh in range(2):
                    u = U_H + hh * HEAD_PS
                    h = i * 2 + hh
                    wait_full(act, u, i, HP2)
                    act.activation(three(FT), wide(u), ACT.Sigmoid).then_inc(ps_free[u % 2], 1)
                    act.wait_ge(f_here, at(i, 2, hh + 1))
                    act.activation(AL, FT, ACT.Ln).then_inc(la_here, 1)
                    wait_full(act, u + 1, i, HP2)
                    act.activation(three(QT), wide(u + 1), ACT.Copy).then_inc(ps_free[(u + 1) % 2], 1)
                    act.wait_ge(a_here, at(i, 2 * NC, (hh + 1) * NC))
                    act.activation(QE, AL[:, 0:T], ACT.Exp).then_inc(exp_here, 1)
                    for lev in range(LEV):
                        act.wait_ge(diff_here, at(i, 2 * (LEV + 1), hh * (LEV + 1) + lev + 1))
                        act.activation(G[:, lev, :], G[:, lev, :], ACT.Exp).then_inc(exp_here, 1)
                    act.wait_ge(diff_here, at(i, 2 * (LEV + 1), (hh + 1) * (LEV + 1)))
                    act.activation(KE, KE, ACT.Exp).then_inc(exp_here, 1)
                    wait_full(act, u + 2, i, HP2)
                    act.activation(three(VT), wide(u + 2), ACT.Copy).then_inc(ps_free[u % 2], 1)
                    wait_full(act, u + 3, i, HP2)
                    act.activation(three(mix[:, ds(h, 1), :].rearrange("p a n -> p (a n)")), wide(u + 3), ACT.Sigmoid
                                   ).then_inc(ps_free[(u + 1) % 2], 1)
                    wait_full(act, u + 4, i, HP2)
                    act.activation(three(mix[:, ds(h + HA, 1), :].rearrange("p a n -> p (a n)")), wide(u + 4), ACT.Copy,
                                   scale=HD ** -0.5).then_inc(ps_free[u % 2], 1)
                    wait_full(act, u + 5, i, HP2)
                    v = bank(u + 5)
                    for n in range(2):
                        act.activation(VH[:, 4 * n:4 * n + 4, :], v[:, n, :].rearrange("p (a b) -> p a b", b=P), ACT.Copy)
                    act.activation(VH[0:NB, NC:NC + 2, :], v[0:NB, 2, 0:2 * P].rearrange("p (a b) -> p a b", b=P),
                                   ACT.Copy).then_inc(ps_free[(u + 1) % 2], 1)
                    act.wait_ge(sn_here, at(i, 2, hh + 1))
                    act.dma_start(o_hgrn_s[:, ds(h, 1)].rearrange("b a k v -> k (b a) v"), SN).then_inc(sn_out, 16)
                    act.wait_ge(s_here, at(i, 2 * (NC + 1), (hh + 1) * (NC + 1)))
                    act.dma_start(o_hgrn_p[ds(h, 1)].rearrange("a k v -> k a v"), S.unsqueeze(1)).then_inc(s_out, 16)
                    wait_emptied(act, u + 14, i, HP2)
                    act.activation(G[:, 0, 0:T], OT[:, 0:T], ACT.Square)
                    act.activation(G[:, 1, 0:NB], OT[:, T:TT], ACT.Square).then_inc(ot_sq, 1)
                    wait_full(act, u + 15, i, HP2)
                    act.activation(G[:, 2, :], bank(u + 15)[:, 0:2, :].rearrange("p a b -> p (a b)"), ACT.Sqrt, bias=eps[:, 0:1])
                    act.activation(G[:, 3, 0:NB], bank(u + 15)[:, 2, 0:NB], ACT.Sqrt,
                                   bias=eps[:, 0:1]).then_inc(ps_free[(u + 1) % 2], 1)

            act.wait_ge(sn_out, 16 * (HA + 1))
            kv_out = (o_cmp_p[:, 0], o_cmp_p[:, 1], o_slc_p[:, 0], o_slc_p[:, 1], o_win_p[:, 0], o_win_p[:, 1])
            kv_out_s = (o_cmp_s[:, 0], o_cmp_s[:, 1], o_slc_s[:, 0], o_slc_s[:, 1], o_win_s[:, WIN - 1, 0],
                        o_win_s[:, WIN - 1, 1])
            held = (KVT[:, 0, :], KVT[:, 1, :], KVT[:, 2, :], VX, KVT[:, 3, :], VX)
            turned = (NAT[:, 0], NAT[:, 1], NAT[:, 2], VSL.rearrange("p a b -> p (a b)"), NAT[:, 3],
                      VWN.rearrange("p a b -> p (a b)"))

            def hold(n):
                wait_full(act, kv_tile[n])
                act.activation(three(held[n]), wide(kv_tile[n]), ACT.Copy).then_inc(ps_free[kv_tile[n] % 2], 1)

            def turn(n):
                u = kv_turn[n]
                wait_full(act, u)
                act.activation(turned[n], bank(u)[:, 0:2, :].rearrange("p a b -> p (a b)"), ACT.Copy)
                act.activation(SNT[0:NB, n, :], bank(u)[0:NB, 2, 0:P], ACT.Copy).then_inc(ps_free[u % 2], 1)
                wait_emptied(act, u)
                rows = turned[n].rearrange("p (c d) -> p c d", d=P)
                if n >= 4:
                    rows = rows[:, NC - WIN // P:]
                act.dma_start(kv_out[n].rearrange("(c p) d -> p c d", p=P), rows).then_inc(nat_out, 16)
                act.dma_start(kv_out_s[n], SNT[0:NB, n, :]).then_inc(snat_out, 16)

            hold(0)
            act.wait_ge(mix_here, HA)
            for n in range(1, 6):
                hold(n)
                turn(n - 1)
            turn(5)
            wait_full(act, U_G)
            act.activation(GT[:, 0:NC, :].rearrange("p a b -> p (a b)"), bank(U_G)[:, 0, 0:NC * 24], ACT.Sigmoid)
            act.activation(GT[0:NB, NC, :], bank(U_G)[0:NB, 0, NC * 24:(NC + 1) * 24], ACT.Sigmoid
                           ).then_inc(ps_free[U_G % 2], 1)

            def squeeze(n, u, i, per, cols):
                hid = bank(u)
                wait_full(act, u, i, per)
                if i is None:
                    act.activation(PB, hid[:, 2, 0:2], ACT.Copy).then_inc(pb_here, 1)
                    act.wait_ge(pb_here, 1)
                act.activation(HID[:, 0, 0:cols], hid[:, 0, 0:cols], ACT.Silu, bias=PB[:, 0:1])
                act.activation(HID[:, 1, 0:cols], hid[:, 1, 0:cols], ACT.Silu, bias=PB[:, 1:2]).then_inc(ps_free[u % 2], 1)
                wait_full(act, u + 1, i, per)
                kv = bank(u + 1)
                act.activation(KC[:, ds(n, 1), 0:cols], kv[:, 0:1, 0:cols], ACT.Copy)
                act.activation(VC[0:cols, ds(n, 1), :], kv[0:cols, 1:2, 0:P], ACT.Copy).then_inc(ps_free[(u + 1) % 2], 1)

            squeeze(NB, U_C, None, 0, NCP)
            with act.Fori(0, NB // 2) as i:
                for b in range(2):
                    squeeze(i * 2 + b, U_C + 2 + 2 * b, i, 4, NCS)

            for n, (row, c) in enumerate(((PC[:, 0:NCS], 0), (SW, 2), (SX, 1))):
                act.wait_ge(sx_max, n + 1)
                act.activation(row, row, ACT.Exp, bias=NM[:, c:c + 1], accum_out=DS[:, c:c + 1]).then_inc(sx_exp, 1)

            def first(n, i, j, half):
                act.wait_ge(mx_here, n + 1)
                for c, cols in spans(i):
                    part = SS[:, n % 3, cols]
                    ins = act.activation(part, part, ACT.Exp, bias=NG[:, n % 3, c:c + 1], accum_out=DG[:, n % 3, c:c + 1])
                ins.then_inc(ex_here, 1)

            def heads_out(pair):
                i, j = pair // HA, pair % HA
                act.wait_ge(pv_full, 2 * pair + 2)
                act.activation(mix[:, HA + j, i * P:(i + 1) * P], PS[:, 6 + pair % 2, 0:P], ACT.Copy).then_inc(pv_free, 1)

            def second(n, i, j, half):
                for g in range(groups[i]):
                    m = len(blocks(i)[4 * g:4 * g + 4])
                    act.wait_ge(t_full, group_at[n] + g + 1)
                    act.activation(PT[:, half, 4 * g * P:(4 * g + m) * P], PS[:, 4 + (group_at[n] + g) % 2, 0:m * P], ACT.Copy
                                   ).then_inc(t_free, 1)
                if half == 0 and n:
                    heads_out(n // 2 - 1)

            act.wait_ge(ob_here, 1)
            attention(1, first, second)
            heads_out(len(units) // 2 - 1)

            for k in range(2):
                split_high(act, k)
            act.wait_ge(pv_free, HA * NC)
            for k in range(HA, 2 * HA):
                act.activation(H2[:, k, 0, :], mix[:, k, :], ACT.Copy).then_inc(mix_hi, 1)

            def squares(k, n, norm, i):
                act.wait_ge(acc_here, at(i, 2, KD * norm + n + 1))
                act.activation(SQ[n].unsqueeze(1), xT[:, ds(k, 1), :], ACT.Square).then_inc(sq_here, 1)

            def after_norm(norm):
                u = PLAN[f"norm{norm}"][0]
                wait_full(act, u)
                act.activation(three(RS), wide(u), ACT.Sqrt, bias=eps[:, 0:1]).then_inc(ps_free[u % 2], 1)
                if norm < 4:
                    for k in range(KD):
                        act.wait_ge(t_here, KD * (norm - 1) + k + 1)
                        act.activation(H2[:, k, 0, :], HN[:, k, :], ACT.Copy).then_inc(hi_here, 1)

            def stage_squares(name, norm, tiles):
                act.wait_ge(st_here, 2 + tiles)
                u, c = PLAN[name][0], STEP[name]
                with act.Fori(0, KD // 2) as i:
                    for n in range(2):
                        wait_full(act, u + n, i, 2)
                        split_high(act, c + n + 2, i, 2)
                        wait_emptied(act, u + n, i, 2)
                        squares(i * 2 + n, n, norm, i)
                after_norm(norm)

            def down_squares(name, norm, tiles, halves_before, last=False):
                act.wait_ge(st_here, 2 + tiles)
                u, c = PLAN[name][0], STEP[name]

                def turn(i, widths):
                    for n in range(2):
                        if widths[n]:
                            act.wait_ge(half_used, at(i, 2, halves_before + n + 1))
                            split_high(act, c + 2 * n + 2, i, 4, widths[n])
                            wait_full(act, u + n, i, 2)
                            split_high(act, c + 2 * n + 3, i, 4, widths[n])
                        wait_emptied(act, u + n, i, 2)
                        squares(i * 2 + n, n, norm, i)

                with act.Fori(0, KD // 2 - 1) as i:
                    turn(i, (WCH, WCH))
                turn(KD // 2 - 1, (WCH, None if last else D))
                after_norm(norm)

            def ffn_up(name, tiles, pairs):
                u, c = PLAN[name][0], STEP[name]

                def turn(i, widths):
                    for p in range(2):
                        for n in range(2):
                            k = 2 * p + n
                            t = u + k
                            wait_full(act, t, i, 4)
                            split_high(act, c + k + 2, i, 4, widths[p])
                            act.wait_ge(z_here, at(i, 2, pairs + p + 1))
                            act.wait_ge(st_here, at(i, 4, tiles + 2 * p + n + 1))
                            act.activation(three(U[n][:, 2:2 + TT]), wide(t), ACT.Copy, scale=1 / UNIT).then_inc(u_here, 1)
                            act.activation(three(Y[n]), wide(t), ACT.Copy, scale=FWD[:, ds(i * 4 + k, 1)]
                                           ).then_inc(ps_free[t % 2], 1)
                        act.wait_ge(y_here, at(i, 2, pairs + p + 1))
                        act.activation(Y[0], Y[0], ACT.Silu).then_inc(silu_here, 1)
                        act.wait_ge(zm_here, at(i, 2, pairs + p + 1))
                        act.activation(Z2[:, ds(i * 2 + p, 1), 0, :], Y[0].unsqueeze(1), ACT.Copy).then_inc(zhi_here, 1)

                with act.Fori(0, KF // 2 - 1) as i:
                    turn(i, (D, D))
                turn(KF // 2 - 1, (D, WCH))

            def last_tap(n, sent):
                act.wait_ge(up_in, 16 * sent)
                act.activation(FWD, FW[:, :, 2], ACT.Copy, scale=1 / UNIT).then_inc(fwd_here, 1)
                act.wait_ge(fwd_here, n)

            stage_squares("mix_out", 1, 0)
            last_tap(1, 4)
            ffn_up("up0", 0, 0)
            down_squares("down0", 2, 2 * KF, 0)
            u, c = PLAN["conv_in"][0], STEP["conv_in"]
            with act.Fori(0, KD // 2) as i:
                for n in range(2):
                    v = u + 3 * n
                    wait_full(act, v, i, 6)
                    split_high(act, c + 3 * n + 2, i, 6)
                    act.wait_ge(u_here, at(i, 2, 2 * KF + n))
                    act.activation(three(Y[0]), wide(v), ACT.Copy, scale=1 / UNIT).then_inc(ps_free[v % 2], 1)
                    wait_full(act, v + 1, i, 6)
                    split_high(act, c + 3 * n + 3, i, 6)
                    wait_full(act, v + 2, i, 6)
                    split_high(act, c + 3 * n + 4, i, 6)
                    wait_emptied(act, v + 2, i, 6)
                    act.activation(Z2[:, ds(i * 2 + n, 1), 0, :], Y[1].unsqueeze(1), ACT.Copy).then_inc(cy_hi, 1)
            stage_squares("conv_out", 3, 2 * KF + KD)
            last_tap(2, 6)
            ffn_up("up1", 2 * KF + KD, KF)
            down_squares("down1", 4, 4 * KF + KD, KD, last=True)

        @block.vector
        def _(dve):
            own = Chain(dve, dve_done)
            dve.memset(ACC, 0.0).then_inc(dve_done, 1)
            own.k += 1
            dve.wait_ge(c_in, 16 * 5)
            lg = sm[:, NORMS * KD:NORMS * KD + 8].rearrange("p (a h) -> p a h", a=2)
            own.link(dve.tensor_tensor(lb[:, 0, :], lg[:, 0, :], lg[:, 1, :], ALU.max))
            dve.tensor_tensor(lb[:, 1, :], lg[:, 0, :], lb[:, 0, :], ALU.subtract)
            dve.tensor_tensor(lb[:, 2, :], lg[:, 1, :], lb[:, 0, :], ALU.subtract).then_inc(lb_sum, 1)
            dve.wait_ge(lb_exp, 1)
            own.link(dve.tensor_tensor(lb[:, 0, :], lb[:, 1, :], lb[:, 2, :], ALU.add))
            own.link(dve.reciprocal(lb[:, 0, :], lb[:, 0, :]))
            own.link(dve.tensor_tensor(lb[:, 3, :], lb[:, 1, :], lb[:, 0, :], ALU.mult))
            own.link(dve.tensor_scalar(lb[:, 4, :], lb[:, 3, :], -1.0, 1.0, ALU.mult, ALU.add))
            for k in range(KD):
                dve.wait_ge(sq_here, k + 1)
                dve.wait_ge(acc_here, k + 2)
                dve.tensor_tensor(ACC, ACC, SQ[k % 2], ALU.add).then_inc(acc_here, 1)
            wait_emptied(dve, U_N0)
            own.link(dve.reciprocal(RS, RS))
            for k in range(KD):
                dve.scalar_tensor_tensor(hT[:, k, :], xT[:, k, :], sm[:, k:k + 1], RS, ALU.mult, ALU.mult
                                         ).then_inc(h_here, 1)
            with own.turns(HA // 2, 2 * 11) as i:
                for hh in range(2):
                    u = U_H + hh * HEAD_PS
                    h = i * 2 + hh
                    wait_emptied(dve, u, i, HP2)
                    dve.tensor_scalar(FT, FT, lb[:, 4, ds(h, 1)], lb[:, 3, ds(h, 1)], ALU.mult, ALU.add
                                      ).then_inc(f_here, 1)
                    dve.wait_ge(la_here, at(i, 2, hh + 1))
                    for c in range(NC):
                        a = AL[:, c * P:(c + 1) * P]
                        dve.tensor_tensor_scan(a, ones, a, 0.0, ALU.mult, ALU.add).then_inc(a_here, 1)
                    dve.wait_ge(a_here, at(i, 2 * NC, (hh + 1) * NC))
                    for lev in range(LEV):
                        m = 1 << lev
                        a = AL[:, 0:T].rearrange("p (n t m) -> p n t m", t=2, m=m)
                        g = G[:, lev, :].rearrange("p (n t m) -> p n t m", t=2, m=m)
                        mid = a[:, :, 0, m - 1:m].to_broadcast([P, T // (2 * m), m])
                        dve.tensor_tensor(g[:, :, 0, :], mid, a[:, :, 0, :], ALU.subtract)
                        dve.tensor_tensor(g[:, :, 1, :], a[:, :, 1, :], mid, ALU.subtract).then_inc(diff_here, 1)
                    a = AL[:, 0:T].rearrange("p (n m) -> p n m", m=P)
                    dve.tensor_tensor(KE.rearrange("p (n m) -> p n m", m=P), a[:, :, P - 1:P].to_broadcast([P, NC, P]),
                                      a, ALU.subtract).then_inc(diff_here, 1)
                    dve.wait_ge(exp_here, at(i, 2 * (LEV + 2), hh * (LEV + 2) + 1))
                    dve.tensor_copy(EE.unsqueeze(2), QE.rearrange("p (n m) -> p n m", m=P)[:, :, P - 1:P]
                                    ).then_inc(s_here, 1)
                    wait_emptied(dve, u + 5, i, HP2)
                    dve.tensor_tensor(VMs, VH[0:NB, NC:NC + 1, :].to_broadcast([NB, NB, P]),
                                      ident[0:NB, 0:NB].unsqueeze(2).to_broadcast([NB, NB, P]), ALU.mult
                                      ).then_inc(vm_here, 1)
                    wait_full(dve, u + 6, i, HP2)
                    dve.wait_ge(sl_in, at(i, 32, 16 * (hh + 1)))
                    dve.wait_ge(sn_out, at(i, 32, 16 * (hh + 1)))
                    ps = bank(u + 6)
                    for b in range(NB):
                        ins = dve.scalar_tensor_tensor(SN[:, b, :], SL[:, b, :], FT[:, T + b:T + b + 1],
                                                       ps[:, b // 4, (b % 4) * P:(b % 4 + 1) * P], ALU.mult, ALU.add)
                    ins.then_inc(sn_here, 1)
                    dve.wait_ge(so_here, at(i, 2, hh + 1))
                    dve.tensor_copy(OT[:, T:TT], ps[:, 2, 0:NB]).then_inc(ps_free[u % 2], 1)
                    for c in range(NC):
                        uc = u + 7 + c
                        ps = bank(uc)
                        wait_full(dve, uc, i, HP2)
                        am = AM[:, c % 2, :]
                        own.link(dve.tensor_tensor(am, ps[:, 0:2, :].rearrange("p a b -> p (a b)"),
                                                   HM[:, :, :].rearrange("p a b -> p (a b)"), ALU.mult))
                        dve.tensor_reduce(AT[:, c % 2, :], am.rearrange("p (l t) -> p t l", t=P), AX_X, ALU.add)
                        dve.tensor_copy(KN[:, c % 2, :], ps[:, 2, 0:P]).then_inc(at_here, 1)
                        dve.wait_ge(oc_here, at(i, 2 * NC, hh * NC + c + 1))
                        if c == 0:
                            dve.wait_ge(s_out, at(i, 32, 16 * (hh + 1)))
                            dve.tensor_copy(S, ps[:, 2, 2 * P:3 * P]).then_inc(s_here, 1)
                        else:
                            dve.wait_ge(s_here, at(i, 2 * (NC + 1), hh * (NC + 1) + c + 1))
                            dve.scalar_tensor_tensor(S, S, EE[:, c:c + 1], ps[:, 2, 2 * P:3 * P], ALU.mult, ALU.add
                                                     ).then_inc(s_here, 1)
                        dve.tensor_copy(OT[:, c * P:(c + 1) * P], ps[:, 2, P:2 * P]).then_inc(ps_free[uc % 2], 1)
                    wait_emptied(dve, u + 15, i, HP2)
                    dve.reciprocal(G[:, 2, :], G[:, 2, :])
                    own.link(dve.reciprocal(G[:, 3, 0:NB], G[:, 3, 0:NB]))
                    gain = sm[:, ds(h + (NORMS * KD + 8), 1)]
                    own.up(dve.scalar_tensor_tensor(OT[:, 0:T], OT[:, 0:T], gain, G[:, 2, :], ALU.mult, ALU.mult))
                    own.link(dve.scalar_tensor_tensor(OT[:, T:TT], OT[:, T:TT], gain, G[:, 3, 0:NB], ALU.mult, ALU.mult))
                    m = mix[:, ds(h, 1), :].rearrange("p a n -> p (a n)")
                    dve.tensor_tensor(m, m, OT, ALU.mult).then_inc(mix_here, 1)

            wait_full(dve, U_S - 1)
            dve.wait_ge(qb_zero, 1)
            qf = QB.rearrange("p b c -> p (b c)")
            for half in range(2):
                rows = slice(64 * half, 64 * half + 64)
                for j in range(HA):
                    ins = dve.tensor_copy(qf[rows, j + 4 * half:j + 4 * half + 72 * (NB - 1) + 1:72],
                                          mix[rows, HA + j, T:TT])
            ins.then_inc(qb_here, 1)

            wait_full(dve, U_S)
            ps = bank(U_S)
            dve.tensor_tensor(G24, ps[0:64, 1, 0:24], H24, ALU.mult)
            dve.tensor_tensor(PC[:, 0:NCS], ps[0:64, 0, 0:NCS], BC, ALU.add).then_inc(ps_free[U_S % 2], 1)
            wait_emptied(dve, U_S)
            own.link(dve.tensor_reduce(GS, G24.rearrange("p (h c) -> p c h", c=3), AX_X, ALU.add))
            dve.tensor_reduce(NM[:, 0:1], PC[:, 0:NCS], AX_X, ALU.max, negate=True).then_inc(sx_max, 1)
            wait_full(dve, U_S + 1)
            ps = bank(U_S + 1)
            dve.wait_ge(vec_in, 32)
            dve.tensor_tensor(SW[:, 0:WIN], ps[0:64, 0, :], BW[:, 0:WIN], ALU.add)
            dve.tensor_tensor(SW[:, WIN:WIN + 1], ps[0:64, 1, 0:1], BW[:, WIN:WIN + 1], ALU.add
                              ).then_inc(ps_free[(U_S + 1) % 2], 1)
            wait_emptied(dve, U_S + 1)
            dve.tensor_reduce(NM[:, 2:3], SW, AX_X, ALU.max, negate=True).then_inc(sx_max, 1)
            dve.wait_ge(sx_exp, 1)
            own.link(dve.reciprocal(RI[:, 0:1], DS[:, 0:1]))
            dve.tensor_scalar(PC[:, 0:NCS], PC[:, 0:NCS], RI[:, 0:1], None, ALU.mult).then_inc(pc_here, 1)
            dve.wait_ge(pc_here, 1)
            dve.tensor_scalar(PCG[:, 0:NCS], PC[:, 0:NCS], GS[:, 0:1], None, ALU.mult).then_inc(pc_here, 1)
            wait_full(dve, U_S + 2)
            dve.tensor_copy(IT[0:NCS], bank(U_S + 2)[0:NCS, 0, 0:64]).then_inc(ps_free[U_S % 2], 1)
            dve.wait_ge(sx_exp, 2)
            own.link(dve.reciprocal(RI[:, 2:3], DS[:, 2:3]))
            dve.tensor_scalar(SW, SW, RI[:, 2:3], GS[:, 2:3], ALU.mult, ALU.mult).then_inc(sw_here, 1)
            wait_full(dve, U_S + 3)
            ps = bank(U_S + 3)
            dve.tensor_copy(SCO, ps[0:64, 0, 0:NBLK])
            dve.tensor_copy(PCT[0:NCS], ps[0:NCS, 1, 0:64]).then_inc(ps_free[(U_S + 3) % 2], 1)
            wait_emptied(dve, U_S + 3)
            own.link(dve.memset(SCO[:, 0:1], 1e9))
            own.link(dve.memset(SCO[:, NBLK - 2:NBLK], 1e9))
            dve.wait_ge(tri_in, 16)
            square = [64, NBLK, NBLK]
            other, mine = SCO.unsqueeze(1).to_broadcast(square), SCO.unsqueeze(2).to_broadcast(square)
            own.up(dve.tensor_tensor(TA, other, mine, ALU.is_gt))
            own.link(dve.tensor_tensor(TB, other, mine, ALU.is_equal))
            own.link(dve.tensor_tensor(TB, TB, TRI, ALU.mult))
            own.link(dve.tensor_tensor(TA, TA, TB, ALU.add))
            own.link(dve.tensor_reduce(RANK, TA, AX_X, ALU.add))
            dve.tensor_scalar(SELB, RANK, float(NSEL), -FAR, ALU.is_ge, ALU.mult).then_inc(rank_done, 1)
            dve.wait_ge(rank_done, 1)
            dve.wait_ge(bias_in, 16)
            sb3 = SB[:, 0:PAST].rearrange("p (b n) -> p b n", n=64)
            own.link(dve.tensor_tensor(sb3, sb3, SELB[:, 0:NBLK - 1].unsqueeze(2).to_broadcast([64, NBLK - 1, 64]), ALU.add))
            wait_full(dve, U_S + 5)
            d, e = bank(U_S + 4), bank(U_S + 5)
            flat = "p a b -> p (a b)"
            dve.tensor_tensor(SX[:, PAST:PAST + 1], d[0:64, 2, 0:1], SB[:, PAST:PAST + 1], ALU.add)
            dve.tensor_tensor(SX[:, 0:1024], d[0:64, 0:2, :].rearrange(flat), SB[:, 0:1024], ALU.add
                              ).then_inc(ps_free[U_S % 2], 1)
            dve.tensor_tensor(SX[:, 1024:PAST], e[0:64, 0:2, :].rearrange(flat), SB[:, 1024:PAST], ALU.add
                              ).then_inc(ps_free[(U_S + 1) % 2], 1)
            wait_emptied(dve, U_S + 4)
            wait_emptied(dve, U_S + 5)
            dve.tensor_reduce(NM[:, 1:2], SX, AX_X, ALU.max, negate=True).then_inc(sx_max, 1)
            dve.wait_ge(sx_exp, 3)
            own.link(dve.reciprocal(RI[:, 1:2], DS[:, 1:2]))
            own.link(dve.tensor_scalar(SX, SX, RI[:, 1:2], GS[:, 1:2], ALU.mult, ALU.mult))
            dve.wait_ge(sw_here, 1)
            own.up(dve.tensor_scalar(T8[:, 0, :], B8, SX[:, PAST:PAST + 1], None, ALU.mult))
            dve.tensor_scalar(T8[:, 1, :], B8, SW[:, WIN:WIN + 1], None, ALU.mult).then_inc(sp_here, 1)
            wait_full(dve, U_S + 6)
            ps = bank(U_S + 6)
            dve.tensor_copy(PTS.rearrange(flat), ps[:, 0:2, :].rearrange(flat))
            dve.tensor_copy(PTW.rearrange(flat), ps[:, 2, 0:256])
            dve.tensor_copy(PN.rearrange(flat), ps[0:NB, 2, 256:384]).then_inc(ps_free[U_S % 2], 1)
            wait_full(dve, U_S + 7)
            own.link(dve.tensor_reduce(OB, bank(U_S + 7)[:, 0, 0:320].rearrange("p (a c) -> p c a", c=64), AX_X, ALU.add))
            ob = OB.rearrange("p (b h) -> p h b", h=HB)
            dve.tensor_copy(mix[0:64, HA:2 * HA, T:TT], ob[0:64, 0:HA, :])
            dve.tensor_copy(mix[64:128, HA:2 * HA, T:TT], ob[64:128, HA:2 * HA, :]).then_inc(ps_free[(U_S + 7) % 2], 1)
            wait_emptied(dve, U_S + 7)
            own.k += 1
            dve.memset(OB[:, 0:1], 0.0).then_inc(dve_done, 1)
            dve.memset(OB[:, 1:2], 0.0).then_inc(ob_here, 1)

            psf = PS[:, :, :].rearrange(flat)
            dve.wait_ge(tab_in, 32)

            def first(n, i, j, half):
                dve.wait_ge(sc_full, n + 1)
                if n >= 3:
                    dve.wait_ge(pv_full, n - 2)
                for c, cols in spans(i):
                    tab = TABC[:, i, 0:NCP] if c == 0 else TAB[:, cols]
                    ins = dve.scalar_tensor_tensor(SS[:, n % 3, cols], tab, NSL[:, j + 4 * half:j + 4 * half + 1],
                                                   psf[:, cols], ALU.mult, ALU.add)
                ins.then_inc(sc_free, 1)
                dve.wait_ge(sc_free, n + 1)
                for c, cols in spans(i):
                    ins = dve.tensor_reduce(NG[:, n % 3, c:c + 1], SS[:, n % 3, cols], AX_X, ALU.max, negate=True)
                ins.then_inc(mx_here, 1)

            def second(n, i, j, half):
                rg = RG[:, n % 3, :]
                dve.wait_ge(ex_here, n + 1)
                dve.reciprocal(rg, DG[:, n % 3, :]).then_inc(rd_here, 1)
                dve.wait_ge(rd_here, n + 1)
                h = j + 4 * half
                gate = GT[:, i, 3 * h:3 * h + 3]
                if i == 0:
                    dve.scalar_tensor_tensor(rg[:, 0:1], rg[:, 0:1], VALID, gate[:, 0:1], ALU.mult, ALU.mult)
                    dve.tensor_tensor(rg[:, 1:3], rg[:, 1:3], gate[:, 1:3], ALU.mult).then_inc(rg_here, 1)
                else:
                    dve.tensor_tensor(rg, rg, gate, ALU.mult).then_inc(rg_here, 1)
                dve.wait_ge(rg_here, n + 1)
                for c, cols in spans(i)[1:]:
                    part = SS[:, n % 3, cols]
                    ins = dve.tensor_scalar(part, part, rg[:, c:c + 1], None, ALU.mult)
                ins.then_inc(pw_here, 1)

            attention(1, first, second)
            dve.wait_ge(pv_full, len(units))
            dve.wait_ge(nat_out, 16 * 6)
            dve.wait_ge(snat_out, 16 * 6)
            for n in range(2):
                ins = dve.memset(U[n][:, 0:2], 0.0)
            ins.then_inc(pad_here, 1)

            for k in range(2):
                split_low(dve, k)
            dve.wait_ge(mix_a, HA)
            for k in range(HA, 2 * HA):
                dve.wait_ge(mix_hi, k + 1)
                dve.tensor_tensor(H2[:, k, 1, :], mix[:, k, :], H2[:, k, 0, :], ALU.subtract).then_inc(mix_b, 1)

            def add_tile(u, k, n, norm, i):
                wait_full(dve, u + n, i, 2)
                t = xT[:, ds(k, 1), :].rearrange("p a (n m) -> p (a n) m", n=TN)
                dve.scalar_tensor_tensor(t, wide(u + n), 1 / UNIT, t, ALU.mult, ALU.add).then_inc(ps_free[(u + n) % 2], 1)
                dve.wait_ge(sq_here, at(i, 2, KD * norm + n + 1))
                dve.wait_ge(acc_here, at(i, 2, KD * norm + n + 2))
                dve.tensor_tensor(ACC, ACC, SQ[n], ALU.add).then_inc(acc_here, 1)

            def normed(norm):
                wait_emptied(dve, PLAN[f"norm{norm}"][0])
                own.link(dve.reciprocal(RS, RS))
                for k in range(KD):
                    to = HN if norm < 4 else hT
                    dve.scalar_tensor_tensor(to[:, k, :], xT[:, k, :], sm[:, norm * KD + k:norm * KD + k + 1], RS,
                                             ALU.mult, ALU.mult).then_inc(t_here if norm < 4 else h_here, 1)
                    if norm < 4 and k % 2:
                        dve.wait_ge(hi_here, KD * (norm - 1) + k)
                        dve.tensor_tensor(H2[:, k - 1, 1, :], HN[:, k - 1, :], H2[:, k - 1, 0, :], ALU.subtract
                                          ).then_inc(lo_even, 1)

            def residual(name, norm):
                u, c = PLAN[name][0], STEP[name]
                own.link(dve.memset(ACC, 0.0))
                with dve.Fori(0, KD // 2) as i:
                    for n in range(2):
                        split_low(dve, c + n + 2, i, 2)
                        add_tile(u, i * 2 + n, n, norm, i)
                normed(norm)

            def down_residual(name, norm, last=False):
                u, c = PLAN[name][0], STEP[name]
                own.link(dve.memset(ACC, 0.0))

                def turn(i, widths):
                    for n in range(2):
                        if widths[n]:
                            for k in range(2):
                                split_low(dve, c + 2 * n + 2 + k, i, 4, widths[n])
                        add_tile(u, i * 2 + n, n, norm, i)

                with dve.Fori(0, KD // 2 - 1) as i:
                    turn(i, (WCH, WCH))
                turn(KD // 2 - 1, (WCH, None if last else D))
                normed(norm)

            def taps(y, row, old, weight, last=None):
                own.up(dve.scalar_tensor_tensor(y[:, 0:T], row[:, 1:1 + T], weight(1), y[:, 0:T], ALU.mult, ALU.add))
                own.link(dve.scalar_tensor_tensor(y[:, T:TT], old(1), weight(1), y[:, T:TT], ALU.mult, ALU.add))
                own.up(dve.scalar_tensor_tensor(y[:, 0:T], row[:, 0:T], weight(0), y[:, 0:T], ALU.mult, ALU.add))
                ins = dve.scalar_tensor_tensor(y[:, T:TT], old(0), weight(0), y[:, T:TT], ALU.mult, ALU.add)
                if last is None:
                    own.link(ins)
                else:
                    ins.then_inc(last, 1)

            def ffn_up(name, tiles, pairs):
                u, c = PLAN[name][0], STEP[name]

                def turn(i, widths):
                    for p in range(2):
                        for n in range(2):
                            t = 2 * p + n
                            split_low(dve, c + t + 2, i, 4, widths[p])
                            wait_emptied(dve, u + t, i, 4)
                            dve.wait_ge(u_here, at(i, 4, tiles + t + 1))
                            taps(Y[n], U[n], lambda r: FS[:, ds(i * 4 + t, 1), r, :].rearrange("p a b -> p (a b)"),
                                 lambda r: FW[:, ds(i * 4 + t, 1), r], None if n else y_here)
                        dve.wait_ge(silu_here, at(i, 2, pairs + p + 1))
                        dve.tensor_tensor(Y[0], Y[0], Y[1], ALU.mult).then_inc(zm_here, 1)

                with own.turns(KF // 2 - 1, 14) as i:
                    turn(i, (D, D))
                turn(KF // 2 - 1, (D, WCH))

            residual("mix_out", 1)
            ffn_up("up0", 0, 0)
            dve.wait_ge(z_here, 1 + KF)
            down_residual("down0", 2)
            u, c = PLAN["conv_in"][0], STEP["conv_in"]
            with own.turns(KD // 2, 8) as i:
                for n in range(2):
                    t = i * 2 + n
                    v = u + 3 * n
                    split_low(dve, c + 3 * n + 2, i, 6)
                    wait_full(dve, v + 1, i, 6)
                    wait_emptied(dve, v, i, 6)
                    dve.wait_ge(st_here, at(i, 2, 2 * KF + n + 1))
                    dve.scalar_tensor_tensor(three(U[n][:, 2:2 + TT]), wide(v + 1), 1 / UNIT, three(Y[0]),
                                             ALU.mult, ALU.mult).then_inc(u_here, 1)
                    split_low(dve, c + 3 * n + 3, i, 6)
                    dve.wait_ge(u_here, at(i, 2, 2 * KF + n + 1))
                    dve.wait_ge(cy_here, at(i, 2, n + 1))
                    dve.tensor_scalar(Y[1], U[n][:, 2:2 + TT], CSW[:, ds(t, 1), 2], None, ALU.mult
                                      ).then_inc(ps_free[(v + 1) % 2], 1)
                    wait_emptied(dve, v + 1, i, 6)
                    taps(Y[1], U[n], lambda r: CSS[:, ds(t, 1), r, :].rearrange("p a b -> p (a b)"),
                         lambda r: CSW[:, ds(t, 1), r])
                    split_low(dve, c + 3 * n + 4, i, 6)
                    wait_full(dve, v + 2, i, 6)
                    dve.scalar_tensor_tensor(three(Y[1]), wide(v + 2), 1 / UNIT, three(Y[1]), ALU.mult, ALU.mult
                                             ).then_inc(ps_free[v % 2], 1)
            dve.wait_ge(cy_here, 1 + KD)
            residual("conv_out", 3)
            ffn_up("up1", 2 * KF + KD, KF)
            dve.wait_ge(z_here, 1 + 2 * KF)
            down_residual("down1", 4, last=True)

        @block.tensor
        def _(pe):
            def norm(u, n):
                pe.wait_ge(c_in, 16 * 5)
                pe.wait_ge(acc_here, 2 + KD * (n + 1))
                wait_free(pe, u)
                for m in range(TN):
                    ins = pe.matmul(wide(u)[:, m, :], mean_d, ACC[:, m * TW:(m + 1) * TW], start=True, stop=True)
                ins.then_inc(ps_full, 1)

            def tile(u, w, src, i=None, up=0, wp=0, ready=0):
                wait_free(pe, u, i, up)
                pe.wait_ge(w_in[w % 2], at(i, 8 * wp, 16 * (w // 2 + 1)))
                for k in range(KD):
                    if ready:
                        pe.wait_ge(h_here, ready + k)
                    for m in range(TN):
                        ins = pe.matmul(wide(u)[:, m, :], W[:, w % 2, k * P:(k + 1) * P],
                                        src[:, k, m * TW:(m + 1) * TW], start=(k == 0), stop=(k == KD - 1))
                ins.then_inc(ps_full, 1)

            norm(U_N0, 0)
            pe.wait_ge(h_here, KD)
            with pe.Fori(0, HA // 2) as i:
                for hh in range(2):
                    u = U_H + hh * HEAD_PS
                    for k in range(HEAD_TILES):
                        tile(u + k, W_H + hh * HEAD_TILES + k, hT, i, HP2, HT2)
                    wait_free(pe, u + 5, i, HP2)
                    wait_emptied(pe, u + 2, i, HP2)
                    pe.wait_ge(k_here, at(i, 2, hh + 1))
                    ps = bank(u + 5)
                    for c in range(NC):
                        pe.transpose(ps[:, c // 4, (c % 4) * P:(c % 4 + 1) * P], VT[:, c * P:(c + 1) * P], ident)
                    pe.transpose(ps[0:NB, 2, 0:P], VT[:, T:TT], ident)
                    pe.transpose(ps[0:NB, 2, P:2 * P], KT[:, T:TT], ident).then_inc(ps_full, 1)
                    wait_free(pe, u + 6, i, HP2)
                    pe.wait_ge(vm_here, at(i, 2, hh + 1))
                    pss = bank(u + 6)
                    for n in range(2):
                        ins = pe.matmul(pss[:, n, :], VH[0:NB, NC + 1, :], VMs[:, 4 * n:4 * n + 4, :],
                                        start=True, stop=True)
                    ins.then_inc(ps_full, 1)

                    def att(c):
                        uc = u + 7 + c
                        wait_free(pe, uc, i, HP2)
                        ps = bank(uc)
                        tok = slice(c * P, (c + 1) * P)
                        pe.matmul(ps[:, 0, 0:P], KT[:, tok], QT[:, tok], start=True, stop=True)
                        for lev in range(LEV):
                            n = lev + 1
                            pe.matmul(ps[:, n // 4, (n % 4) * P:(n % 4 + 1) * P], G[:, lev, tok], G[:, lev, tok],
                                      start=True, stop=True)
                        pe.transpose(ps[:, 2, 0:P], KE[:, tok], ident).then_inc(ps_full, 1)

                    pe.wait_ge(g_here, at(i, 2 * (LEV + 1), (hh + 1) * (LEV + 1)))
                    att(0)
                    pe.wait_ge(sn_here, at(i, 2, hh + 1))
                    for b in range(NB):
                        ins = pe.matmul(pss[:, 2, b:b + 1], SN[:, b, :], QT[:, T + b:T + b + 1], start=True, stop=True)
                    ins.then_inc(so_here, 1)
                    for c in range(NC):
                        if c + 1 < NC:
                            att(c + 1)
                        ps = bank(u + 7 + c)
                        tok = slice(c * P, (c + 1) * P)
                        pe.wait_ge(at_here, at(i, 2 * NC, hh * NC + c + 1))
                        pe.matmul(ps[:, 2, P:2 * P], VH[:, c, :], AT[:, c % 2, :], start=True, stop=(c == 0))
                        if c:
                            pe.wait_ge(s_here, at(i, 2 * (NC + 1), hh * (NC + 1) + c + 1))
                            pe.matmul(ps[:, 2, P:2 * P], S, QE[:, tok], start=False, stop=True)
                        pe.matmul(ps[:, 2, 2 * P:3 * P], KN[:, c % 2, :], VH[:, c, :], start=True, stop=True
                                  ).then_inc(oc_here, 1)
                    wait_free(pe, u + 15, i, HP2)
                    pe.wait_ge(ot_sq, at(i, 2, hh + 1))
                    ps = bank(u + 15)
                    for n in range(2):
                        pe.matmul(ps[:, n, :], mean_v, G[:, 0, n * 512:(n + 1) * 512], start=True, stop=True)
                    pe.matmul(ps[:, 2, 0:NB], mean_v, G[:, 1, 0:NB], start=True, stop=True).then_inc(ps_full, 1)

            held = (KVT[:, 0, :], KVT[:, 1, :], KVT[:, 2, :], VX, KVT[:, 3, :], VX)

            def turn(n):
                u = kv_turn[n]
                wait_free(pe, u)
                wait_emptied(pe, kv_tile[n])
                ps = bank(u)
                for c in range(NC):
                    pe.transpose(ps[:, c // 4, (c % 4) * P:(c % 4 + 1) * P], held[n][:, c * P:(c + 1) * P], ident)
                pe.transpose(ps[0:NB, 2, 0:P], held[n][:, T:TT], ident).then_inc(ps_full, 1)

            tile(kv_tile[0], W_KV, hT)
            for n in range(1, 6):
                tile(kv_tile[n], W_KV + n, hT)
                turn(n - 1)
            turn(5)
            wait_free(pe, U_G)
            for c in range(NC + 1):
                tok = slice(c * P, min((c + 1) * P, TT))
                for k in range(KD):
                    ins = pe.matmul(bank(U_G)[0:min(P, TT - c * P), 0, c * 24:(c + 1) * 24], hT[:, k, tok], WG[:, k, :],
                                    start=(k == 0), stop=(k == KD - 1))
            ins.then_inc(ps_full, 1)

            def squeeze(u, i, per, cols, source):
                wait_free(pe, u, i, per)
                ps = bank(u)
                for k in range(2):
                    for r in range(CMP):
                        ins = pe.matmul(ps[:, k, 0:cols], W1[:, k, r, :], source(k, r), start=(r == 0), stop=(r == CMP - 1))
                if i is None:
                    for k in range(2):
                        for r in range(CMP):
                            ins = pe.matmul(ps[:, 2, k:k + 1], W1[:, k, r, :], PE_T[:, k, r:r + 1],
                                            start=(r == 0), stop=(r == CMP - 1))
                ins.then_inc(ps_full, 1)
                wait_free(pe, u + 1, i, per)
                wait_emptied(pe, u, i, per)
                kv = bank(u + 1)
                pe.matmul(kv[:, 0, 0:cols], W2[:, 0, :], HID[:, 0, 0:cols], start=True, stop=True)
                pe.matmul(kv[0:cols, 1, 0:P], HID[:, 1, 0:cols], W2[:, 1, :], start=True, stop=True).then_inc(ps_full, 1)

            pe.wait_ge(w1_in, 16 * 6)
            squeeze(U_C, None, 0, NCP, lambda k, r: KVT[:, k, r:r + STRIDE * (NCP - 1) + 1:STRIDE])
            with pe.Fori(0, NB // 2) as i:
                for b in range(2):
                    pe.wait_ge(xc_in[b], at(i, 16 * NPG, 16 * NPG))
                    squeeze(U_C + 2 + 2 * b, i, 4, NCS,
                            lambda k, r: XC[b][:, k, r:r + STRIDE * (NCS - 1) + 1:STRIDE])

            pe.wait_ge(qb_here, 1)
            pe.wait_ge(vec_in, 32)
            wait_emptied(pe, U_S - 1)
            wait_free(pe, U_S)
            ps = bank(U_S)
            pe.matmul(ps[0:64, 1, 0:24], B8T, GT[0:NB, NC, :], start=True, stop=True)
            for b in range(NB):
                ins = pe.matmul(ps[0:64, 0, 0:NCS], QB[:, b, :], KC[:, b, 0:NCS], start=(b == 0), stop=(b == NB - 1))
            ins.then_inc(ps_full, 1)
            wait_free(pe, U_S + 1)
            pe.wait_ge(win_in, 32)
            ps = bank(U_S + 1)
            for b in range(NB):
                pe.matmul(ps[0:64, 0, :], QB[:, b, :], KW[:, b, :], start=(b == 0), stop=(b == NB - 1))
            for b in range(NB):
                ins = pe.matmul(ps[0:64, 1, 0:1], QB[:, b, :], KVT[:, 3, T + b:T + b + 1], start=(b == 0),
                                stop=(b == NB - 1))
            ins.then_inc(ps_full, 1)
            wait_free(pe, U_S + 2)
            pe.wait_ge(pc_here, 1)
            pe.matmul(bank(U_S + 2)[0:NCS, 0, 0:64], PC[:, 0:NCS], SAME, start=True, stop=True).then_inc(ps_full, 1)
            wait_free(pe, U_S + 3)
            ps = bank(U_S + 3)
            pe.wait_ge(pc_here, 2)
            pe.transpose(ps[0:NCS, 1, 0:64], PCG[:, 0:NCS], ident[0:64, 0:64])
            wait_emptied(pe, U_S + 2)
            pe.matmul(ps[0:64, 0, 0:NBLK], IT[0:NCS], COVER, start=True, stop=True).then_inc(ps_full, 1)
            wait_free(pe, U_S + 4)
            wait_free(pe, U_S + 5)
            d, e = bank(U_S + 4), bank(U_S + 5)
            for b in range(NB):
                pe.matmul(d[0:64, 2, 0:1], QB[:, b, :], KVT[:, 2, T + b:T + b + 1], start=(b == 0), stop=(b == NB - 1))
            for b in range(NB):
                pe.wait_ge(kb_in[b % 2], 16 * NPG * (b // 2 + 1))
                for n in range(4):
                    ins = pe.matmul((d, e)[n // 2][0:64, n % 2, :], QB[:, b, :], KB[b % 2][:, n * 512:(n + 1) * 512],
                                    start=(b == 0), stop=(b == NB - 1))
                    if b == NB - 1 and n % 2:
                        ins.then_inc(ps_full, 1)
                if b < NB - 1:
                    ins.then_inc(kb_used, 1)
            wait_free(pe, U_S + 6)
            pe.wait_ge(sp_here, 1)
            ps = bank(U_S + 6)
            i64 = ident[0:64, 0:64]
            for t in range(NPG):
                pe.transpose(ps[:, t // 8, (t % 8) * 64:(t % 8 + 1) * 64], SX[:, t * P:(t + 1) * P], i64)
            for t in range(WIN // P):
                pe.transpose(ps[:, 2, t * 64:(t + 1) * 64], SW[:, t * P:(t + 1) * P], i64)
            for n in range(2):
                ins = pe.matmul(ps[0:NB, 2, 256 + 64 * n:320 + 64 * n], T8[:, n, :], i64, start=True, stop=True)
            ins.then_inc(ps_full, 1)
            wait_free(pe, U_S + 7)
            wait_emptied(pe, U_S + 6)
            ps = bank(U_S + 7)
            pe.matmul(ps[:, 0, 128:192], SNT[0:NB, 3, :], PN[:, 0, :], start=True, stop=True)
            pe.matmul(ps[:, 0, 256:320], SNT[0:NB, 5, :], PN[:, 1, :], start=True, stop=True)
            for b in range(NB):
                pe.matmul(ps[:, 0, b * 8:b * 8 + 8], VC[0:NCS, b, :], PCT[0:NCS, b * 8:b * 8 + 8], start=True, stop=True)
                for t in range(WIN // P):
                    pe.matmul(ps[:, 0, 192 + b * 8:200 + b * 8], VW[:, b, t, :], PTW[:, t, b * 8:b * 8 + 8],
                              start=(t == 0), stop=(t == WIN // P - 1))
            for b in range(NB):
                pe.wait_ge(vb_in[b % 2], 16 * NPG * (b // 2 + 1))
                for t in range(NPG):
                    ins = pe.matmul(ps[:, 0, 64 + b * 8:72 + b * 8], VB[b % 2][:, t, :], PTS[:, t, b * 8:b * 8 + 8],
                                    start=(t == 0), stop=(t == NPG - 1))
                if b < NB - 1:
                    ins.then_inc(vb_used, 1)
            ins.then_inc(ps_full, 1)

            def first(n, i, j, half):
                rows = slice(64 * half, 64 * half + 64)
                q = mix[rows, HA + j, i * P:(i + 1) * P]
                psf = PS[:, :, :].rearrange("p a b -> p (a b)")
                if n:
                    pe.wait_ge(sc_free, n)
                (_, slc), (_, win), (_, cmp) = spans(i)
                for cols, key, src in (slc, 0, 2), (win, max(0, i - 4) * P, 3):
                    lo = cols.start
                    while lo < cols.stop:
                        end = min(cols.stop, (lo // 512 + 1) * 512)
                        pe.matmul(psf[:, lo:end], q, KVT[rows, src, key:key + end - lo], start=True, stop=True)
                        lo, key = end, key + end - lo
                pe.matmul(psf[:, cmp], q, KC[rows, NB, 0:NCP], start=True, stop=True).then_inc(sc_full, 1)

            def second(n, i, j, half):
                bl = blocks(i)
                rows = slice(64 * half, 64 * half + 64)

                def values(g):
                    pe.wait_ge(t_free, group_at[n] + g + 1)
                    if g == 0 and half == 0 and n >= 4:
                        pe.wait_ge(pv_free, n // 2 - 1)
                    for b, (kind, t, _) in enumerate(bl[4 * g:4 * g + 4]):
                        p = PT[:, half, (4 * g + b) * P:(4 * g + b + 1) * P]
                        if kind == "cmp":
                            v, p = VC[0:NCP, NB, rows], p[0:NCP]
                        else:
                            v = (VSL if kind == "slc" else VWN)[:, t, rows]
                        ins = pe.matmul(PS[rows, 6 + n // 2 % 2, 0:P], v, p, start=(g == b == 0),
                                        stop=(4 * g + b == len(bl) - 1), skip_group_check=True)
                    return ins

                pe.wait_ge(p_here, n + 1)
                pe.wait_ge(pw_here, n + 1)
                for g in range(groups[i]):
                    if group_at[n] + g >= 2:
                        pe.wait_ge(t_free, group_at[n] + g - 1)
                    for b, (kind, _, c) in enumerate(bl[4 * g:4 * g + 4]):
                        m = NCP if kind == "cmp" else P
                        ins = pe.transpose(PS[0:m, 4 + (group_at[n] + g) % 2, b * P:(b + 1) * P],
                                           SS[:, n % 3, c:c + m], ident)
                    ins.then_inc(t_full, 1)
                    if g:
                        values(g - 1)
                values(groups[i] - 1).then_inc(pv_full, 1)

            wait_free(pe, U_S + 8)
            wait_free(pe, U_S + 9)
            attention(2, first, second)
            pe.wait_ge(pv_free, HA * NC)

            def product(u, n, f, src, first, last):
                for half, others in ((0, (0, 1)), (1, (0,))):
                    weights = W2H[:, n, half, f * P:(f + 1) * P]
                    for m in range(TN):
                        for other in others:
                            ins = pe.matmul(wide(u)[:, m, :], weights, src[:, other, m * TW:(m + 1) * TW],
                                            start=(first and half == other == 0), stop=(last and half == 1))
                return ins

            def stage(name, src, ready):
                u, c = PLAN[name][0], STEP[name]
                with pe.Fori(0, PLAN_N[name] // 2) as i:
                    for k in range(2):
                        wait_free(pe, u + k, i, 2)
                        pe.wait_ge(w_split, at(i, 2, c + k + 1))
                        for f in range(KD):
                            if k == 0:
                                ready(f)
                            ins = product(u + k, k, f, src[:, f], f == 0, f == KD - 1)
                        ins.then_inc(ps_full, 1)

            def down(name, base):
                u, c = PLAN[name][0], STEP[name]
                with pe.Fori(0, KD // 2) as i:
                    for k in range(2):
                        wait_free(pe, u + k, i, 2)
                        for n in range(2):
                            pe.wait_ge(w_split, at(i, 4, c + 2 * k + n + 1))
                            for f in range(KH):
                                g = n * KH + f
                                if k == 0:
                                    pe.wait_ge(z_here, base + g + 2)
                                ins = product(u + k, n, f, Z2[:, g], g == 0, g == KF - 1)
                            ins.then_inc(ps_full if n else half_used, 1)

            def normed(norm):
                return lambda f: pe.wait_ge((lo_even, lo_odd)[f % 2], (norm - 1) * KD // 2 + f // 2 + 1)

            stage("mix_out", H2, lambda f: pe.wait_ge(*((mix_a, f + 1) if f < HA else (mix_b, f - HA + 1))))
            norm(PLAN["norm1"][0], 1)
            stage("up0", H2, normed(1))
            down("down0", 0)
            norm(PLAN["norm2"][0], 2)
            stage("conv_in", H2, normed(2))
            stage("conv_out", Z2, lambda f: pe.wait_ge(cy_here, f + 2))
            norm(PLAN["norm3"][0], 3)
            stage("up1", H2, normed(3))
            down("down1", KF)
            norm(PLAN["norm4"][0], 4)


def kernel(**inputs):
    import concourse.bacc as bacc
    from concourse.bass_utils import run_bass_kernel_spmd as run

    a = {k: np.asarray(v) for k, v in inputs.items()}
    r = np.arange

    def columns(w, cols):
        k = w.shape[0] // P
        return w[:, cols].reshape(k, P, len(cols)).transpose(1, 0, 2).reshape(P, -1)

    def feature(v):
        v = v.reshape(v.shape[:-1] + (-1, P))
        return np.moveaxis(v, (-1, -2), (0, 1))

    ab, ab_out = a["ab_w_in"][0], a["ab_w_out"][0]
    pair = [np.concatenate([j * HD + r(HD), (j + HA) * HD + r(HD)]) for j in range(HA)]
    chunks = []
    for h in range(HA):
        chunks += [columns(ab, off + h * P + r(P)) for off in (512, 0, 1024, 1536)] + [columns(ab, 2048 + pair[h])]
    chunks += [columns(ab, 2560 + n * P + r(P)) for n in range(6)]
    mixed = np.concatenate([r(HA * P)] + [HA * P + p for p in pair])
    chunks += [columns(ab_out[mixed], n * P + r(P)) for n in range(KD)]
    hidden = np.stack([r(KF), KF + r(KF)], 1).reshape(-1)
    up = [[columns(a["ffn_up"][n], t * P + r(P)) for t in hidden] for n in range(2)]
    three = np.stack([r(KD), KD + r(KD), 2 * KD + r(KD)], 1).reshape(-1)
    chunks += up[0] + [columns(a["c_w_in"][0], t * P + r(P)) for t in three]
    chunks += [columns(a["c_w_out"][0], t * P + r(P)) for t in range(KD)] + up[1]
    down = [[columns(a["ffn_down"][n][h * KH * P:(h + 1) * KH * P], t * P + r(P)) for t in range(KD) for h in range(2)]
            for n in range(2)]

    x = np.concatenate([a["x_prompt"][0], a["x_sample"][:, 0]])
    small = np.concatenate([feature(v) for v in (
        a["norm_mix"][0], a["norm_ffn"][0], a["norm_mix"][1], a["norm_ffn"][1], a["norm_final"],
        a["hgrn_lb_logits"][0], a["hgrn_lb_logits"][1], a["hgrn_norm"][0])], 1)

    s, t = np.meshgrid(r(P), r(P), indexing="ij")
    cst = np.zeros((P, 4, P), np.float32)
    cst[:, 0], cst[:, 1], cst[:, 2], cst[:, 3] = np.eye(P), 1 / D, 1 / P, 1
    hmask = np.zeros((P, LEV + 1, P), np.float32)
    hmask[:, 0] = np.eye(P)
    for lev in range(LEV):
        m = 1 << lev
        hmask[:, lev + 1] = (s // (2 * m) == t // (2 * m)) & (s // m % 2 == 0) & (t // m % 2 == 1)
    slope = 2.0 ** (-8.0 * (r(HB) + 1) / HB)
    row = r(NB * HB)
    csn = np.zeros((P, 330), np.float32)
    csn[0:64, 0:64] = row[:, None] // HA == row[None] // HA
    start, block = r(NCS)[:, None] * STRIDE, r(NBLK)[None] * 64
    csn[0:NCS, 64:97] = (start < block + 64) & (start + CMP > block)
    by_row = slope[row % HB][:, None]
    csn[0:64, 97:97 + NCS] = -by_row * (PAST - (start[:, 0] + CMP - 1))[None]
    csn[0:64, 224:232] = row[:, None] // HB == r(NB)[None]
    csn[0:NB, 232:296] = row[None] // HB == r(NB)[:, None]
    csn[0:64, 296:320] = row[:, None] % HB == r(3 * HB)[None] // 3
    csn[:, 320:328] = -slope
    csn[:, 328] = r(P) >= CMP - 1
    bias_w = (-by_row * (WIN - r(WIN + 1))[None]).astype(np.float32)
    bias_w[:, 0] = -FAR
    bias_s = (-by_row * (PAST - r(PAST + 1))[None]).astype(np.float32)
    tri = np.broadcast_to((r(NBLK)[None] < r(NBLK)[:, None]).astype(np.float32), (64, NBLK, NBLK))
    far = lambda dist, keep: np.where(keep, dist, FAR).astype(np.float32)
    dist = r(P)[:, None] - (r(T) - (T - P))[None]
    dist_w = r(P)[:, None] - (r(640) - 512)[None]
    table = np.concatenate([far(dist, dist >= 0), far(dist_w, (dist_w >= 0) & (dist_w < WIN))], 1)
    dist_c = (r(NC) * P)[None, :, None] + r(P)[:, None, None] - (r(64) * STRIDE + CMP - 1)[None, None]
    table_c = far(dist_c, dist_c >= 0)

    def rows_t(v):
        return feature(v).transpose(0, 1, 3, 2)

    w1 = a["cmp_w1"][0].reshape(2, CMP, HD, 64).transpose(2, 0, 1, 3).reshape(HD, 2 * CMP, 64)
    win = a["state_win_kv"][0].reshape(NB, WIN, 2, P)
    cmp_pool, slc_pool = (a[n].reshape(NPOOL, PAGE, 2, P) for n in ("cache_cmp_kv", "cache_slc_kv"))
    given = {
        "x": feature(x).transpose(0, 1, 2), "wk8": np.stack(chunks), "wdn": np.stack([np.stack(d) for d in down]),
        "small": small, "cst": cst, "hmask": hmask, "s_hgrn": a["state_hgrn"][0],
        "wgate": columns(ab, 3328 + r(24)).reshape(P, KD, 24), "pages": a["page_table"].reshape(1, -1),
        "cmp_t": cmp_pool.transpose(0, 3, 2, 1), "slc_kt": slc_pool[:, :, 0].transpose(0, 2, 1), "slc_v": slc_pool[:, :, 1],
        "win_kt": win[:, :, 0].transpose(2, 0, 1),
        "win_v": win[:, :, 1].reshape(NB, WIN // P, P, P).transpose(2, 0, 1, 3), "state_win": win,
        "w1": w1, "w2": a["cmp_w2"][0].transpose(1, 0, 2), "pe_t": a["cmp_pe"][0].transpose(2, 0, 1),
        "csn": csn, "bias_w": bias_w, "bias_s": bias_s, "tri": tri, "table": table, "table_c": table_c,
        "s_ff": np.stack([rows_t(a["state_ffn"][n])[:, hidden] for n in range(2)]),
        "w_ff": np.stack([feature(a["ffn_conv"][n])[:, hidden] for n in range(2)]),
        "s_sc": rows_t(a["state_sconv"][0]), "w_sc": feature(a["c_conv"][0]),
    }
    made = {
        "o_y": (P, KD, TT), "o_hgrn_p": (HA, P, P), "o_hgrn_s": (NB, HA, P, P), "o_cmp_p": (T, 2, P), "o_slc_p": (T, 2, P),
        "o_win_p": (WIN, 2, P), "o_cmp_s": (NB, 2, P), "o_slc_s": (NB, 2, P), "o_win_s": (NB, WIN, 2, P),
        "o_sc": (P, KD, 2 * (NB + 1)), "o_ff": (2, P, 2 * KF, 2 * (NB + 1)),
    }
    nc = bacc.Bacc("TRN2", target_bir_lowering=False, num_devices=1)
    arrays = {n: np.ascontiguousarray(v) for n, v in given.items()}
    args = [nc.dram_tensor(n, v.shape, mybir.dt.from_np(v.dtype), kind="ExternalInput").ap() for n, v in arrays.items()]
    args += [nc.dram_tensor(n, v, F32, kind="ExternalOutput").ap() for n, v in made.items()]
    program(nc, *args)
    o = run(nc, [arrays], core_ids=[0]).results[0]

    y = o["o_y"].transpose(2, 1, 0).reshape(TT, D)

    def last_rows(v, order=None):
        if order is not None:
            back = np.empty_like(v)
            back[:, order] = v
            v = back
        v = v.transpose(2, 1, 0).reshape(2 * (NB + 1), -1)
        return v[:2][None], v[2:].reshape(NB, 2, -1)

    sc_p, sc_s = last_rows(o["o_sc"])
    ff = [last_rows(o["o_ff"][n], hidden) for n in range(2)]
    kv = (2, 2, HD)
    return (
        y[:T][None], y[T:][:, None],
        o["o_cmp_p"].reshape(1, T, 1, *kv), o["o_slc_p"].reshape(1, T, 1, *kv), o["o_win_p"].reshape(1, 1, WIN, *kv),
        o["o_hgrn_p"][None, None], sc_p[None], np.stack([f[0] for f in ff]),
        o["o_cmp_s"].reshape(NB, 1, 1, *kv), o["o_slc_s"].reshape(NB, 1, 1, *kv), o["o_win_s"].reshape(1, NB, WIN, *kv),
        o["o_hgrn_s"][None], sc_s[None], np.stack([f[1] for f in ff]),
    )
```

```python
from contextlib import ExitStack, contextmanager

import numpy as np

import concourse.bass as bass
from concourse import mybir

F32 = mybir.dt.float32
F16 = mybir.dt.float16
I32 = mybir.dt.int32
ALU = mybir.AluOpType
ACT = mybir.ActivationFunctionType
AX_X = mybir.AxisListType.X
ds = bass.ds

P = 128
D = 1024
KD = D // P
T = 1024
NB = 8
TT = T + NB
NC = T // P
TN = 3
TW = TT // TN
FF = 2816
KF = FF // P
KH = KF // 2
HA = 4
LEV = 7
HB, HD = 8, 64
PAST, PAGE = 2048, 128
NPG = PAST // PAGE
NPOOL = 160
WIN = 512
CMP, STRIDE = 32, 16
NCP = T // STRIDE - 1
NCS = PAST // STRIDE - 1
NBLK = PAST // 64 + 1
NSEL = 16
EPS = 1e-6
FAR = 1e30
WCH = KH * P
NORMS = 5
UNIT = 64.0


class Chain:

    def __init__(self, engine, sem):
        self.engine, self.sem, self.base, self.k = engine, sem, 0, 0

    def up(self, instruction):
        instruction.then_inc(self.sem, 1)
        self.k += 1

    def settle(self):
        self.engine.wait_ge(self.sem, self.base + self.k)

    def link(self, instruction):
        self.up(instruction)
        self.settle()

    @contextmanager
    def turns(self, count, per):
        start = self.base + self.k
        with self.engine.Fori(0, count) as i:
            self.base, self.k = i * per + start, 0
            yield i
            assert self.k == per, f"the body raises {self.k} times, not {per}"
        self.base, self.k = start + count * per, 0


def at(i, per, first):
    return first if i is None else i * per + first


HEAD_TILES = 5
HEAD_PS = HEAD_TILES + 1 + 1 + NC + 1
PLAN = {}
PLAN_N = {}


def plan():
    u, w = 2, 0
    for name, tiles, chunks in (
        ("norm0", 1, 0), ("heads", HA * HEAD_PS, HA * HEAD_TILES), ("kv", 12, 6), ("gates", 1, 0),
        ("squeeze", 2 * (NB + 1), 0), ("sample", 8, 0),
        ("mix_out", KD, KD), ("norm1", 1, 0), ("up0", 2 * KF, 2 * KF), ("down0", KD, 2 * KD), ("norm2", 1, 0),
        ("conv_in", 3 * KD, 3 * KD), ("conv_out", KD, KD), ("norm3", 1, 0), ("up1", 2 * KF, 2 * KF), ("down1", KD, 2 * KD),
        ("norm4", 1, 0),
    ):
        PLAN[name] = (u, w)
        PLAN_N[name] = tiles
        u += tiles
        w += chunks


plan()


WK = KF * TT
WKW = 1056


def program(nc, x, wk8, wdn, small, cst, hmask, s_hgrn, wgate, pages, cmp_t, slc_kt, slc_v, win_kt, win_v, state_win,
            w1, w2, pe_t, csn, bias_w, bias_s, tri, table, table_c, s_ff, w_ff, s_sc, w_sc,
            o_y, o_hgrn_p, o_hgrn_s, o_cmp_p, o_slc_p, o_win_p, o_cmp_s, o_slc_s, o_win_s, o_sc, o_ff):
    with ExitStack() as ctx:
        def sb(name, shape, dt=F32):
            return ctx.enter_context(nc.sbuf_tensor(name, shape, dt))

        def sem(name):
            return ctx.enter_context(nc.semaphore(name))

        xT = sb("xT", [P, KD, TT])
        hT = sb("hT", [P, KD, TT])
        W = sb("W", [P, 2, WCH])
        R = sb("R", [P, 31900])
        sm = sb("sm", [P, NORMS * KD + 12])
        lb = sb("lb", [P, 5, HA])
        cs = sb("cs", [P, 4, P])
        eps = sb("eps", [P, 10])
        pg = sb("pg", [1, NB * NPG], I32)
        PS = ctx.enter_context(nc.psum_tensor("PS", [P, 8, 512], F32))
        ident, mean_d, mean_v, ones = (cs[:, n, :] for n in range(4))

        def reg(at0, *shape):
            n = 1
            for s in shape:
                n *= s
            v = R[:, at0:at0 + n]
            if len(shape) == 2:
                v = v.rearrange("p (a b) -> p a b", b=shape[1])
            if len(shape) == 3:
                v = v.rearrange("p (a b c) -> p a b c", b=shape[1], c=shape[2])
            return v

        mix = reg(0, KD, TT)
        QT, FT, KT, VT = (reg(8256 + n * TT, TT) for n in range(4))
        SL, SN = reg(12384, NB, P), reg(13408, NB, P)
        o = 15416
        AL = reg(o, TT)
        G = reg(o + 1032, LEV, T)
        QE = reg(o + 8200, T)
        KE = reg(o + 9224, T)
        VH = reg(o + 10248, NC + 2, P)
        AM = reg(o + 11528, 2, (LEV + 1) * P)
        AT = reg(o + 13576, 2, P)
        KN = reg(o + 13832, 2, P)
        OT = reg(o + 14088, TT)
        S = reg(o + 15120, P)
        EE = reg(o + 15248, NC)
        VMs = reg(o + 11528, NB, P)[0:NB]
        WG = sb("WG", [P, KD, 3 * HB])
        HM = sb("HM", [P, LEV + 1, P])
        KVT = reg(8256, 4, TT)
        VSL, VWN = reg(12384, NC, P), reg(13408, NC, P)
        SNT = reg(14432, 6, P)
        GT = reg(15200, NC + 1, 3 * HB)
        NAT = reg(15416, 4, T)
        VX = reg(27712, TT)
        W1 = reg(19520, 2 * CMP * P).rearrange("p (k i m) -> p k i m", k=2, i=CMP)
        XC = [hT[:, :, :].rearrange("p a b -> p (a b)")[:, n * 2 * PAST:(n + 1) * 2 * PAST].rearrange(
            "p (k n) -> p k n", k=2) for n in range(2)]
        KC, VC = reg(27712, NB + 1, P), reg(28864, NB + 1, P)
        W2, PE_T, HID = reg(30016, 2, P), reg(30528, 2, CMP), reg(30272, 2, P)
        PB = reg(30592, 2)
        PEB = reg(30600, 2, P)
        QB = reg(30016, NB, NB * HB)
        KW = hT[:, :, :].rearrange("p a b -> p (a b)")[:, 0:NB * WIN].rearrange("p (b n) -> p b n", b=NB)
        VW = hT[:, :, :].rearrange("p a b -> p (a b)")[:, NB * WIN:2 * NB * WIN].rearrange(
            "p (b t n) -> p b t n", b=NB, t=WIN // P)
        KB = [reg(19520 + n * PAST, PAST) for n in range(2)]
        VB = [reg(23616 + n * PAST, NPG, P) for n in range(2)]
        TRI, TA, TB = (reg(23616 + n * 1089, NBLK, NBLK)[0:64] for n in range(3))
        SX, SB = reg(15416, PAST + 1)[0:64], reg(17465, PAST + 1)[0:64]
        PTS, PTW = reg(17465, NPG, 64), reg(27712, WIN // P, 64)
        SW = reg(31214, WIN + 1)[0:64]
        PC, PCG = reg(30600, P)[0:64], reg(31086, P)[0:64]
        IT, PCT = reg(30728, 64), reg(30792, 64)
        SCO, RANK, SELB = (reg(30856 + n * NBLK, NBLK)[0:64] for n in range(3))
        GS, NM, DS, RI = (reg(30956 + 3 * n, 3)[0:64] for n in range(4))
        T8 = reg(30968, 2, NB)[0:64]
        G24 = reg(30984, 3 * HB)[0:64]
        OB, OB2 = reg(31008, 64), reg(27968, 2, 64)
        PN = reg(31728, 2, 64)[0:NB]
        HF = HM[:, :, :].rearrange("p a b -> p (a b)")
        BW, CSN = HF[0:64, 0:WIN + 1], HF[:, WIN + 1:WIN + 1 + 330]
        SAME, COVER, BC = CSN[0:64, 0:64], CSN[0:NCS, 64:97], CSN[0:64, 97:97 + NCS]
        B8, B8T, H24 = CSN[0:64, 224:232], CSN[0:NB, 232:296], CSN[0:64, 296:320]
        NSL, VALID = CSN[:, 320:328], CSN[:, 328:329]
        TAB, TABC = reg(15416, T + 640), reg(17080, NC, 64)
        SS = reg(17592, 3, 1792)
        PT = reg(22968, 2, 14 * P)
        NG, DG, RG = (reg(26552 + 9 * n, 3, 3) for n in range(3))
        U = [reg(WK + n * WKW, WKW) for n in range(2)]
        Y = [reg(WK + (2 + n) * WKW, TT) for n in range(2)]
        o = WK + 4 * WKW
        FS = reg(o, 2 * KF, 2, NB)
        FW = reg(o + 704, 2 * KF, 3)
        FO = reg(o + 836, 2 * KF, 2 * (NB + 1))
        CSS = reg(o + 1628, KD, 2, NB)
        CSW = reg(o + 1756, KD, 3)
        CO = reg(o + 1780, KD, 2 * (NB + 1))
        SQ = [reg(WK + n * WKW + 2, TT) for n in range(2)]
        FWD = reg(31668, 2 * KF)

        def halves(v):
            return v.bitcast(F16)

        H2 = halves(hT[:, :, :].rearrange("p a b -> p (a b)")).rearrange("p (k s n) -> p k s n", s=2, n=TT)
        Z2 = halves(reg(0, KF * TT)).rearrange("p (k s n) -> p k s n", s=2, n=TT)
        W2H = halves(reg(28852, 2 * WCH)).rearrange("p (w s n) -> p w s n", w=2, s=2)
        HN = reg(0, KD, TT)
        ACC, RS = reg(WK + 2 * WKW, TT), reg(WK + 3 * WKW, TT)

        x_in = [sem(f"x_in{k}") for k in range(KD)]
        c_in = sem("c_in")
        w_in = [sem(f"w_in{n}") for n in range(2)]
        ps_full = sem("ps_full")
        ps_free = [sem(f"ps_free{n}") for n in range(2)]
        ms_here = sem("ms_here")
        rs_here = sem("rs_here")
        sq_here = sem("sq_here")
        acc_here = sem("acc_here")
        h_here = sem("h_here")
        lb_exp = sem("lb_exp")
        lb_sum = sem("lb_sum")
        f_here = sem("f_here")
        k_here = sem("k_here")
        la_here = sem("la_here")
        a_here = sem("a_here")
        diff_here = sem("diff_here")
        exp_here = sem("exp_here")
        g_here = sem("g_here")
        sl_in = sem("sl_in")
        vm_here = sem("vm_here")
        sn_here = sem("sn_here")
        so_here = sem("so_here")
        at_here = sem("at_here")
        oc_here = sem("oc_here")
        s_here = sem("s_here")
        ot_here = sem("ot_here")
        ot_sq = sem("ot_sq")
        mix_here = sem("mix_here")
        sn_out = sem("sn_out")
        s_out = sem("s_out")
        half_used = sem("half_used")
        nat_out = sem("nat_out")
        snat_out = sem("snat_out")
        w1_zero = sem("w1_zero")
        w1_in = sem("w1_in")
        xc_in = [sem(f"xc_in{n}") for n in range(2)]
        xc_sw = [sem(f"xc_sw{n}") for n in range(2)]
        vec_in = sem("vec_in")
        win_in = sem("win_in")
        bias_in = sem("bias_in")
        tri_in = sem("tri_in")
        qb_zero = sem("qb_zero")
        qb_here = sem("qb_here")
        sx_max = sem("sx_max")
        sx_exp = sem("sx_exp")
        pc_here = sem("pc_here")
        kb_in = [sem(f"kb_in{n}") for n in range(2)]
        kb_sw = [sem(f"kb_sw{n}") for n in range(2)]
        kb_used = sem("kb_used")
        vb_in = [sem(f"vb_in{n}") for n in range(2)]
        vb_sw = [sem(f"vb_sw{n}") for n in range(2)]
        vb_used = sem("vb_used")
        rank_done = sem("rank_done")
        sp_here = sem("sp_here")
        win_copied = sem("win_copied")
        tab_in = sem("tab_in")
        sc_full = sem("sc_full")
        sc_free = sem("sc_free")
        mx_here = sem("mx_here")
        ex_here = sem("ex_here")
        rg_here = sem("rg_here")
        t_full = sem("t_full")
        t_free = sem("t_free")
        pv_full = sem("pv_full")
        pv_free = sem("pv_free")
        ptw_full = sem("ptw_full")
        ptw_here = sem("ptw_here")
        ob_here = sem("ob_here")
        rd_here = sem("rd_here")
        pw_here = sem("pw_here")
        up_in = sem("up_in")
        y_here = sem("y_here")
        silu_here = sem("silu_here")
        z_here = sem("z_here")
        u_here = sem("u_here")
        st_here = sem("st_here")
        out_y = sem("out_y")
        out_st = sem("out_st")
        pb_here = sem("pb_here")
        peb_here = sem("peb_here")
        sw_here = sem("sw_here")
        wh_here = sem("wh_here")
        w_split = sem("w_split")
        t_here = sem("t_here")
        hi_here = sem("hi_here")
        lo_even = sem("lo_even")
        lo_odd = sem("lo_odd")
        mix_hi = sem("mix_hi")
        mix_hb = sem("mix_hb")
        mix_a = sem("mix_a")
        mix_b = sem("mix_b")
        zm_here = sem("zm_here")
        zhi_here = sem("zhi_here")
        cy_here = sem("cy_here")
        cy_hi = sem("cy_hi")
        fwd_here = sem("fwd_here")
        dve_done = sem("dve_done")

        def bank(u):
            return PS[:, 3 * (u % 2):3 * (u % 2) + 3, :]

        def wide(u):
            return bank(u)[:, :, 0:TW]

        def three(v):
            return v.rearrange("p (n m) -> p n m", n=TN)

        def wait_full(e, u, i=None, per=0):
            e.wait_ge(ps_full, at(i, per, u - 1))

        def wait_free(e, u, i=None, per=0):
            e.wait_ge(ps_free[u % 2], at(i, per // 2, u // 2))

        def wait_emptied(e, u, i=None, per=0):
            wait_free(e, u + 2, i, per)

        block = ctx.enter_context(nc.Block())
        U_N0, _ = PLAN["norm0"]
        U_H, W_H = PLAN["heads"]
        HP2, HT2 = 2 * HEAD_PS, 2 * HEAD_TILES
        U_KV, W_KV = PLAN["kv"]
        U_G, _ = PLAN["gates"]
        U_C, _ = PLAN["squeeze"]
        U_S, _ = PLAN["sample"]
        _, W_M = PLAN["mix_out"]
        kv_tile = [U_KV] + [U_KV + 2 * n - 1 for n in range(1, 6)]
        kv_turn = [U_KV + 2 * n + 2 for n in range(5)] + [U_KV + 11]
        groups = [-(-(i + 1 + min(i + 1, 5) + 1) // 4) for i in range(NC)]

        def blocks(i):
            wide_ones = ([("slc", t, (NC - 1 - i + t) * P) for t in range(i + 1)]
                         + [("win", t, T + (4 - i + t) * P) for t in range(max(0, i - 4), i + 1)])
            return wide_ones[:1] + [("cmp", 0, T + 640)] + wide_ones[1:]

        units = [(i, j, half) for i in range(NC) for j in range(HA) for half in range(2)]
        TURN_BANKS = (4, 5, 7)
        group_at = [0]
        for i, _, _ in units:
            group_at.append(group_at[-1] + groups[i])

        def attention(ahead, first, second):
            for n in range(ahead):
                first(n, *units[n])
            for n in range(len(units)):
                if n + ahead < len(units):
                    first(n + ahead, *units[n + ahead])
                second(n, *units[n])

        def spans(i):
            return ((1, slice((NC - 1 - i) * P, T)), (2, slice(T + (4 - min(i, 4)) * P, T + 640)),
                    (0, slice(T + 640, T + 640 + NCP)))

        def pages_of(engine, part, first, what, dst, signal, free):
            pages = [engine.value_load(pg[0:1, ds(first + n, 1)], min_val=0, max_val=NPOOL - 1) for n in part]
            free()
            for n, page in zip(part, pages):
                src = what[ds(page, 1)]
                src = src.rearrange("a p b -> p a b" if len(what.shape) == 3 else "a p k b -> p (a k) b")
                engine.dma_start(dst(n), src).then_inc(signal, 16)

        def cmp_page(engine, part, signals, i, b):
            pages_of(engine, part, i * (2 * NPG) + b * NPG, cmp_t, lambda j: XC[b][:, :, j * P:(j + 1) * P], signals[b],
                     lambda: wait_full(engine, U_C - 2 + 2 * b, i, 4))

        def key_page(engine, part, signals, i, b):
            pages_of(engine, part, i * (2 * NPG) + b * NPG, slc_kt,
                     lambda j: KB[b].unsqueeze(1)[:, :, j * P:(j + 1) * P], signals[b],
                     lambda: engine.wait_ge(kb_used, at(i, 2, b + 1)))

        def value_page(engine, part, signals, i, b):
            pages_of(engine, part, i * (2 * NPG) + b * NPG, slc_v, lambda j: VB[b][:, j:j + 1, :], signals[b],
                     lambda: engine.wait_ge(vb_used, at(i, 2, b + 1)))

        SP_PART, ACT_PART, POOL_PART = range(0, 5), range(5, 10), range(10, NPG)
        HW_PAGES = 16 * (len(SP_PART) + len(ACT_PART))
        SW_PAGES = 16 * len(POOL_PART)

        def samples(engine, load, part, signals, turns=(0, NB // 2)):
            with engine.Fori(0, turns[1] - turns[0]) as i:
                for b in range(2):
                    load(engine, part, signals, i + turns[0], b)

        STEP, at_step = {}, 0
        for name, steps in (("mix_out", KD), ("up0", 2 * KF), ("down0", 2 * KD), ("conv_in", 3 * KD), ("conv_out", KD),
                            ("up1", 2 * KF), ("down1", 2 * KD)):
            STEP[name] = at_step
            at_step += steps

        def split_high(act, c, i=None, per=0, width=D):
            n = c % 2
            act.wait_ge(w_in[n], at(i, 8 * per, 16 * ((W_M + c) // 2 + 1)))
            act.activation(W2H[:, n, 0, 0:width], W[:, n, 0:width], ACT.Copy, scale=UNIT).then_inc(wh_here, 1)

        def split_low(dve, c, i=None, per=0, width=D):
            n = c % 2
            dve.wait_ge(wh_here, at(i, per, c + 1))
            dve.scalar_tensor_tensor(W2H[:, n, 1, 0:width], W[:, n, 0:width], UNIT, W2H[:, n, 0, 0:width],
                                     ALU.mult, ALU.subtract).then_inc(w_split, 1)

        @block.sync
        def _(sp):
            for k in range(KD):
                sp.dma_start(xT[:, k, :], x[:, k, :]).then_inc(x_in[k], 16)
            sp.dma_start(cs[:, :, :], cst).then_inc(c_in, 16)
            sp.dma_start(sm[:, :], small).then_inc(c_in, 16)
            sp.dma_start(HM[:, :, :], hmask).then_inc(c_in, 16)
            sp.dma_start(WG[:, :, :], wgate).then_inc(c_in, 16)
            sp.dma_start(pg[:, :], pages).then_inc(c_in, 16)
            for w in range(2):
                sp.dma_start(W[:, w, 0:D], wk8[w]).then_inc(w_in[w], 16)
            with sp.Fori(0, HA // 2) as i:
                for hh in range(2):
                    for k in range(HEAD_TILES):
                        w = W_H + hh * HEAD_TILES + k
                        wait_full(sp, U_H + hh * HEAD_PS + k, i, HP2)
                        sp.dma_start(W[:, w % 2, 0:D].unsqueeze(1),
                                     wk8[ds(i * HT2 + (w + 2), 1)].rearrange("a p n -> p a n")
                                     ).then_inc(w_in[w % 2], 16)
            for n in range(6):
                wait_full(sp, kv_tile[n])
                sp.dma_start(W[:, n % 2, 0:D], wk8[W_KV + n + 2]).then_inc(w_in[n % 2], 16)
            sp.wait_ge(w1_zero, 1)
            sp.wait_ge(s_out, 16 * (HA + 1))
            w1f = W1.rearrange("p k i m -> p (k i) m")
            for n in range(2):
                sp.dma_start(w1f[64 * n:64 * n + 64, :, 64 * n:64 * n + 64], w1).then_inc(w1_in, 16)
                sp.dma_start(W2[64 * n:64 * n + 64, :, 64 * n:64 * n + 64], w2).then_inc(w1_in, 16)
                sp.dma_start(PE_T[64 * n:64 * n + 64], pe_t).then_inc(w1_in, 16)

            sp.wait_ge(c_in, 16 * 5)
            wait_full(sp, U_G)
            sp.wait_ge(mix_here, HA)
            sp.dma_start(CSN, csn).then_inc(vec_in, 16)
            sp.dma_start(BW, bias_w).then_inc(vec_in, 16)
            samples(sp, cmp_page, SP_PART, xc_in)
            wait_full(sp, U_S - 1)
            sp.dma_start(KW, win_kt).then_inc(win_in, 16)
            sp.dma_start(VW, win_v).then_inc(win_in, 16)
            sp.wait_ge(nat_out, 16 * 6)
            sp.dma_start(SB, bias_s).then_inc(bias_in, 16)
            sp.dma_start(TRI, tri).then_inc(tri_in, 16)
            samples(sp, key_page, SP_PART, kb_in)
            sp.wait_ge(rank_done, 1)
            samples(sp, value_page, SP_PART, vb_in)
            wait_full(sp, U_S + 7)
            sp.dma_start(TAB, table).then_inc(tab_in, 16)
            sp.dma_start(TABC, table_c).then_inc(tab_in, 16)
            sp.wait_ge(pv_full, len(units))

            def after_tiles(name, index, following):
                c, n = STEP[name], PLAN_N[name]
                with sp.Fori(0, n // 2 - 1) as i:
                    for k in range(2):
                        sp.wait_ge(w_split, at(i, 2, c + k + 1))
                        sp.dma_start(W[:, k, 0:D].unsqueeze(1),
                                     wk8[ds(i * 2 + (index + 2 + k), 1)].rearrange("a p n -> p a n")
                                     ).then_inc(w_in[k], 16)
                for k in range(2):
                    sp.wait_ge(w_split, c + n - 2 + k + 1)
                    sp.dma_start(W[:, k, 0:following.shape[2]], following[k]).then_inc(w_in[k], 16)

            def after_down(name, chunks, following):
                c = STEP[name]
                with sp.Fori(0, KD - 1) as i:
                    for k in range(2):
                        sp.wait_ge(w_split, at(i, 2, c + k + 1))
                        sp.dma_start(W[:, k, :].unsqueeze(1), chunks[ds(i * 2 + 2 + k, 1)].rearrange("a p n -> p a n")
                                     ).then_inc(w_in[k], 16)
                if following is not None:
                    for k in range(2):
                        sp.wait_ge(w_split, c + 2 * KD - 1 + k)
                        sp.dma_start(W[:, k, 0:D], following[k]).then_inc(w_in[k], 16)

            def states(layer):
                sp.dma_start(FS, s_ff[layer]).then_inc(up_in, 16)
                sp.dma_start(FW, w_ff[layer]).then_inc(up_in, 16)

            states(0)
            sp.dma_start(CSS, s_sc).then_inc(up_in, 16)
            sp.dma_start(CSW, w_sc).then_inc(up_in, 16)
            i8 = PLAN["mix_out"][1]
            after_tiles("mix_out", i8, wk8[i8 + KD:i8 + KD + 2])
            i8 += KD
            after_tiles("up0", i8, wdn[0, 0:2])
            sp.wait_ge(st_here, 2 + 2 * KF)
            sp.dma_start(o_ff[0], FO).then_inc(out_st, 16)
            i8 += 2 * KF
            after_down("down0", wdn[0], wk8[i8:i8 + 2])
            sp.wait_ge(out_st, 16)
            states(1)
            after_tiles("conv_in", i8, wk8[i8 + 3 * KD:i8 + 3 * KD + 2])
            i8 += 3 * KD
            sp.wait_ge(st_here, 2 + 2 * KF + KD)
            sp.dma_start(o_sc, CO).then_inc(out_st, 16)
            after_tiles("conv_out", i8, wk8[i8 + KD:i8 + KD + 2])
            i8 += KD
            after_tiles("up1", i8, wdn[1, 0:2])
            sp.wait_ge(st_here, 2 + 4 * KF + KD)
            sp.dma_start(o_ff[1], FO).then_inc(out_st, 16)
            after_down("down1", wdn[1], None)
            for k in range(KD):
                sp.wait_ge(h_here, KD + k + 1)
                sp.dma_start(o_y[:, k, :], hT[:, k, :]).then_inc(out_y, 16)
            sp.wait_ge(out_y, 16 * KD)
            sp.wait_ge(out_st, 16 * 3)
            sp.wait_ge(nat_out, 16 * 6)
            sp.wait_ge(snat_out, 16 * 6)
            sp.wait_ge(win_copied, 16)
            sp.wait_ge(sn_out, 16 * 5)
            sp.wait_ge(s_out, 16 * 5)

        @block.gpsimd
        def _(pool):
            pool.memset(eps[:, 0:1], EPS).then_inc(ps_free[0], 1)
            pool.memset(eps[:, 1:2], 0.0).then_inc(ps_free[1], 1)
            pool.memset(eps[:, 2:3], 0.0).then_inc(acc_here, 2)
            pool.memset(eps[:, 3:4], 0.0).then_inc(sn_out, 16)
            pool.memset(eps[:, 4:5], 0.0).then_inc(s_out, 16)
            pool.memset(eps[:, 5:6], 0.0).then_inc(st_here, 2)
            pool.memset(eps[:, 6:7], 0.0).then_inc(z_here, 1)
            pool.memset(eps[:, 7:8], 0.0).then_inc(cy_here, 1)
            pool.memset(eps[:, 8:9], 0.0).then_inc(kb_used, 2)
            pool.memset(eps[:, 9:10], 0.0).then_inc(vb_used, 2)
            with pool.Fori(0, HA // 2) as i:
                for hh in range(2):
                    u = U_H + hh * HEAD_PS
                    h = i * 2 + hh
                    pool.dma_start(SL, s_hgrn[:, ds(h, 1)].rearrange("b a k v -> k (b a) v")).then_inc(sl_in, 16)
                    pool.wait_ge(f_here, at(i, 2, hh + 1))
                    pool.tensor_tensor(KT, ones[:, 0:1].to_broadcast([P, TT]), FT, ALU.subtract).then_inc(k_here, 1)
                    pool.wait_ge(k_here, at(i, 2, hh + 1))
                    wait_emptied(pool, u + 1, i, HP2)
                    for lev in range(LEV):
                        g = G[:, lev, :].rearrange("p (n t m) -> p n t m", t=2, m=1 << lev)
                        q = QT[:, 0:T].rearrange("p (n t m) -> p n t m", t=2, m=1 << lev)
                        k = KT[:, 0:T].rearrange("p (n t m) -> p n t m", t=2, m=1 << lev)
                        pool.wait_ge(exp_here, at(i, 2 * (LEV + 2), hh * (LEV + 2) + lev + 2))
                        pool.tensor_tensor(g[:, :, 0, :], g[:, :, 0, :], k[:, :, 0, :], ALU.mult)
                        pool.tensor_tensor(g[:, :, 1, :], g[:, :, 1, :], q[:, :, 1, :], ALU.mult).then_inc(g_here, 1)
                    pool.wait_ge(s_here, at(i, 2 * (NC + 1), hh * (NC + 1) + 1))
                    pool.tensor_tensor(QE, QE, QT[:, 0:T], ALU.mult)
                    pool.wait_ge(exp_here, at(i, 2 * (LEV + 2), (hh + 1) * (LEV + 2)))
                    pool.tensor_tensor(KE, KE, KT[:, 0:T], ALU.mult).then_inc(g_here, 1)
                    pool.wait_ge(sn_here, at(i, 2, hh + 1))

            pool.dma_start(o_win_s[:, 0:WIN - 1], state_win[:, 1:WIN]).then_inc(win_copied, 16)
            pool.wait_ge(mix_here, HA)
            pool.wait_ge(s_out, 16 * (HA + 1))
            pool.memset(W2, 0.0)
            pool.memset(W1, 0.0).then_inc(w1_zero, 1)
            pool.wait_ge(c_in, 16 * 5)
            wait_full(pool, U_G)
            samples(pool, cmp_page, POOL_PART, xc_sw)
            wait_full(pool, U_S - 1)
            pool.memset(QB, 0.0).then_inc(qb_zero, 1)
            samples(pool, key_page, POOL_PART, kb_sw)
            pool.wait_ge(rank_done, 1)
            samples(pool, value_page, POOL_PART, vb_sw)

            wait_full(pool, U_S + 7)
            for k in range(HA):
                pool.tensor_copy(H2[:, k, 0, :], mix[:, k, :]).then_inc(mix_hi, 1)
                pool.wait_ge(mix_hi, k + 1)
                pool.tensor_tensor(H2[:, k, 1, :], mix[:, k, :], H2[:, k, 0, :], ALU.subtract).then_inc(mix_a, 1)

            def ffn_rows(tiles, pairs):
                with pool.Fori(0, KF // 2) as i:
                    for p in range(2):
                        for n in range(2):
                            k = 2 * p + n
                            t = i * 4 + k
                            pool.wait_ge(u_here, at(i, 4, tiles + k + 1))
                            o18 = FO[:, ds(t, 1), :]
                            smp = o18[:, :, 2:2 + 2 * NB].rearrange("p a (b r) -> p a b r", r=2)
                            pool.tensor_copy(o18[:, :, 0:2], U[n][:, T:T + 2].unsqueeze(1))
                            pool.tensor_copy(smp[:, :, :, 1], U[n][:, T + 2:T + 2 + NB].unsqueeze(1))
                            pool.tensor_copy(smp[:, :, :, 0], FS[:, ds(t, 1), 1, :]).then_inc(st_here, 1)
                        row = Z2[:, ds(i * 2 + p, 1), :, :]
                        pool.wait_ge(zhi_here, at(i, 2, pairs + p + 1))
                        pool.tensor_tensor(row[:, :, 1, :], Y[0].unsqueeze(1), row[:, :, 0, :], ALU.subtract
                                           ).then_inc(z_here, 1)

            def low_halves(norm):
                for k in range(1, KD, 2):
                    pool.wait_ge(hi_here, KD * (norm - 1) + k + 1)
                    pool.tensor_tensor(H2[:, k, 1, :], HN[:, k, :], H2[:, k, 0, :], ALU.subtract).then_inc(lo_odd, 1)

            pool.wait_ge(up_in, 16 * 4)
            low_halves(1)
            ffn_rows(0, 0)
            low_halves(2)
            with pool.Fori(0, KD // 2) as i:
                for n in range(2):
                    t = i * 2 + n
                    pool.wait_ge(u_here, at(i, 2, 2 * KF + n + 1))
                    o18 = CO[:, ds(t, 1), :]
                    smp = o18[:, :, 2:2 + 2 * NB].rearrange("p a (b r) -> p a b r", r=2)
                    pool.tensor_copy(o18[:, :, 0:2], U[n][:, T:T + 2].unsqueeze(1))
                    pool.tensor_copy(smp[:, :, :, 1], U[n][:, T + 2:T + 2 + NB].unsqueeze(1))
                    pool.tensor_copy(smp[:, :, :, 0], CSS[:, ds(t, 1), 1, :]).then_inc(st_here, 1)
                    row = Z2[:, ds(t, 1), :, :]
                    pool.wait_ge(cy_hi, at(i, 2, n + 1))
                    pool.tensor_tensor(row[:, :, 1, :], Y[1].unsqueeze(1), row[:, :, 0, :], ALU.subtract
                                       ).then_inc(cy_here, 1)
            pool.wait_ge(up_in, 16 * 6)
            low_halves(3)
            ffn_rows(2 * KF + KD, KF)

        @block.scalar
        def _(act):
            def roots(norm, u):
                for m in range(TN):
                    last = m == TN - 1
                    if last:
                        wait_full(act, u)
                    else:
                        act.wait_ge(ms_here, (TN - 1) * norm + m + 1)
                    act.activation(three(RS)[:, m, :], wide(u)[:, m, :], ACT.Sqrt, bias=eps[:, 0:1]
                                   ).then_inc(ps_free[u % 2] if last else rs_here, 1)

            act.wait_ge(lb_sum, 1)
            act.activation(lb[:, 1:3, :], lb[:, 1:3, :], ACT.Exp).then_inc(lb_exp, 1)
            for k in range(KD):
                act.wait_ge(x_in[k], 16)
                act.wait_ge(acc_here, k + 1)
                act.activation(SQ[k % 2], xT[:, k, :], ACT.Square).then_inc(sq_here, 1)
            roots(0, U_N0)
            with act.Fori(0, HA // 2) as i:
                for hh in range(2):
                    u = U_H + hh * HEAD_PS
                    h = i * 2 + hh
                    wait_full(act, u, i, HP2)
                    act.activation(three(FT), wide(u), ACT.Sigmoid).then_inc(ps_free[u % 2], 1)
                    act.wait_ge(f_here, at(i, 2, hh + 1))
                    act.activation(AL, FT, ACT.Ln).then_inc(la_here, 1)
                    wait_full(act, u + 1, i, HP2)
                    act.activation(three(QT), wide(u + 1), ACT.Copy).then_inc(ps_free[(u + 1) % 2], 1)
                    act.wait_ge(a_here, at(i, 2 * NC, (hh + 1) * NC))
                    act.activation(QE, AL[:, 0:T], ACT.Exp).then_inc(exp_here, 1)
                    for lev in range(LEV):
                        act.wait_ge(diff_here, at(i, 2 * (LEV + 1), hh * (LEV + 1) + lev + 1))
                        act.activation(G[:, lev, :], G[:, lev, :], ACT.Exp).then_inc(exp_here, 1)
                    act.wait_ge(diff_here, at(i, 2 * (LEV + 1), (hh + 1) * (LEV + 1)))
                    act.activation(KE, KE, ACT.Exp).then_inc(exp_here, 1)
                    wait_full(act, u + 2, i, HP2)
                    act.activation(three(VT), wide(u + 2), ACT.Copy).then_inc(ps_free[u % 2], 1)
                    wait_full(act, u + 3, i, HP2)
                    act.activation(three(mix[:, ds(h, 1), :].rearrange("p a n -> p (a n)")), wide(u + 3), ACT.Sigmoid
                                   ).then_inc(ps_free[(u + 1) % 2], 1)
                    wait_full(act, u + 4, i, HP2)
                    act.activation(three(mix[:, ds(h + HA, 1), :].rearrange("p a n -> p (a n)")), wide(u + 4), ACT.Copy,
                                   scale=HD ** -0.5).then_inc(ps_free[u % 2], 1)
                    wait_full(act, u + 5, i, HP2)
                    v = bank(u + 5)
                    for n in range(2):
                        act.activation(VH[:, 4 * n:4 * n + 4, :], v[:, n, :].rearrange("p (a b) -> p a b", b=P), ACT.Copy)
                    act.activation(VH[0:NB, NC:NC + 2, :], v[0:NB, 2, 0:2 * P].rearrange("p (a b) -> p a b", b=P),
                                   ACT.Copy).then_inc(ps_free[(u + 1) % 2], 1)
                    act.wait_ge(sn_here, at(i, 2, hh + 1))
                    act.dma_start(o_hgrn_s[:, ds(h, 1)].rearrange("b a k v -> k (b a) v"), SN).then_inc(sn_out, 16)
                    for c in range(NC):
                        act.wait_ge(oc_here, at(i, 2 * NC, hh * NC + c + 1))
                        act.activation(OT[:, c * P:(c + 1) * P], PS[:, 6, 0:P], ACT.Copy).then_inc(ot_here, 1)
                    act.wait_ge(s_here, at(i, 2 * (NC + 1), (hh + 1) * (NC + 1)))
                    act.dma_start(o_hgrn_p[ds(h, 1)].rearrange("a k v -> k a v"), S.unsqueeze(1)).then_inc(s_out, 16)
                    wait_emptied(act, u + 14, i, HP2)
                    act.wait_ge(ot_here, at(i, 2 * NC, (hh + 1) * NC))
                    act.activation(G[:, 0, 0:T], OT[:, 0:T], ACT.Square)
                    act.activation(G[:, 1, 0:NB], OT[:, T:TT], ACT.Square).then_inc(ot_sq, 1)
                    wait_full(act, u + 15, i, HP2)
                    act.activation(G[:, 2, :], bank(u + 15)[:, 0:2, :].rearrange("p a b -> p (a b)"), ACT.Sqrt,
                                   bias=eps[:, 0:1])
                    act.activation(G[:, 3, 0:NB], bank(u + 15)[:, 2, 0:NB], ACT.Sqrt,
                                   bias=eps[:, 0:1]).then_inc(ps_free[(u + 1) % 2], 1)

            act.wait_ge(sn_out, 16 * (HA + 1))
            kv_out = (o_cmp_p[:, 0], o_cmp_p[:, 1], o_slc_p[:, 0], o_slc_p[:, 1], o_win_p[:, 0], o_win_p[:, 1])
            kv_out_s = (o_cmp_s[:, 0], o_cmp_s[:, 1], o_slc_s[:, 0], o_slc_s[:, 1], o_win_s[:, WIN - 1, 0],
                        o_win_s[:, WIN - 1, 1])
            held = (KVT[:, 0, :], KVT[:, 1, :], KVT[:, 2, :], VX, KVT[:, 3, :], VX)
            turned = (NAT[:, 0], NAT[:, 1], NAT[:, 2], VSL.rearrange("p a b -> p (a b)"), NAT[:, 3],
                      VWN.rearrange("p a b -> p (a b)"))

            def hold(n):
                wait_full(act, kv_tile[n])
                act.activation(three(held[n]), wide(kv_tile[n]), ACT.Copy).then_inc(ps_free[kv_tile[n] % 2], 1)

            def turn(n):
                u = kv_turn[n]
                wait_full(act, u)
                act.activation(turned[n], bank(u)[:, 0:2, :].rearrange("p a b -> p (a b)"), ACT.Copy)
                act.activation(SNT[0:NB, n, :], bank(u)[0:NB, 2, 0:P], ACT.Copy).then_inc(ps_free[u % 2], 1)
                wait_emptied(act, u)
                rows = turned[n].rearrange("p (c d) -> p c d", d=P)
                if n >= 4:
                    rows = rows[:, NC - WIN // P:]
                act.dma_start(kv_out[n].rearrange("(c p) d -> p c d", p=P), rows).then_inc(nat_out, 16)
                act.dma_start(kv_out_s[n], SNT[0:NB, n, :]).then_inc(snat_out, 16)

            hold(0)
            act.wait_ge(mix_here, HA)
            for n in range(1, 6):
                hold(n)
                turn(n - 1)
            turn(5)
            wait_full(act, U_G)
            act.activation(GT[:, 0:NC, :].rearrange("p a b -> p (a b)"), bank(U_G)[:, 0, 0:NC * 24], ACT.Sigmoid)
            act.activation(GT[0:NB, NC, :], bank(U_G)[0:NB, 0, NC * 24:(NC + 1) * 24], ACT.Sigmoid
                           ).then_inc(ps_free[U_G % 2], 1)

            def squeeze(n, u, i, per, cols):
                hid = bank(u)
                wait_full(act, u, i, per)
                if i is None:
                    act.activation(PB, hid[:, 2, 0:2], ACT.Copy).then_inc(pb_here, 1)
                    act.wait_ge(pb_here, 1)
                act.activation(HID[:, 0, 0:cols], hid[:, 0, 0:cols], ACT.Silu, bias=PB[:, 0:1])
                act.activation(HID[:, 1, 0:cols], hid[:, 1, 0:cols], ACT.Silu, bias=PB[:, 1:2]).then_inc(ps_free[u % 2], 1)
                wait_full(act, u + 1, i, per)
                kv = bank(u + 1)
                act.activation(KC[:, ds(n, 1), 0:cols], kv[:, 0:1, 0:cols], ACT.Copy)
                act.activation(VC[0:cols, ds(n, 1), :], kv[0:cols, 1:2, 0:P], ACT.Copy).then_inc(ps_free[(u + 1) % 2], 1)

            act.wait_ge(c_in, 16 * 5)
            cmp_page(act, ACT_PART, xc_in, 0, 0)
            squeeze(NB, U_C, None, 0, NCP)

            def squeeze_turn(i, last=False):
                cmp_page(act, ACT_PART, xc_in, i, 1)
                squeeze(i * 2, U_C + 2, i, 4, NCS)
                if not last:
                    cmp_page(act, ACT_PART, xc_in, i + 1, 0)
                squeeze(i * 2 + 1, U_C + 4, i, 4, NCS)

            with act.Fori(0, NB // 2 - 1) as i:
                squeeze_turn(i)
            squeeze_turn(NB // 2 - 1, last=True)

            def exponentials(n, row, c):
                act.wait_ge(sx_max, n)
                act.activation(row, row, ACT.Exp, bias=NM[:, c:c + 1], accum_out=DS[:, c:c + 1]).then_inc(sx_exp, 1)

            wait_full(act, U_S - 1)
            for b in range(2):
                key_page(act, ACT_PART, kb_in, 0, b)
            exponentials(1, PC[:, 0:NCS], 0)
            exponentials(2, SW, 2)
            samples(act, key_page, ACT_PART, kb_in, (1, NB // 2))
            act.wait_ge(rank_done, 1)
            for b in range(2):
                value_page(act, ACT_PART, vb_in, 0, b)
            exponentials(3, SX, 1)
            samples(act, value_page, ACT_PART, vb_in, (1, NB // 2))

            def first(n, i, j, half):
                act.wait_ge(mx_here, n + 1)
                for c, cols in spans(i):
                    part = SS[:, n % 3, cols]
                    ins = act.activation(part, part, ACT.Exp, bias=NG[:, n % 3, c:c + 1], accum_out=DG[:, n % 3, c:c + 1])
                ins.then_inc(ex_here, 1)

            def heads_out(pair):
                i, j = pair // HA, pair % HA
                act.wait_ge(pv_full, 2 * pair + 2)
                act.activation(mix[:, HA + j, i * P:(i + 1) * P], PS[:, 6, 0:P], ACT.Copy).then_inc(pv_free, 1)

            def second(n, i, j, half):
                if half == 0 and n:
                    heads_out(n // 2 - 1)
                for g in range(groups[i]):
                    m = len(blocks(i)[4 * g:4 * g + 4])
                    act.wait_ge(t_full, group_at[n] + g + 1)
                    act.activation(PT[:, half, 4 * g * P:(4 * g + m) * P],
                                   PS[:, TURN_BANKS[(group_at[n] + g) % 3], 0:m * P], ACT.Copy).then_inc(t_free, 1)

            act.wait_ge(ob_here, 1)
            attention(1, first, second)
            heads_out(len(units) // 2 - 1)

            for k in range(2):
                split_high(act, k)
            act.wait_ge(pv_free, HA * NC)
            for k in range(HA, 2 * HA):
                act.activation(H2[:, k, 0, :], mix[:, k, :], ACT.Copy).then_inc(mix_hb, 1)

            def squares(k, n, norm, i):
                act.wait_ge(acc_here, at(i, 2, KD * norm + n + 1))
                act.activation(SQ[n].unsqueeze(1), xT[:, ds(k, 1), :], ACT.Square).then_inc(sq_here, 1)

            def after_norm(norm):
                u = PLAN[f"norm{norm}"][0]
                roots(norm, u)
                if norm < 4:
                    for k in range(KD):
                        act.wait_ge(t_here, KD * (norm - 1) + k + 1)
                        act.activation(H2[:, k, 0, :], HN[:, k, :], ACT.Copy).then_inc(hi_here, 1)

            def stage_squares(name, norm, tiles):
                act.wait_ge(st_here, 2 + tiles)
                u, c = PLAN[name][0], STEP[name]
                with act.Fori(0, KD // 2) as i:
                    for n in range(2):
                        wait_full(act, u + n, i, 2)
                        split_high(act, c + n + 2, i, 2)
                        wait_emptied(act, u + n, i, 2)
                        squares(i * 2 + n, n, norm, i)
                after_norm(norm)

            def down_squares(name, norm, tiles, halves_before, last=False):
                act.wait_ge(st_here, 2 + tiles)
                u, c = PLAN[name][0], STEP[name]

                def turn(i, widths):
                    for n in range(2):
                        if widths[n]:
                            act.wait_ge(half_used, at(i, 2, halves_before + n + 1))
                            split_high(act, c + 2 * n + 2, i, 4, widths[n])
                            wait_full(act, u + n, i, 2)
                            split_high(act, c + 2 * n + 3, i, 4, widths[n])
                        wait_emptied(act, u + n, i, 2)
                        squares(i * 2 + n, n, norm, i)

                with act.Fori(0, KD // 2 - 1) as i:
                    turn(i, (WCH, WCH))
                turn(KD // 2 - 1, (WCH, None if last else D))
                after_norm(norm)

            def ffn_up(name, tiles, pairs):
                u, c = PLAN[name][0], STEP[name]

                def turn(i, widths):
                    for p in range(2):
                        for n in range(2):
                            k = 2 * p + n
                            t = u + k
                            wait_full(act, t, i, 4)
                            split_high(act, c + k + 2, i, 4, widths[p])
                            act.wait_ge(z_here, at(i, 2, pairs + p + 1))
                            act.wait_ge(st_here, at(i, 4, tiles + 2 * p + n + 1))
                            act.activation(three(U[n][:, 2:2 + TT]), wide(t), ACT.Copy, scale=1 / UNIT).then_inc(u_here, 1)
                            act.activation(three(Y[n]), wide(t), ACT.Copy, scale=FWD[:, ds(i * 4 + k, 1)]
                                           ).then_inc(ps_free[t % 2], 1)
                        act.wait_ge(y_here, at(i, 2, pairs + p + 1))
                        act.activation(Y[0], Y[0], ACT.Silu).then_inc(silu_here, 1)
                        act.wait_ge(zm_here, at(i, 2, pairs + p + 1))
                        act.activation(Z2[:, ds(i * 2 + p, 1), 0, :], Y[0].unsqueeze(1), ACT.Copy).then_inc(zhi_here, 1)

                with act.Fori(0, KF // 2 - 1) as i:
                    turn(i, (D, D))
                turn(KF // 2 - 1, (D, WCH))

            def last_tap(n, sent):
                act.wait_ge(up_in, 16 * sent)
                act.activation(FWD, FW[:, :, 2], ACT.Copy, scale=1 / UNIT).then_inc(fwd_here, 1)
                act.wait_ge(fwd_here, n)

            stage_squares("mix_out", 1, 0)
            last_tap(1, 4)
            ffn_up("up0", 0, 0)
            down_squares("down0", 2, 2 * KF, 0)
            u, c = PLAN["conv_in"][0], STEP["conv_in"]
            with act.Fori(0, KD // 2) as i:
                for n in range(2):
                    v = u + 3 * n
                    wait_full(act, v, i, 6)
                    split_high(act, c + 3 * n + 2, i, 6)
                    act.wait_ge(u_here, at(i, 2, 2 * KF + n))
                    act.activation(three(Y[0]), wide(v), ACT.Copy, scale=1 / UNIT).then_inc(ps_free[v % 2], 1)
                    wait_full(act, v + 1, i, 6)
                    split_high(act, c + 3 * n + 3, i, 6)
                    wait_full(act, v + 2, i, 6)
                    split_high(act, c + 3 * n + 4, i, 6)
                    wait_emptied(act, v + 2, i, 6)
                    act.activation(Z2[:, ds(i * 2 + n, 1), 0, :], Y[1].unsqueeze(1), ACT.Copy).then_inc(cy_hi, 1)
            stage_squares("conv_out", 3, 2 * KF + KD)
            last_tap(2, 6)
            ffn_up("up1", 2 * KF + KD, KF)
            down_squares("down1", 4, 4 * KF + KD, KD, last=True)

        @block.vector
        def _(dve):
            own = Chain(dve, dve_done)

            def one_over(norm, u):
                for m in range(TN):
                    if m == TN - 1:
                        wait_emptied(dve, u)
                    else:
                        dve.wait_ge(rs_here, (TN - 1) * norm + m + 1)
                    own.up(dve.reciprocal(three(RS)[:, m, :], three(RS)[:, m, :]))
                own.settle()

            dve.memset(ACC, 0.0).then_inc(dve_done, 1)
            own.k += 1
            dve.wait_ge(c_in, 16 * 5)
            lg = sm[:, NORMS * KD:NORMS * KD + 8].rearrange("p (a h) -> p a h", a=2)
            own.link(dve.tensor_tensor(lb[:, 0, :], lg[:, 0, :], lg[:, 1, :], ALU.max))
            dve.tensor_tensor(lb[:, 1, :], lg[:, 0, :], lb[:, 0, :], ALU.subtract)
            dve.tensor_tensor(lb[:, 2, :], lg[:, 1, :], lb[:, 0, :], ALU.subtract).then_inc(lb_sum, 1)
            dve.wait_ge(lb_exp, 1)
            own.link(dve.tensor_tensor(lb[:, 0, :], lb[:, 1, :], lb[:, 2, :], ALU.add))
            own.link(dve.reciprocal(lb[:, 0, :], lb[:, 0, :]))
            own.link(dve.tensor_tensor(lb[:, 3, :], lb[:, 1, :], lb[:, 0, :], ALU.mult))
            own.link(dve.tensor_scalar(lb[:, 4, :], lb[:, 3, :], -1.0, 1.0, ALU.mult, ALU.add))
            for k in range(KD):
                dve.wait_ge(sq_here, k + 1)
                dve.wait_ge(acc_here, k + 2)
                dve.tensor_tensor(ACC, ACC, SQ[k % 2], ALU.add).then_inc(acc_here, 1)
            one_over(0, U_N0)
            for k in range(KD):
                dve.scalar_tensor_tensor(hT[:, k, :], xT[:, k, :], sm[:, k:k + 1], RS, ALU.mult, ALU.mult
                                         ).then_inc(h_here, 1)
            with own.turns(HA // 2, 2 * 3) as i:
                for hh in range(2):
                    u = U_H + hh * HEAD_PS
                    h = i * 2 + hh
                    wait_emptied(dve, u, i, HP2)
                    dve.tensor_scalar(FT, FT, lb[:, 4, ds(h, 1)], lb[:, 3, ds(h, 1)], ALU.mult, ALU.add
                                      ).then_inc(f_here, 1)
                    dve.wait_ge(la_here, at(i, 2, hh + 1))
                    for c in range(NC):
                        a = AL[:, c * P:(c + 1) * P]
                        dve.tensor_tensor_scan(a, ones, a, 0.0, ALU.mult, ALU.add).then_inc(a_here, 1)
                    dve.wait_ge(a_here, at(i, 2 * NC, (hh + 1) * NC))
                    for lev in range(LEV):
                        m = 1 << lev
                        a = AL[:, 0:T].rearrange("p (n t m) -> p n t m", t=2, m=m)
                        g = G[:, lev, :].rearrange("p (n t m) -> p n t m", t=2, m=m)
                        mid = a[:, :, 0, m - 1:m].to_broadcast([P, T // (2 * m), m])
                        dve.tensor_tensor(g[:, :, 0, :], mid, a[:, :, 0, :], ALU.subtract)
                        dve.tensor_tensor(g[:, :, 1, :], a[:, :, 1, :], mid, ALU.subtract).then_inc(diff_here, 1)
                    a = AL[:, 0:T].rearrange("p (n m) -> p n m", m=P)
                    dve.tensor_tensor(KE.rearrange("p (n m) -> p n m", m=P), a[:, :, P - 1:P].to_broadcast([P, NC, P]),
                                      a, ALU.subtract).then_inc(diff_here, 1)
                    dve.wait_ge(exp_here, at(i, 2 * (LEV + 2), hh * (LEV + 2) + 1))
                    dve.tensor_copy(EE.unsqueeze(2), QE.rearrange("p (n m) -> p n m", m=P)[:, :, P - 1:P]
                                    ).then_inc(s_here, 1)
                    wait_emptied(dve, u + 5, i, HP2)
                    dve.tensor_tensor(VMs, VH[0:NB, NC:NC + 1, :].to_broadcast([NB, NB, P]),
                                      ident[0:NB, 0:NB].unsqueeze(2).to_broadcast([NB, NB, P]), ALU.mult
                                      ).then_inc(vm_here, 1)
                    wait_full(dve, u + 6, i, HP2)
                    dve.wait_ge(sl_in, at(i, 32, 16 * (hh + 1)))
                    dve.wait_ge(sn_out, at(i, 32, 16 * (hh + 1)))
                    ps = bank(u + 6)
                    for b in range(NB):
                        ins = dve.scalar_tensor_tensor(SN[:, b, :], SL[:, b, :], FT[:, T + b:T + b + 1],
                                                       ps[:, b // 4, (b % 4) * P:(b % 4 + 1) * P], ALU.mult, ALU.add)
                    ins.then_inc(sn_here, 1)
                    dve.wait_ge(so_here, at(i, 2, hh + 1))
                    dve.tensor_copy(OT[:, T:TT], ps[:, 2, 0:NB]).then_inc(ps_free[u % 2], 1)
                    def state(c):
                        new = PS[:, 7, 0:P]
                        dve.wait_ge(oc_here, at(i, 2 * NC, hh * NC + c + 1))
                        if c == 0:
                            dve.wait_ge(s_out, at(i, 32, 16 * (hh + 1)))
                            dve.tensor_copy(S, new).then_inc(s_here, 1)
                        else:
                            dve.wait_ge(s_here, at(i, 2 * (NC + 1), hh * (NC + 1) + c + 1))
                            dve.scalar_tensor_tensor(S, S, EE[:, c:c + 1], new, ALU.mult, ALU.add).then_inc(s_here, 1)

                    for c in range(NC):
                        uc = u + 7 + c
                        ps = bank(uc)
                        wait_full(dve, uc, i, HP2)
                        am = AM[:, c % 2, :]
                        dve.tensor_copy(KN[:, c % 2, :], ps[:, 2, 0:P])
                        dve.tensor_tensor(am, ps[:, 0:2, :].rearrange("p a b -> p (a b)"),
                                          HM[:, :, :].rearrange("p a b -> p (a b)"), ALU.mult
                                          ).then_inc(ps_free[uc % 2], 1)
                        wait_emptied(dve, uc, i, HP2)
                        dve.tensor_reduce(AT[:, c % 2, :], am.rearrange("p (l t) -> p t l", t=P), AX_X, ALU.add
                                          ).then_inc(at_here, 1)
                        if c:
                            state(c - 1)
                    state(NC - 1)
                    wait_emptied(dve, u + 15, i, HP2)
                    dve.reciprocal(G[:, 2, :], G[:, 2, :])
                    own.link(dve.reciprocal(G[:, 3, 0:NB], G[:, 3, 0:NB]))
                    gain = sm[:, ds(h + (NORMS * KD + 8), 1)]
                    own.up(dve.scalar_tensor_tensor(OT[:, 0:T], OT[:, 0:T], gain, G[:, 2, :], ALU.mult, ALU.mult))
                    own.link(dve.scalar_tensor_tensor(OT[:, T:TT], OT[:, T:TT], gain, G[:, 3, 0:NB], ALU.mult, ALU.mult))
                    m = mix[:, ds(h, 1), :].rearrange("p a n -> p (a n)")
                    dve.tensor_tensor(m, m, OT, ALU.mult).then_inc(mix_here, 1)

            dve.wait_ge(w1_in, 16 * 6)
            for k in range(2):
                own.up(dve.tensor_scalar(PEB[:, k, :], W1[:, k, 0, :], PE_T[:, k, 0:1], None, ALU.mult))
            for r in range(1, CMP):
                own.settle()
                for k in range(2):
                    ins = dve.scalar_tensor_tensor(PEB[:, k, :], W1[:, k, r, :], PE_T[:, k, r:r + 1], PEB[:, k, :],
                                                   ALU.mult, ALU.add)
                    if r < CMP - 1:
                        own.up(ins)
                    else:
                        ins.then_inc(peb_here, 1)

            wait_full(dve, U_S - 1)
            dve.wait_ge(qb_zero, 1)
            qf = QB.rearrange("p b c -> p (b c)")
            for half in range(2):
                rows = slice(64 * half, 64 * half + 64)
                for j in range(HA):
                    ins = dve.tensor_copy(qf[rows, j + 4 * half:j + 4 * half + 72 * (NB - 1) + 1:72],
                                          mix[rows, HA + j, T:TT])
            ins.then_inc(qb_here, 1)

            wait_full(dve, U_S)
            ps = bank(U_S)
            dve.tensor_tensor(G24, ps[0:64, 1, 0:24], H24, ALU.mult)
            dve.tensor_tensor(PC[:, 0:NCS], ps[0:64, 0, 0:NCS], BC, ALU.add).then_inc(ps_free[U_S % 2], 1)
            wait_emptied(dve, U_S)
            own.link(dve.tensor_reduce(GS, G24.rearrange("p (h c) -> p c h", c=3), AX_X, ALU.add))
            dve.tensor_reduce(NM[:, 0:1], PC[:, 0:NCS], AX_X, ALU.max, negate=True).then_inc(sx_max, 1)
            wait_full(dve, U_S + 1)
            ps = bank(U_S + 1)
            dve.wait_ge(vec_in, 32)
            dve.tensor_tensor(SW[:, 0:WIN], ps[0:64, 0, :], BW[:, 0:WIN], ALU.add)
            dve.tensor_tensor(SW[:, WIN:WIN + 1], ps[0:64, 1, 0:1], BW[:, WIN:WIN + 1], ALU.add
                              ).then_inc(ps_free[(U_S + 1) % 2], 1)
            wait_emptied(dve, U_S + 1)
            dve.tensor_reduce(NM[:, 2:3], SW, AX_X, ALU.max, negate=True).then_inc(sx_max, 1)
            dve.wait_ge(sx_exp, 1)
            own.link(dve.reciprocal(RI[:, 0:1], DS[:, 0:1]))
            dve.tensor_scalar(PC[:, 0:NCS], PC[:, 0:NCS], RI[:, 0:1], None, ALU.mult).then_inc(pc_here, 1)
            dve.wait_ge(pc_here, 1)
            dve.tensor_scalar(PCG[:, 0:NCS], PC[:, 0:NCS], GS[:, 0:1], None, ALU.mult).then_inc(pc_here, 1)
            wait_full(dve, U_S + 2)
            dve.tensor_copy(IT[0:NCS], bank(U_S + 2)[0:NCS, 0, 0:64]).then_inc(ps_free[U_S % 2], 1)
            dve.wait_ge(sx_exp, 2)
            own.link(dve.reciprocal(RI[:, 2:3], DS[:, 2:3]))
            dve.tensor_scalar(SW, SW, RI[:, 2:3], GS[:, 2:3], ALU.mult, ALU.mult).then_inc(sw_here, 1)
            wait_full(dve, U_S + 3)
            ps = bank(U_S + 3)
            dve.tensor_copy(SCO, ps[0:64, 0, 0:NBLK])
            dve.tensor_copy(PCT[0:NCS], ps[0:NCS, 1, 0:64]).then_inc(ps_free[(U_S + 3) % 2], 1)
            wait_emptied(dve, U_S + 3)
            own.link(dve.memset(SCO[:, 0:1], 1e9))
            own.link(dve.memset(SCO[:, NBLK - 2:NBLK], 1e9))
            dve.wait_ge(tri_in, 16)
            square = [64, NBLK, NBLK]
            other, mine = SCO.unsqueeze(1).to_broadcast(square), SCO.unsqueeze(2).to_broadcast(square)
            own.up(dve.tensor_tensor(TA, other, mine, ALU.is_gt))
            own.link(dve.tensor_tensor(TB, other, mine, ALU.is_equal))
            own.link(dve.tensor_tensor(TB, TB, TRI, ALU.mult))
            own.link(dve.tensor_tensor(TA, TA, TB, ALU.add))
            own.link(dve.tensor_reduce(RANK, TA, AX_X, ALU.add))
            dve.tensor_scalar(SELB, RANK, float(NSEL), -FAR, ALU.is_ge, ALU.mult).then_inc(rank_done, 1)
            dve.wait_ge(rank_done, 1)
            dve.wait_ge(bias_in, 16)
            sb3 = SB[:, 0:PAST].rearrange("p (b n) -> p b n", n=64)
            own.link(dve.tensor_tensor(sb3, sb3, SELB[:, 0:NBLK - 1].unsqueeze(2).to_broadcast([64, NBLK - 1, 64]), ALU.add))
            dve.wait_ge(ptw_full, 1)
            dve.tensor_copy(PTW.rearrange("p a b -> p (a b)"), PS[:, 7, 0:256]).then_inc(ptw_here, 1)
            wait_full(dve, U_S + 5)
            d, e = bank(U_S + 4), bank(U_S + 5)
            flat = "p a b -> p (a b)"
            dve.tensor_tensor(SX[:, PAST:PAST + 1], d[0:64, 2, 0:1], SB[:, PAST:PAST + 1], ALU.add)
            dve.tensor_tensor(SX[:, 0:1024], d[0:64, 0:2, :].rearrange(flat), SB[:, 0:1024], ALU.add
                              ).then_inc(ps_free[U_S % 2], 1)
            dve.tensor_tensor(SX[:, 1024:PAST], e[0:64, 0:2, :].rearrange(flat), SB[:, 1024:PAST], ALU.add
                              ).then_inc(ps_free[(U_S + 1) % 2], 1)
            wait_emptied(dve, U_S + 4)
            wait_emptied(dve, U_S + 5)
            dve.tensor_reduce(NM[:, 1:2], SX, AX_X, ALU.max, negate=True).then_inc(sx_max, 1)
            dve.wait_ge(sx_exp, 3)
            own.link(dve.reciprocal(RI[:, 1:2], DS[:, 1:2]))
            own.link(dve.tensor_scalar(SX, SX, RI[:, 1:2], GS[:, 1:2], ALU.mult, ALU.mult))
            dve.wait_ge(sw_here, 1)
            own.up(dve.tensor_scalar(T8[:, 0, :], B8, SX[:, PAST:PAST + 1], None, ALU.mult))
            dve.tensor_scalar(T8[:, 1, :], B8, SW[:, WIN:WIN + 1], None, ALU.mult).then_inc(sp_here, 1)
            wait_full(dve, U_S + 6)
            ps = bank(U_S + 6)
            dve.tensor_copy(PTS.rearrange(flat), ps[:, 0:2, :].rearrange(flat))
            dve.tensor_copy(PN.rearrange(flat), ps[0:NB, 2, 0:128]).then_inc(ps_free[U_S % 2], 1)
            wait_full(dve, U_S + 7)
            for part, src in ((0, PS[:, 6, 0:128]), (1, bank(U_S + 7)[:, 0, 0:192])):
                own.up(dve.tensor_reduce(OB2[:, part, :], src.rearrange("p (a c) -> p c a", c=64), AX_X, ALU.add))
            own.settle()
            own.link(dve.tensor_tensor(OB, OB2[:, 0, :], OB2[:, 1, :], ALU.add))
            ob = OB.rearrange("p (b h) -> p h b", h=HB)
            dve.tensor_copy(mix[0:64, HA:2 * HA, T:TT], ob[0:64, 0:HA, :])
            dve.tensor_copy(mix[64:128, HA:2 * HA, T:TT], ob[64:128, HA:2 * HA, :]).then_inc(ps_free[(U_S + 7) % 2], 1)
            wait_emptied(dve, U_S + 7)
            own.k += 1
            dve.memset(OB[:, 0:1], 0.0).then_inc(dve_done, 1)
            dve.memset(OB[:, 1:2], 0.0).then_inc(ob_here, 1)

            psf = PS[:, :, :].rearrange(flat)
            dve.wait_ge(tab_in, 32)

            def first(n, i, j, half):
                dve.wait_ge(sc_full, n + 1)
                if n >= 3:
                    dve.wait_ge(pv_full, n - 2)
                for c, cols in spans(i):
                    tab = TABC[:, i, 0:NCP] if c == 0 else TAB[:, cols]
                    ins = dve.scalar_tensor_tensor(SS[:, n % 3, cols], tab, NSL[:, j + 4 * half:j + 4 * half + 1],
                                                   psf[:, cols], ALU.mult, ALU.add)
                ins.then_inc(sc_free, 1)
                dve.wait_ge(sc_free, n + 1)
                for c, cols in spans(i):
                    ins = dve.tensor_reduce(NG[:, n % 3, c:c + 1], SS[:, n % 3, cols], AX_X, ALU.max, negate=True)
                ins.then_inc(mx_here, 1)

            def second(n, i, j, half):
                rg = RG[:, n % 3, :]
                dve.wait_ge(ex_here, n + 1)
                dve.reciprocal(rg, DG[:, n % 3, :]).then_inc(rd_here, 1)
                dve.wait_ge(rd_here, n + 1)
                h = j + 4 * half
                gate = GT[:, i, 3 * h:3 * h + 3]
                if i == 0:
                    dve.scalar_tensor_tensor(rg[:, 0:1], rg[:, 0:1], VALID, gate[:, 0:1], ALU.mult, ALU.mult)
                    dve.tensor_tensor(rg[:, 1:3], rg[:, 1:3], gate[:, 1:3], ALU.mult).then_inc(rg_here, 1)
                else:
                    dve.tensor_tensor(rg, rg, gate, ALU.mult).then_inc(rg_here, 1)
                dve.wait_ge(rg_here, n + 1)
                for c, cols in spans(i):
                    part = SS[:, n % 3, cols]
                    ins = dve.tensor_scalar(part, part, rg[:, c:c + 1], None, ALU.mult)
                ins.then_inc(pw_here, 1)

            attention(1, first, second)
            dve.wait_ge(pv_full, len(units))
            dve.wait_ge(nat_out, 16 * 6)
            dve.wait_ge(snat_out, 16 * 6)
            for n in range(2):
                own.up(dve.memset(U[n][:, 0:2], 0.0))
            own.settle()

            for k in range(2):
                split_low(dve, k)
            dve.wait_ge(mix_a, HA)
            for k in range(HA, 2 * HA):
                dve.wait_ge(mix_hb, k - HA + 1)
                dve.tensor_tensor(H2[:, k, 1, :], mix[:, k, :], H2[:, k, 0, :], ALU.subtract).then_inc(mix_b, 1)

            def add_tile(u, k, n, norm, i):
                wait_full(dve, u + n, i, 2)
                t = xT[:, ds(k, 1), :].rearrange("p a (n m) -> p (a n) m", n=TN)
                dve.scalar_tensor_tensor(t, wide(u + n), 1 / UNIT, t, ALU.mult, ALU.add).then_inc(ps_free[(u + n) % 2], 1)
                dve.wait_ge(sq_here, at(i, 2, KD * norm + n + 1))
                dve.wait_ge(acc_here, at(i, 2, KD * norm + n + 2))
                dve.tensor_tensor(ACC, ACC, SQ[n], ALU.add).then_inc(acc_here, 1)

            def normed(norm):
                one_over(norm, PLAN[f"norm{norm}"][0])
                for k in range(KD):
                    to = HN if norm < 4 else hT
                    dve.scalar_tensor_tensor(to[:, k, :], xT[:, k, :], sm[:, norm * KD + k:norm * KD + k + 1], RS,
                                             ALU.mult, ALU.mult).then_inc(t_here if norm < 4 else h_here, 1)
                    if norm < 4 and k % 2:
                        dve.wait_ge(hi_here, KD * (norm - 1) + k)
                        dve.tensor_tensor(H2[:, k - 1, 1, :], HN[:, k - 1, :], H2[:, k - 1, 0, :], ALU.subtract
                                          ).then_inc(lo_even, 1)

            def residual(name, norm):
                u, c = PLAN[name][0], STEP[name]
                own.link(dve.memset(ACC, 0.0))
                with dve.Fori(0, KD // 2) as i:
                    for n in range(2):
                        split_low(dve, c + n + 2, i, 2)
                        add_tile(u, i * 2 + n, n, norm, i)
                normed(norm)

            def down_residual(name, norm, last=False):
                u, c = PLAN[name][0], STEP[name]
                own.link(dve.memset(ACC, 0.0))

                def turn(i, widths):
                    for n in range(2):
                        if widths[n]:
                            for k in range(2):
                                split_low(dve, c + 2 * n + 2 + k, i, 4, widths[n])
                        add_tile(u, i * 2 + n, n, norm, i)

                with dve.Fori(0, KD // 2 - 1) as i:
                    turn(i, (WCH, WCH))
                turn(KD // 2 - 1, (WCH, None if last else D))
                normed(norm)

            def taps(y, row, old, weight, last=None):
                own.up(dve.scalar_tensor_tensor(y[:, 0:T], row[:, 1:1 + T], weight(1), y[:, 0:T], ALU.mult, ALU.add))
                own.link(dve.scalar_tensor_tensor(y[:, T:TT], old(1), weight(1), y[:, T:TT], ALU.mult, ALU.add))
                own.up(dve.scalar_tensor_tensor(y[:, 0:T], row[:, 0:T], weight(0), y[:, 0:T], ALU.mult, ALU.add))
                ins = dve.scalar_tensor_tensor(y[:, T:TT], old(0), weight(0), y[:, T:TT], ALU.mult, ALU.add)
                if last is None:
                    own.link(ins)
                else:
                    ins.then_inc(last, 1)

            def ffn_up(name, tiles, pairs):
                u, c = PLAN[name][0], STEP[name]

                def turn(i, widths):
                    for p in range(2):
                        for n in range(2):
                            t = 2 * p + n
                            split_low(dve, c + t + 2, i, 4, widths[p])
                            wait_emptied(dve, u + t, i, 4)
                            dve.wait_ge(u_here, at(i, 4, tiles + t + 1))
                            taps(Y[n], U[n], lambda r: FS[:, ds(i * 4 + t, 1), r, :].rearrange("p a b -> p (a b)"),
                                 lambda r: FW[:, ds(i * 4 + t, 1), r], None if n else y_here)
                        dve.wait_ge(silu_here, at(i, 2, pairs + p + 1))
                        dve.tensor_tensor(Y[0], Y[0], Y[1], ALU.mult).then_inc(zm_here, 1)

                with own.turns(KF // 2 - 1, 14) as i:
                    turn(i, (D, D))
                turn(KF // 2 - 1, (D, WCH))

            residual("mix_out", 1)
            ffn_up("up0", 0, 0)
            dve.wait_ge(z_here, 1 + KF)
            down_residual("down0", 2)
            u, c = PLAN["conv_in"][0], STEP["conv_in"]
            with own.turns(KD // 2, 8) as i:
                for n in range(2):
                    t = i * 2 + n
                    v = u + 3 * n
                    split_low(dve, c + 3 * n + 2, i, 6)
                    wait_full(dve, v + 1, i, 6)
                    wait_emptied(dve, v, i, 6)
                    dve.wait_ge(st_here, at(i, 2, 2 * KF + n + 1))
                    dve.scalar_tensor_tensor(three(U[n][:, 2:2 + TT]), wide(v + 1), 1 / UNIT, three(Y[0]),
                                             ALU.mult, ALU.mult).then_inc(u_here, 1)
                    split_low(dve, c + 3 * n + 3, i, 6)
                    dve.wait_ge(u_here, at(i, 2, 2 * KF + n + 1))
                    dve.wait_ge(cy_here, at(i, 2, n + 1))
                    dve.tensor_scalar(Y[1], U[n][:, 2:2 + TT], CSW[:, ds(t, 1), 2], None, ALU.mult
                                      ).then_inc(ps_free[(v + 1) % 2], 1)
                    wait_emptied(dve, v + 1, i, 6)
                    taps(Y[1], U[n], lambda r: CSS[:, ds(t, 1), r, :].rearrange("p a b -> p (a b)"),
                         lambda r: CSW[:, ds(t, 1), r])
                    split_low(dve, c + 3 * n + 4, i, 6)
                    wait_full(dve, v + 2, i, 6)
                    dve.scalar_tensor_tensor(three(Y[1]), wide(v + 2), 1 / UNIT, three(Y[1]), ALU.mult, ALU.mult
                                             ).then_inc(ps_free[v % 2], 1)
            dve.wait_ge(cy_here, 1 + KD)
            residual("conv_out", 3)
            ffn_up("up1", 2 * KF + KD, KF)
            dve.wait_ge(z_here, 1 + 2 * KF)
            down_residual("down1", 4, last=True)

        @block.tensor
        def _(pe):
            def norm(u, n):
                pe.wait_ge(c_in, 16 * 5)
                pe.wait_ge(acc_here, 2 + KD * (n + 1))
                wait_free(pe, u)
                for m in range(TN):
                    pe.matmul(wide(u)[:, m, :], mean_d, ACC[:, m * TW:(m + 1) * TW], start=True, stop=True
                              ).then_inc(ms_here if m < TN - 1 else ps_full, 1)

            def tile(u, w, src, i=None, up=0, wp=0, ready=0):
                wait_free(pe, u, i, up)
                pe.wait_ge(w_in[w % 2], at(i, 8 * wp, 16 * (w // 2 + 1)))
                for k in range(KD):
                    if ready:
                        pe.wait_ge(h_here, ready + k)
                    for m in range(TN):
                        ins = pe.matmul(wide(u)[:, m, :], W[:, w % 2, k * P:(k + 1) * P],
                                        src[:, k, m * TW:(m + 1) * TW], start=(k == 0), stop=(k == KD - 1))
                ins.then_inc(ps_full, 1)

            norm(U_N0, 0)
            with pe.Fori(0, HA // 2) as i:
                for hh in range(2):
                    u = U_H + hh * HEAD_PS
                    for k in range(HEAD_TILES):
                        tile(u + k, W_H + hh * HEAD_TILES + k, hT, i, HP2, HT2, ready=int(hh == k == 0))
                    wait_free(pe, u + 5, i, HP2)
                    wait_emptied(pe, u + 2, i, HP2)
                    pe.wait_ge(k_here, at(i, 2, hh + 1))
                    ps = bank(u + 5)
                    for c in range(NC):
                        pe.transpose(ps[:, c // 4, (c % 4) * P:(c % 4 + 1) * P], VT[:, c * P:(c + 1) * P], ident)
                    pe.transpose(ps[0:NB, 2, 0:P], VT[:, T:TT], ident)
                    pe.transpose(ps[0:NB, 2, P:2 * P], KT[:, T:TT], ident).then_inc(ps_full, 1)
                    wait_free(pe, u + 6, i, HP2)
                    pe.wait_ge(vm_here, at(i, 2, hh + 1))
                    pss = bank(u + 6)
                    for n in range(2):
                        ins = pe.matmul(pss[:, n, :], VH[0:NB, NC + 1, :], VMs[:, 4 * n:4 * n + 4, :],
                                        start=True, stop=True)
                    ins.then_inc(ps_full, 1)

                    def att(c):
                        uc = u + 7 + c
                        wait_free(pe, uc, i, HP2)
                        ps = bank(uc)
                        tok = slice(c * P, (c + 1) * P)
                        pe.matmul(ps[:, 0, 0:P], KT[:, tok], QT[:, tok], start=True, stop=True)
                        for lev in range(LEV):
                            n = lev + 1
                            pe.matmul(ps[:, n // 4, (n % 4) * P:(n % 4 + 1) * P], G[:, lev, tok], G[:, lev, tok],
                                      start=True, stop=True)
                        pe.transpose(ps[:, 2, 0:P], KE[:, tok], ident).then_inc(ps_full, 1)

                    pe.wait_ge(g_here, at(i, 2 * (LEV + 1), (hh + 1) * (LEV + 1)))
                    att(0)
                    pe.wait_ge(sn_here, at(i, 2, hh + 1))
                    for b in range(NB):
                        ins = pe.matmul(pss[:, 2, b:b + 1], SN[:, b, :], QT[:, T + b:T + b + 1], start=True, stop=True)
                    ins.then_inc(so_here, 1)
                    for c in range(NC):
                        if c + 1 < NC:
                            att(c + 1)
                        out = PS[:, 6, 0:P]
                        tok = slice(c * P, (c + 1) * P)
                        pe.wait_ge(at_here, at(i, 2 * NC, hh * NC + c + 1))
                        if c:
                            pe.wait_ge(ot_here, at(i, 2 * NC, hh * NC + c))
                        pe.matmul(out, VH[:, c, :], AT[:, c % 2, :], start=True, stop=(c == 0))
                        if c:
                            pe.wait_ge(s_here, at(i, 2 * (NC + 1), hh * (NC + 1) + c + 1))
                            pe.matmul(out, S, QE[:, tok], start=False, stop=True)
                        pe.matmul(PS[:, 7, 0:P], KN[:, c % 2, :], VH[:, c, :], start=True, stop=True
                                  ).then_inc(oc_here, 1)
                    wait_free(pe, u + 15, i, HP2)
                    pe.wait_ge(ot_sq, at(i, 2, hh + 1))
                    ps = bank(u + 15)
                    for n in range(2):
                        pe.matmul(ps[:, n, :], mean_v, G[:, 0, n * 512:(n + 1) * 512], start=True, stop=True)
                    pe.matmul(ps[:, 2, 0:NB], mean_v, G[:, 1, 0:NB], start=True, stop=True).then_inc(ps_full, 1)

            held = (KVT[:, 0, :], KVT[:, 1, :], KVT[:, 2, :], VX, KVT[:, 3, :], VX)

            def turn(n):
                u = kv_turn[n]
                wait_free(pe, u)
                wait_emptied(pe, kv_tile[n])
                ps = bank(u)
                for c in range(NC):
                    pe.transpose(ps[:, c // 4, (c % 4) * P:(c % 4 + 1) * P], held[n][:, c * P:(c + 1) * P], ident)
                pe.transpose(ps[0:NB, 2, 0:P], held[n][:, T:TT], ident).then_inc(ps_full, 1)

            tile(kv_tile[0], W_KV, hT)
            for n in range(1, 6):
                tile(kv_tile[n], W_KV + n, hT)
                turn(n - 1)
            turn(5)
            wait_free(pe, U_G)
            for c in range(NC + 1):
                tok = slice(c * P, min((c + 1) * P, TT))
                for k in range(KD):
                    ins = pe.matmul(bank(U_G)[0:min(P, TT - c * P), 0, c * 24:(c + 1) * 24], hT[:, k, tok], WG[:, k, :],
                                    start=(k == 0), stop=(k == KD - 1))
            ins.then_inc(ps_full, 1)

            def squeeze(u, i, per, cols, source):
                wait_free(pe, u, i, per)
                ps = bank(u)
                for k in range(2):
                    for r in range(CMP):
                        ins = pe.matmul(ps[:, k, 0:cols], W1[:, k, r, :], source(k, r), start=(r == 0), stop=(r == CMP - 1))
                if i is None:
                    pe.wait_ge(peb_here, 2)
                    for k in range(2):
                        ins = pe.matmul(ps[:, 2, k:k + 1], PEB[:, k, :], ones[:, 0:1], start=True, stop=True)
                ins.then_inc(ps_full, 1)
                wait_free(pe, u + 1, i, per)
                wait_emptied(pe, u, i, per)
                kv = bank(u + 1)
                pe.matmul(kv[:, 0, 0:cols], W2[:, 0, :], HID[:, 0, 0:cols], start=True, stop=True)
                pe.matmul(kv[0:cols, 1, 0:P], HID[:, 1, 0:cols], W2[:, 1, :], start=True, stop=True).then_inc(ps_full, 1)

            pe.wait_ge(w1_in, 16 * 6)
            squeeze(U_C, None, 0, NCP, lambda k, r: KVT[:, k, r:r + STRIDE * (NCP - 1) + 1:STRIDE])
            with pe.Fori(0, NB // 2) as i:
                for b in range(2):
                    pe.wait_ge(xc_in[b], at(i, HW_PAGES, HW_PAGES))
                    pe.wait_ge(xc_sw[b], at(i, SW_PAGES, SW_PAGES))
                    squeeze(U_C + 2 + 2 * b, i, 4, NCS,
                            lambda k, r: XC[b][:, k, r:r + STRIDE * (NCS - 1) + 1:STRIDE])

            pe.wait_ge(qb_here, 1)
            pe.wait_ge(vec_in, 32)
            wait_emptied(pe, U_S - 1)
            wait_free(pe, U_S)
            ps = bank(U_S)
            pe.matmul(ps[0:64, 1, 0:24], B8T, GT[0:NB, NC, :], start=True, stop=True)
            for b in range(NB):
                ins = pe.matmul(ps[0:64, 0, 0:NCS], QB[:, b, :], KC[:, b, 0:NCS], start=(b == 0), stop=(b == NB - 1))
            ins.then_inc(ps_full, 1)
            wait_free(pe, U_S + 1)
            pe.wait_ge(win_in, 32)
            ps = bank(U_S + 1)
            for b in range(NB):
                pe.matmul(ps[0:64, 0, :], QB[:, b, :], KW[:, b, :], start=(b == 0), stop=(b == NB - 1))
            for b in range(NB):
                ins = pe.matmul(ps[0:64, 1, 0:1], QB[:, b, :], KVT[:, 3, T + b:T + b + 1], start=(b == 0),
                                stop=(b == NB - 1))
            ins.then_inc(ps_full, 1)
            wait_free(pe, U_S + 2)
            pe.wait_ge(pc_here, 1)
            pe.matmul(bank(U_S + 2)[0:NCS, 0, 0:64], PC[:, 0:NCS], SAME, start=True, stop=True).then_inc(ps_full, 1)
            wait_free(pe, U_S + 3)
            ps = bank(U_S + 3)
            pe.wait_ge(pc_here, 2)
            pe.transpose(ps[0:NCS, 1, 0:64], PCG[:, 0:NCS], ident[0:64, 0:64])
            wait_emptied(pe, U_S + 2)
            pe.matmul(ps[0:64, 0, 0:NBLK], IT[0:NCS], COVER, start=True, stop=True).then_inc(ps_full, 1)
            wait_free(pe, U_S + 4)
            wait_free(pe, U_S + 5)
            d, e = bank(U_S + 4), bank(U_S + 5)
            for b in range(NB):
                pe.matmul(d[0:64, 2, 0:1], QB[:, b, :], KVT[:, 2, T + b:T + b + 1], start=(b == 0), stop=(b == NB - 1))
            for b in range(NB):
                pe.wait_ge(kb_in[b % 2], HW_PAGES * (b // 2 + 1))
                pe.wait_ge(kb_sw[b % 2], SW_PAGES * (b // 2 + 1))
                for n in range(4):
                    ins = pe.matmul((d, e)[n // 2][0:64, n % 2, :], QB[:, b, :], KB[b % 2][:, n * 512:(n + 1) * 512],
                                    start=(b == 0), stop=(b == NB - 1))
                    if b == NB - 1 and n % 2:
                        ins.then_inc(ps_full, 1)
                if b < NB - 1:
                    ins.then_inc(kb_used, 1)
                if b == 1:
                    pe.wait_ge(sw_here, 1)
                    for t in range(WIN // P):
                        ins = pe.transpose(PS[:, 7, t * 64:(t + 1) * 64], SW[:, t * P:(t + 1) * P], ident[0:64, 0:64])
                    ins.then_inc(ptw_full, 1)
                if 2 <= b < 6:
                    pe.wait_ge(ptw_here, 1)
                    for e8 in (2 * b - 4, 2 * b - 3):
                        ins = pe.matmul(PS[:, 6, e8 * HB:(e8 + 1) * HB], VC[0:NCS, e8, :], PCT[0:NCS, e8 * HB:(e8 + 1) * HB],
                                        start=True, stop=True)
                        for t in range(WIN // P):
                            ins = pe.matmul(PS[:, 6, 64 + e8 * HB:64 + (e8 + 1) * HB], VW[:, e8, t, :],
                                            PTW[:, t, e8 * HB:(e8 + 1) * HB], start=(t == 0), stop=(t == WIN // P - 1))
            wait_free(pe, U_S + 6)
            pe.wait_ge(sp_here, 1)
            ps = bank(U_S + 6)
            i64 = ident[0:64, 0:64]
            for t in range(NPG):
                pe.transpose(ps[:, t // 8, (t % 8) * 64:(t % 8 + 1) * 64], SX[:, t * P:(t + 1) * P], i64)
            for n in range(2):
                ins = pe.matmul(ps[0:NB, 2, 64 * n:64 * n + 64], T8[:, n, :], i64, start=True, stop=True)
            ins.then_inc(ps_full, 1)
            wait_free(pe, U_S + 7)
            wait_emptied(pe, U_S + 6)
            ps = bank(U_S + 7)
            pe.matmul(ps[:, 0, 64:128], SNT[0:NB, 3, :], PN[:, 0, :], start=True, stop=True)
            pe.matmul(ps[:, 0, 128:192], SNT[0:NB, 5, :], PN[:, 1, :], start=True, stop=True)
            for b in range(NB):
                pe.wait_ge(vb_in[b % 2], HW_PAGES * (b // 2 + 1))
                pe.wait_ge(vb_sw[b % 2], SW_PAGES * (b // 2 + 1))
                for t in range(NPG):
                    ins = pe.matmul(ps[:, 0, b * 8:b * 8 + 8], VB[b % 2][:, t, :], PTS[:, t, b * 8:b * 8 + 8],
                                    start=(t == 0), stop=(t == NPG - 1))
                if b < NB - 1:
                    ins.then_inc(vb_used, 1)
            ins.then_inc(ps_full, 1)

            def first(n, i, j, half):
                rows = slice(64 * half, 64 * half + 64)
                q = mix[rows, HA + j, i * P:(i + 1) * P]
                psf = PS[:, :, :].rearrange("p a b -> p (a b)")
                if n:
                    pe.wait_ge(sc_free, n)
                (_, slc), (_, win), (_, cmp) = spans(i)
                for cols, key, src in (slc, 0, 2), (win, max(0, i - 4) * P, 3):
                    lo = cols.start
                    while lo < cols.stop:
                        end = min(cols.stop, (lo // 512 + 1) * 512)
                        pe.matmul(psf[:, lo:end], q, KVT[rows, src, key:key + end - lo], start=True, stop=True)
                        lo, key = end, key + end - lo
                pe.matmul(psf[:, cmp], q, KC[rows, NB, 0:NCP], start=True, stop=True).then_inc(sc_full, 1)

            def second(n, i, j, half):
                bl = blocks(i)
                rows = slice(64 * half, 64 * half + 64)

                def values(g):
                    pe.wait_ge(t_free, group_at[n] + g + 1)
                    if g == 0 and half == 0 and n:
                        pe.wait_ge(pv_free, n // 2)
                    for b, (kind, t, _) in enumerate(bl[4 * g:4 * g + 4]):
                        p = PT[:, half, (4 * g + b) * P:(4 * g + b + 1) * P]
                        if kind == "cmp":
                            v, p = VC[0:NCP, NB, rows], p[0:NCP]
                        else:
                            v = (VSL if kind == "slc" else VWN)[:, t, rows]
                        ins = pe.matmul(PS[rows, 6, 0:P], v, p, start=(g == b == 0),
                                        stop=(4 * g + b == len(bl) - 1), skip_group_check=True)
                    return ins

                pe.wait_ge(pw_here, n + 1)
                for g in range(groups[i]):
                    if group_at[n] + g >= 3:
                        pe.wait_ge(t_free, group_at[n] + g - 2)
                    for b, (kind, _, c) in enumerate(bl[4 * g:4 * g + 4]):
                        m = NCP if kind == "cmp" else P
                        ins = pe.transpose(PS[0:m, TURN_BANKS[(group_at[n] + g) % 3], b * P:(b + 1) * P],
                                           SS[:, n % 3, c:c + m], ident)
                    ins.then_inc(t_full, 1)
                    if g >= 2:
                        values(g - 2)
                if groups[i] > 1:
                    values(groups[i] - 2)
                values(groups[i] - 1).then_inc(pv_full, 1)

            wait_free(pe, U_S + 8)
            wait_free(pe, U_S + 9)
            attention(2, first, second)
            pe.wait_ge(pv_free, HA * NC)

            def product(u, n, f, src, first, last):
                for half, others in ((0, (0, 1)), (1, (0,))):
                    weights = W2H[:, n, half, f * P:(f + 1) * P]
                    for m in range(TN):
                        for other in others:
                            ins = pe.matmul(wide(u)[:, m, :], weights, src[:, other, m * TW:(m + 1) * TW],
                                            start=(first and half == other == 0), stop=(last and half == 1))
                return ins

            def stage(name, src, ready):
                u, c = PLAN[name][0], STEP[name]
                with pe.Fori(0, PLAN_N[name] // 2) as i:
                    for k in range(2):
                        wait_free(pe, u + k, i, 2)
                        pe.wait_ge(w_split, at(i, 2, c + k + 1))
                        for f in range(KD):
                            if k == 0:
                                ready(f)
                            ins = product(u + k, k, f, src[:, f], f == 0, f == KD - 1)
                        ins.then_inc(ps_full, 1)

            def down(name, base):
                u, c = PLAN[name][0], STEP[name]
                with pe.Fori(0, KD // 2) as i:
                    for k in range(2):
                        wait_free(pe, u + k, i, 2)
                        for n in range(2):
                            pe.wait_ge(w_split, at(i, 4, c + 2 * k + n + 1))
                            for f in range(KH):
                                g = n * KH + f
                                if k == 0:
                                    pe.wait_ge(z_here, base + g + 2)
                                ins = product(u + k, n, f, Z2[:, g], g == 0, g == KF - 1)
                            ins.then_inc(ps_full if n else half_used, 1)

            def normed(norm):
                return lambda f: pe.wait_ge((lo_even, lo_odd)[f % 2], (norm - 1) * KD // 2 + f // 2 + 1)

            stage("mix_out", H2, lambda f: pe.wait_ge(*((mix_a, f + 1) if f < HA else (mix_b, f - HA + 1))))
            norm(PLAN["norm1"][0], 1)
            stage("up0", H2, normed(1))
            down("down0", 0)
            norm(PLAN["norm2"][0], 2)
            stage("conv_in", H2, normed(2))
            stage("conv_out", Z2, lambda f: pe.wait_ge(cy_here, f + 2))
            norm(PLAN["norm3"][0], 3)
            stage("up1", H2, normed(3))
            down("down1", KF)
            norm(PLAN["norm4"][0], 4)


def kernel(**inputs):
    import concourse.bacc as bacc
    from concourse.bass_utils import run_bass_kernel_spmd as run

    a = {k: np.asarray(v) for k, v in inputs.items()}
    r = np.arange

    def columns(w, cols):
        k = w.shape[0] // P
        return w[:, cols].reshape(k, P, len(cols)).transpose(1, 0, 2).reshape(P, -1)

    def feature(v):
        v = v.reshape(v.shape[:-1] + (-1, P))
        return np.moveaxis(v, (-1, -2), (0, 1))

    ab, ab_out = a["ab_w_in"][0], a["ab_w_out"][0]
    pair = [np.concatenate([j * HD + r(HD), (j + HA) * HD + r(HD)]) for j in range(HA)]
    chunks = []
    for h in range(HA):
        chunks += [columns(ab, off + h * P + r(P)) for off in (512, 0, 1024, 1536)] + [columns(ab, 2048 + pair[h])]
    chunks += [columns(ab, 2560 + n * P + r(P)) for n in range(6)]
    mixed = np.concatenate([r(HA * P)] + [HA * P + p for p in pair])
    chunks += [columns(ab_out[mixed], n * P + r(P)) for n in range(KD)]
    hidden = np.stack([r(KF), KF + r(KF)], 1).reshape(-1)
    up = [[columns(a["ffn_up"][n], t * P + r(P)) for t in hidden] for n in range(2)]
    three = np.stack([r(KD), KD + r(KD), 2 * KD + r(KD)], 1).reshape(-1)
    chunks += up[0] + [columns(a["c_w_in"][0], t * P + r(P)) for t in three]
    chunks += [columns(a["c_w_out"][0], t * P + r(P)) for t in range(KD)] + up[1]
    down = [[columns(a["ffn_down"][n][h * KH * P:(h + 1) * KH * P], t * P + r(P)) for t in range(KD) for h in range(2)]
            for n in range(2)]

    x = np.concatenate([a["x_prompt"][0], a["x_sample"][:, 0]])
    small = np.concatenate([feature(v) for v in (
        a["norm_mix"][0], a["norm_ffn"][0], a["norm_mix"][1], a["norm_ffn"][1], a["norm_final"],
        a["hgrn_lb_logits"][0], a["hgrn_lb_logits"][1], a["hgrn_norm"][0])], 1)

    s, t = np.meshgrid(r(P), r(P), indexing="ij")
    cst = np.zeros((P, 4, P), np.float32)
    cst[:, 0], cst[:, 1], cst[:, 2], cst[:, 3] = np.eye(P), 1 / D, 1 / P, 1
    hmask = np.zeros((P, LEV + 1, P), np.float32)
    hmask[:, 0] = np.eye(P)
    for lev in range(LEV):
        m = 1 << lev
        hmask[:, lev + 1] = (s // (2 * m) == t // (2 * m)) & (s // m % 2 == 0) & (t // m % 2 == 1)
    slope = 2.0 ** (-8.0 * (r(HB) + 1) / HB)
    row = r(NB * HB)
    csn = np.zeros((P, 330), np.float32)
    csn[0:64, 0:64] = row[:, None] // HA == row[None] // HA
    start, block = r(NCS)[:, None] * STRIDE, r(NBLK)[None] * 64
    csn[0:NCS, 64:97] = (start < block + 64) & (start + CMP > block)
    by_row = slope[row % HB][:, None]
    csn[0:64, 97:97 + NCS] = -by_row * (PAST - (start[:, 0] + CMP - 1))[None]
    csn[0:64, 224:232] = row[:, None] // HB == r(NB)[None]
    csn[0:NB, 232:296] = row[None] // HB == r(NB)[:, None]
    csn[0:64, 296:320] = row[:, None] % HB == r(3 * HB)[None] // 3
    csn[:, 320:328] = -slope
    csn[:, 328] = r(P) >= CMP - 1
    bias_w = (-by_row * (WIN - r(WIN + 1))[None]).astype(np.float32)
    bias_w[:, 0] = -FAR
    bias_s = (-by_row * (PAST - r(PAST + 1))[None]).astype(np.float32)
    tri = np.broadcast_to((r(NBLK)[None] < r(NBLK)[:, None]).astype(np.float32), (64, NBLK, NBLK))
    far = lambda dist, keep: np.where(keep, dist, FAR).astype(np.float32)
    dist = r(P)[:, None] - (r(T) - (T - P))[None]
    dist_w = r(P)[:, None] - (r(640) - 512)[None]
    table = np.concatenate([far(dist, dist >= 0), far(dist_w, (dist_w >= 0) & (dist_w < WIN))], 1)
    dist_c = (r(NC) * P)[None, :, None] + r(P)[:, None, None] - (r(64) * STRIDE + CMP - 1)[None, None]
    table_c = far(dist_c, dist_c >= 0)

    def rows_t(v):
        return feature(v).transpose(0, 1, 3, 2)

    w1 = a["cmp_w1"][0].reshape(2, CMP, HD, 64).transpose(2, 0, 1, 3).reshape(HD, 2 * CMP, 64)
    win = a["state_win_kv"][0].reshape(NB, WIN, 2, P)
    cmp_pool, slc_pool = (a[n].reshape(NPOOL, PAGE, 2, P) for n in ("cache_cmp_kv", "cache_slc_kv"))
    given = {
        "x": feature(x).transpose(0, 1, 2), "wk8": np.stack(chunks), "wdn": np.stack([np.stack(d) for d in down]),
        "small": small, "cst": cst, "hmask": hmask, "s_hgrn": a["state_hgrn"][0],
        "wgate": columns(ab, 3328 + r(24)).reshape(P, KD, 24), "pages": a["page_table"].reshape(1, -1),
        "cmp_t": cmp_pool.transpose(0, 3, 2, 1), "slc_kt": slc_pool[:, :, 0].transpose(0, 2, 1), "slc_v": slc_pool[:, :, 1],
        "win_kt": win[:, :, 0].transpose(2, 0, 1),
        "win_v": win[:, :, 1].reshape(NB, WIN // P, P, P).transpose(2, 0, 1, 3), "state_win": win,
        "w1": w1, "w2": a["cmp_w2"][0].transpose(1, 0, 2), "pe_t": a["cmp_pe"][0].transpose(2, 0, 1),
        "csn": csn, "bias_w": bias_w, "bias_s": bias_s, "tri": tri, "table": table, "table_c": table_c,
        "s_ff": np.stack([rows_t(a["state_ffn"][n])[:, hidden] for n in range(2)]),
        "w_ff": np.stack([feature(a["ffn_conv"][n])[:, hidden] for n in range(2)]),
        "s_sc": rows_t(a["state_sconv"][0]), "w_sc": feature(a["c_conv"][0]),
    }
    made = {
        "o_y": (P, KD, TT), "o_hgrn_p": (HA, P, P), "o_hgrn_s": (NB, HA, P, P), "o_cmp_p": (T, 2, P), "o_slc_p": (T, 2, P),
        "o_win_p": (WIN, 2, P), "o_cmp_s": (NB, 2, P), "o_slc_s": (NB, 2, P), "o_win_s": (NB, WIN, 2, P),
        "o_sc": (P, KD, 2 * (NB + 1)), "o_ff": (2, P, 2 * KF, 2 * (NB + 1)),
    }
    nc = bacc.Bacc("TRN2", target_bir_lowering=False, num_devices=1)
    arrays = {n: np.ascontiguousarray(v) for n, v in given.items()}
    args = [nc.dram_tensor(n, v.shape, mybir.dt.from_np(v.dtype), kind="ExternalInput").ap() for n, v in arrays.items()]
    args += [nc.dram_tensor(n, v, F32, kind="ExternalOutput").ap() for n, v in made.items()]
    program(nc, *args)
    o = run(nc, [arrays], core_ids=[0]).results[0]

    y = o["o_y"].transpose(2, 1, 0).reshape(TT, D)

    def last_rows(v, order=None):
        if order is not None:
            back = np.empty_like(v)
            back[:, order] = v
            v = back
        v = v.transpose(2, 1, 0).reshape(2 * (NB + 1), -1)
        return v[:2][None], v[2:].reshape(NB, 2, -1)

    sc_p, sc_s = last_rows(o["o_sc"])
    ff = [last_rows(o["o_ff"][n], hidden) for n in range(2)]
    kv = (2, 2, HD)
    return (
        y[:T][None], y[T:][:, None],
        o["o_cmp_p"].reshape(1, T, 1, *kv), o["o_slc_p"].reshape(1, T, 1, *kv), o["o_win_p"].reshape(1, 1, WIN, *kv),
        o["o_hgrn_p"][None, None], sc_p[None], np.stack([f[0] for f in ff]),
        o["o_cmp_s"].reshape(NB, 1, 1, *kv), o["o_slc_s"].reshape(NB, 1, 1, *kv), o["o_win_s"].reshape(1, NB, WIN, *kv),
        o["o_hgrn_s"][None], sc_s[None], np.stack([f[1] for f in ff]),
    )
```
